# Optimizing a Trainium2 kernel written in Bass

```python
import math
import jax, jax.numpy as jnp
from jax import lax
import numpy as np

D_MODEL = 1024
BATCH = 1
SEQ = 512
DEPTH = 2
DEC_BATCH = 8
DEC_SEQ = 4
PAST_LEN = 4096
PAGE_SIZE = 128

N_MIXERS = 2
N_HGRN = (DEPTH + N_MIXERS - 1) // N_MIXERS
N_GDN = DEPTH // N_MIXERS
HGRN_HEADS = 8
HGRN_DK = 128
HGRN_DV = D_MODEL // HGRN_HEADS
HGRN_F = HGRN_HEADS * HGRN_DK
HGRN_IN = 2 * HGRN_F + 2 * D_MODEL
GDN_HEADS = 8
GDN_DK = 128
GDN_DV = 128
GDN_QK = GDN_HEADS * GDN_DK
GDN_V = GDN_HEADS * GDN_DV
GDN_CONV = 4
GDN_CONV_DIM = 2 * GDN_QK + GDN_V
GDN_IN = GDN_CONV_DIM + GDN_V + 2 * GDN_HEADS
D_FF = 4 * D_MODEL
CHUNK = 64
EPS = 1e-6
LB_FLOOR = 1e-30

kernel_name = "hgrn2_gated_deltanet_hybrid_step"

F32 = jnp.float32

def _rmsnorm(x, w):
    xf = x.astype(F32)
    y = xf * lax.rsqrt(jnp.mean(xf * xf, axis=-1, keepdims=True) + EPS)
    return (y * w.astype(F32)).astype(x.dtype)

def _l2norm(x):
    return x * lax.rsqrt(jnp.sum(x * x, axis=-1, keepdims=True) + EPS)

def _chunking(T):
    C = min(CHUNK, T)
    n = -(-T // C)
    return C, n, n * C - T

def _pad_time(x, pad):
    return jnp.pad(x, [(0, 0), (0, pad)] + [(0, 0)] * (x.ndim - 2))

def _to_chunks(x, C, n):
    x = x.reshape((x.shape[0], n, C) + x.shape[2:])
    return jnp.moveaxis(x, (1, 3), (0, 2))

def _from_chunks(o, T):
    o = jnp.moveaxis(o, (0, 2), (1, 3))
    n, C = o.shape[1], o.shape[2]
    return o.reshape((o.shape[0], n * C) + o.shape[3:])[:, :T]

def _hgrn_recurrence(q, k, v, log_f, S0):
    T = q.shape[1]
    C, n, pad = _chunking(T)
    q, k, v, log_f = [_to_chunks(_pad_time(a, pad), C, n) for a in (q, k, v, log_f)]
    b = jnp.cumsum(log_f, axis=3)
    causal = jnp.tril(jnp.ones((C, C), bool))[:, :, None]

    def step(S, inp):
        qc, kc, vc, bc = inp
        diff = bc[:, :, :, None, :] - bc[:, :, None, :, :]
        dec = jnp.where(causal, jnp.exp(jnp.where(causal, diff, 0.0)), 0.0)
        A = jnp.einsum('bhtk,bhsk,bhtsk->bhts', qc, kc, dec)
        bl = bc[:, :, -1]
        o = (jnp.einsum('bhtk,bhkv->bhtv', qc * jnp.exp(bc), S)
             + jnp.einsum('bhts,bhsv->bhtv', A, vc))
        S = (jnp.exp(bl)[..., None] * S
             + jnp.einsum('bhsk,bhsv->bhkv', kc * jnp.exp(bl[:, :, None, :] - bc), vc))
        return S, o

    S, o = lax.scan(step, S0, (q, k, v, b))
    return _from_chunks(o, T), S

def _gdn_recurrence(q, k, v, beta, g, S0):
    T = q.shape[1]
    C, n, pad = _chunking(T)
    q, k, v, beta, g = [_to_chunks(_pad_time(a, pad), C, n) for a in (q, k, v, beta, g)]
    G = jnp.cumsum(g, axis=-1)
    incl = jnp.tril(jnp.ones((C, C), bool))
    strict = jnp.tril(jnp.ones((C, C), bool), k=-1)
    diff = G[..., :, None] - G[..., None, :]
    decay = jnp.where(incl, jnp.exp(jnp.where(incl, diff, 0.0)), 0.0)
    kk = jnp.einsum('nbhtk,nbhsk->nbhts', k, k)
    M = jnp.eye(C, dtype=F32) + jnp.where(strict, beta[..., :, None] * kk * decay, 0.0)
    u = lax.linalg.triangular_solve(M, v * beta[..., None], left_side=True, lower=True)
    w = lax.linalg.triangular_solve(M, k * (beta * jnp.exp(G))[..., None],
                                    left_side=True, lower=True)
    Aqk = jnp.einsum('nbhtk,nbhsk->nbhts', q, k) * decay
    qg = q * jnp.exp(G)[..., None]
    kd = k * jnp.exp(G[..., -1:] - G)[..., None]
    gl = jnp.exp(G[..., -1])

    def step(S, inp):
        uc, wc, qc, ac, kc, glc = inp
        v_new = uc - jnp.einsum('bhtk,bhkv->bhtv', wc, S)
        o = jnp.einsum('bhtk,bhkv->bhtv', qc, S) + jnp.einsum('bhts,bhsv->bhtv', ac, v_new)
        S = glc[..., None, None] * S + jnp.einsum('bhsk,bhsv->bhkv', kc, v_new)
        return S, o

    S, o = lax.scan(step, S0, (u, w, qg, Aqk, kd, gl))
    return _from_chunks(o, T), S

def _causal_conv(x, buf, w):
    T = x.shape[1]
    xp = jnp.concatenate([buf.astype(x.dtype), x], axis=1)
    y = xp[:, 0:T] * w[0]
    for j in range(1, GDN_CONV):
        y = y + xp[:, j:j + T] * w[j]
    return jax.nn.silu(y), xp[:, T:]

def _hgrn_mixer(h, w_in, lb, out_norm, w_out, S0):
    B, T, _ = h.shape
    proj = h @ w_in
    q, fz, i, g = jnp.split(proj, [HGRN_F, 2 * HGRN_F, 2 * HGRN_F + D_MODEL], axis=-1)
    q = jax.nn.silu(q.astype(F32)).reshape(B, T, HGRN_HEADS, HGRN_DK)
    fz = fz.astype(F32).reshape(B, T, HGRN_HEADS, HGRN_DK)
    lb = lb.astype(F32).reshape(HGRN_HEADS, HGRN_DK)
    log_f = jnp.logaddexp(jnp.log(jnp.maximum(lb, LB_FLOOR)),
                          jnp.log1p(-lb) + jax.nn.log_sigmoid(fz))
    k = (1.0 - lb) * jax.nn.sigmoid(-fz)
    v = i.astype(F32).reshape(B, T, HGRN_HEADS, HGRN_DV)
    o, S = _hgrn_recurrence(q, k, v, log_f, S0.astype(F32))
    o = _rmsnorm(o, out_norm) * jax.nn.silu(g.astype(F32).reshape(B, T, HGRN_HEADS, HGRN_DV))
    return o.reshape(B, T, D_MODEL).astype(h.dtype) @ w_out, S

def _gdn_mixer(h, w_in, conv_w, A_log, dt_bias, out_norm, w_out, S0, buf):
    B, T, _ = h.shape
    proj = h @ w_in
    qkv, z, a, b = jnp.split(
        proj, [GDN_CONV_DIM, GDN_CONV_DIM + GDN_V, GDN_CONV_DIM + GDN_V + GDN_HEADS], axis=-1)
    qkv, new_buf = _causal_conv(qkv, buf, conv_w)
    q, k, v = jnp.split(qkv.astype(F32), [GDN_QK, 2 * GDN_QK], axis=-1)
    q = _l2norm(q.reshape(B, T, GDN_HEADS, GDN_DK)) * (GDN_DK ** -0.5)
    k = _l2norm(k.reshape(B, T, GDN_HEADS, GDN_DK))
    v = v.reshape(B, T, GDN_HEADS, GDN_DV)
    beta = jax.nn.sigmoid(b.astype(F32))
    g = -jnp.exp(A_log.astype(F32)) * jax.nn.softplus(a.astype(F32) + dt_bias.astype(F32))
    o, S = _gdn_recurrence(q, k, v, beta, g, S0.astype(F32))
    o = _rmsnorm(o, out_norm) * jax.nn.silu(z.astype(F32).reshape(B, T, GDN_HEADS, GDN_DV))
    return o.reshape(B, T, GDN_V).astype(h.dtype) @ w_out, S, new_buf

def _trunk(x, s_hgrn, s_gdn, s_conv, norm_mix, norm_mlp, norm_final, hgrn_w_in, hgrn_lb_eff,
           hgrn_out_norm, hgrn_w_out, gdn_w_in, gdn_conv_w, gdn_A_log, gdn_dt_bias,
           gdn_out_norm, gdn_w_out, mlp_w_up, mlp_w_down):
    new_h, new_g, new_c = [], [], []
    for i in range(DEPTH):
        j = i // N_MIXERS
        h = _rmsnorm(x, norm_mix[i])
        if i % N_MIXERS == 0:
            y, S = _hgrn_mixer(h, hgrn_w_in[j], hgrn_lb_eff[j], hgrn_out_norm[j],
                               hgrn_w_out[j], s_hgrn[j])
            new_h.append(S)
        else:
            y, S, c = _gdn_mixer(h, gdn_w_in[j], gdn_conv_w[j], gdn_A_log[j], gdn_dt_bias[j],
                                 gdn_out_norm[j], gdn_w_out[j], s_gdn[j], s_conv[j])
            new_g.append(S)
            new_c.append(c)
        x = x + y
        u = _rmsnorm(x, norm_mlp[i]) @ mlp_w_up[i]
        x = x + jnp.square(jax.nn.relu(u)) @ mlp_w_down[i]
    return _rmsnorm(x, norm_final), jnp.stack(new_h), jnp.stack(new_g), jnp.stack(new_c)

def setup_inputs(seed: int = 0) -> dict:
    key = jax.random.key(seed)
    ks = jax.random.split(key, 20)

    def nrm(k, shape, scale):
        return jax.random.normal(k, shape, F32) * scale

    dt = jnp.exp(jax.random.uniform(ks[15], (N_GDN, GDN_HEADS), F32,
                                    math.log(1e-3), math.log(1e-1)))
    return {
        "x_prompt": nrm(ks[0], (BATCH, SEQ, D_MODEL), 1.0),
        "x_sample": nrm(ks[1], (DEC_BATCH, DEC_SEQ, D_MODEL), 1.0),
        "state_hgrn": nrm(ks[2], (N_HGRN, DEC_BATCH, HGRN_HEADS, HGRN_DK, HGRN_DV), 0.5),
        "state_gdn": nrm(ks[3], (N_GDN, DEC_BATCH, GDN_HEADS, GDN_DK, GDN_DV), 0.1),
        "state_gdn_conv": nrm(ks[4], (N_GDN, DEC_BATCH, GDN_CONV - 1, GDN_CONV_DIM), 1.0),
        "norm_mix": 1.0 + nrm(ks[5], (DEPTH, D_MODEL), 0.02),
        "norm_mlp": 1.0 + nrm(ks[6], (DEPTH, D_MODEL), 0.02),
        "norm_final": 1.0 + nrm(ks[7], (D_MODEL,), 0.02),
        "hgrn_w_in": nrm(ks[8], (N_HGRN, D_MODEL, HGRN_IN), D_MODEL ** -0.5),
        "hgrn_lb": nrm(ks[9], (N_HGRN, HGRN_F), 0.5),
        "hgrn_out_norm": 1.0 + nrm(ks[10], (N_HGRN, HGRN_DV), 0.02),
        "hgrn_w_out": nrm(ks[11], (N_HGRN, D_MODEL, D_MODEL), D_MODEL ** -0.5),
        "gdn_w_in": nrm(ks[12], (N_GDN, D_MODEL, GDN_IN), D_MODEL ** -0.5),
        "gdn_conv_w": nrm(ks[13], (N_GDN, GDN_CONV, GDN_CONV_DIM), GDN_CONV ** -0.5),
        "gdn_A_log": jnp.log(jax.random.uniform(ks[14], (N_GDN, GDN_HEADS), F32, 1.0, 16.0)),
        "gdn_dt_bias": dt + jnp.log(-jnp.expm1(-dt)),
        "gdn_out_norm": 1.0 + nrm(ks[16], (N_GDN, GDN_DV), 0.02),
        "gdn_w_out": nrm(ks[17], (N_GDN, GDN_V, D_MODEL), GDN_V ** -0.5),
        "mlp_w_up": nrm(ks[18], (DEPTH, D_MODEL, D_FF), D_MODEL ** -0.5),
        "mlp_w_down": nrm(ks[19], (DEPTH, D_FF, D_MODEL), D_FF ** -0.5),
    }

def reference(x_prompt, x_sample, state_hgrn, state_gdn, state_gdn_conv, norm_mix, norm_mlp,
              norm_final, hgrn_w_in, hgrn_lb, hgrn_out_norm, hgrn_w_out, gdn_w_in, gdn_conv_w,
              gdn_A_log, gdn_dt_bias, gdn_out_norm, gdn_w_out, mlp_w_up, mlp_w_down):
    lb = jax.nn.softmax(hgrn_lb.astype(F32), axis=0)
    lb_eff = jnp.cumsum(lb, axis=0) - lb[0]
    weights = (norm_mix, norm_mlp, norm_final, hgrn_w_in, lb_eff, hgrn_out_norm, hgrn_w_out,
               gdn_w_in, gdn_conv_w, gdn_A_log, gdn_dt_bias, gdn_out_norm, gdn_w_out,
               mlp_w_up, mlp_w_down)
    B = x_prompt.shape[0]
    zh = jnp.zeros((N_HGRN, B, HGRN_HEADS, HGRN_DK, HGRN_DV), F32)
    zg = jnp.zeros((N_GDN, B, GDN_HEADS, GDN_DK, GDN_DV), F32)
    zc = jnp.zeros((N_GDN, B, GDN_CONV - 1, GDN_CONV_DIM), x_prompt.dtype)
    y_prompt, hgrn_prompt, gdn_prompt, conv_prompt = _trunk(x_prompt, zh, zg, zc, *weights)
    y_sample, hgrn_sample, gdn_sample, conv_sample = _trunk(
        x_sample, state_hgrn, state_gdn, state_gdn_conv, *weights)
    return (y_prompt, y_sample, hgrn_prompt, hgrn_sample, gdn_prompt, gdn_sample,
            conv_prompt, conv_sample)


_drawn_inputs = setup_inputs


def setup_inputs(seed=0):
    import zlib

    import numpy as np

    out = dict(_drawn_inputs(seed))
    spreads = {}
    factors = {'norm_final': 8.191, 'hgrn_out_norm': 2.827, 'gdn_out_norm': 23.871, 'norm_mlp': 2.753}
    for name, (base, spread) in spreads.items():
        noise = np.random.default_rng([zlib.crc32(name.encode()), seed]).standard_normal(out[name].shape)
        drawn = base * np.exp(spread * noise) if base else spread * noise
        out[name] = __import__('jax').numpy.asarray(drawn.astype(out[name].dtype))
    for name, factor in factors.items():
        out[name] = (out[name] * factor).astype(out[name].dtype)
    return out
```

```python
from contextlib import ExitStack

import numpy as np

import concourse.bass as bass
from concourse import mybir

F32 = mybir.dt.float32
F32R = mybir.dt.float32r
U8 = mybir.dt.uint8
ALU = mybir.AluOpType
ACT = mybir.ActivationFunctionType
ds = bass.ds

P = 128
D = 1024
KT = D // P
TP = 512
NSEQ, SLEN = 8, 4
TS = NSEQ * SLEN
T = TP + TS
HALF = T // 2
NC = TP // P
H = 8
FF = 4 * D
NGRP = FF // D
EPS = 1e-6
LB_FLOOR = 1e-30
LN_SHIFT = 2.0 ** 60
CONV = 4
XW = CONV - 1
SB0 = XW + TP
SROW = XW + SLEN
XPW = SB0 + NSEQ * SROW
YW = XPW - XW
LEVELS = [1, 2, 4, 8, 16, 32, 64]
SLEVELS = [m for m in LEVELS if 2 * m <= SLEN]
RAW, SPLIT = 4, 2

V_MIX, V_MLP, V_FIN, V_LB, V_HON, V_GON, V_CONV = 0, 16, 32, 40, 48, 49, 50
V_N = V_CONV

C_EYE, C_INCL, C_NSTR, C_IND, C_RESET, C_SEQ, C_INCLS, C_NSTRS, C_HSEL = 0, 128, 256, 384, 640, 1184, 1192, 1224, 1256
C_W = C_HSEL + H
CU_HALF = len(LEVELS) * (T // 2)


def shape_constants():
    cf = np.zeros((P, C_W), np.float32)
    p = np.arange(P)
    cf[:, C_EYE:C_EYE + P] = np.eye(P)
    cf[:, C_INCL:C_INCL + P] = p[None, :] >= p[:, None]
    cf[:, C_NSTR:C_NSTR + P] = -(p[None, :] > p[:, None]).astype(np.float32)
    cf[0:32, C_IND:C_IND + P] = 1
    cf[32:64, C_IND + P:C_IND + 2 * P] = 1
    t = np.arange(T)
    first = np.where(t < TP, t % P == 0, (t - TP) % SLEN == 0)
    cf[:, C_RESET:C_RESET + T] = ~first
    s = np.arange(TS)
    cf[:TS, C_SEQ:C_SEQ + NSEQ] = s[:, None] // SLEN == np.arange(NSEQ)[None, :]
    same = s[:, None] // SLEN == s[None, :] // SLEN
    cf[:TS, C_INCLS:C_INCLS + TS] = same & (s[None, :] >= s[:, None])
    cf[:TS, C_NSTRS:C_NSTRS + TS] = -(same & (s[None, :] > s[:, None])).astype(np.float32)
    cf[:, C_HSEL:C_HSEL + H] = p[:, None] % 32 == np.arange(H)[None, :]
    cu = np.zeros((P, 2, len(LEVELS), T // 2), np.float32)
    for n, m in enumerate(LEVELS):
        c = np.arange(T // 2)
        blk, local = c // m, np.where(c < TP // 2, (c // m) % (P // (2 * m)), (c - TP // 2) // m)
        rb, rh = p // (2 * m), (p // m) % 2
        hit = rb[:, None] == local[None, :]
        cu[:, 0, n] = hit & (rh[:, None] == 0)
        cu[:, 1, n] = hit & (rh[:, None] == 1)
    return cf, cu.reshape(P, -1)


N_CONST = 12


class Steps:

    def __init__(self, sem, names):
        self.sem, self.names, self.at = sem, names, 0

    def did(self, instruction, name):
        assert self.names[self.at % len(self.names)] == name, (self.names[self.at % len(self.names)], name)
        self.at += 1
        instruction.then_inc(self.sem, 1)

    def after(self, name, i):
        return i * len(self.names) + (self.names.index(name) + 1)


def fixed(eng, value):
    return value if isinstance(value, int) else eng.to_reg(value)


def build(nc, x_prompt, x_sample, state_hgrn, state_gdn, state_conv, norm_mix, norm_mlp, norm_final, hgrn_w_in,
          hgrn_lb, hgrn_out_norm, hgrn_w_out, gdn_w_in, gdn_conv_w, gdn_A_log, gdn_dt_bias, gdn_out_norm, gdn_w_out,
          mlp_w_up, mlp_w_down, const_f, const_u, y_prompt, y_sample, hgrn_p, hgrn_s, gdn_p, gdn_s, conv_p, conv_s):
    with ExitStack() as ctx:
        def sb(name, shape, dt=F32):
            return ctx.enter_context(nc.sbuf_tensor(name, shape, dt))

        def sem(name):
            return ctx.enter_context(nc.semaphore(name))

        xT = sb("xT", [P, KT, T])
        xh = sb("xh", [P, KT, T], F32R)
        xl = sb("xl", [P, KT, T], F32R)
        oh = sb("oh", [P, KT, T], F32R)
        ol = sb("ol", [P, KT, T], F32R)
        w_raw = sb("w_raw", [P, RAW, KT, P])
        w_hi = sb("w_hi", [P, SPLIT, KT, P], F32R)
        w_lo = sb("w_lo", [P, SPLIT, KT, P], F32R)
        cf = sb("cf", [P, C_W])
        cu = sb("cu", [P, 2 * len(LEVELS) * (T // 2)], U8)
        vec = sb("vec", [P, V_N])
        cw = sb("cw", [P, CONV, 3 * H])
        hc = sb("hc", [P, 16])
        lbt = sb("lbt", [P, 4, H])
        ones = sb("ones", [P, P])
        epsc = sb("epsc", [P, 2])
        zeros = sb("zeros", [P, 1])
        rstd = sb("rstd", [P, T])
        sq = sb("sq", [P, 2, T])
        eye = cf[:, C_EYE:C_EYE + P]
        reset = cf[:, C_RESET:C_RESET + T]
        mask = cu[:, :].rearrange("p (a l n) -> p a l n", a=2, l=len(LEVELS))

        pr = sb("pr", [P, 4, XPW])
        ng = sb("ng", [P, 4, XPW])
        xp = sb("xp", [P, 3, XPW])
        q3 = sb("q3", [P, 3, T])
        Q, K, val = q3[:, 0], q3[:, 1], q3[:, 2]
        gate = sb("gate", [P, T])
        B = sb("B", [P, 4, T])
        b1, b2, b3, b4 = (B[:, n] for n in range(4))
        qe = sb("qe", [P, T])
        kd = sb("kd", [P, T])
        dd = sb("dd", [P, 2, T])
        QL = sb("QL", [P, 2, T // 2])
        KL = sb("KL", [P, 2, T])
        A = sb("A", [P, T])
        vT, kdT = (xp[:, n, XW:XW + TP].rearrange("p (c n) -> p c n", n=P) for n in range(2))
        vTs = sb("vTs", [TS, P])
        kdTs = sb("kdTs", [TS, P])
        vbig = pr[0:TS, :, :].rearrange("p g n -> p (g n)")[:, 0:NSEQ * P].rearrange("p (b n) -> p b n", n=P)
        Sp = sb("Sp", [P, NC, P])
        S0 = sb("S0", [P, NSEQ, P])
        Sn = ng[:, :, :].rearrange("p g n -> p (g n)")[:, 0:NSEQ * P].rearrange("p (b n) -> p b n", n=P)
        oo, og = b4, b1
        gt4 = sb("gt4", [P, T])
        gcol = sb("gcol", [P, NC + 1, P])
        gsel = b4
        gcols = sb("gcols", [P, NC + 1, 4])
        nbe = sb("nbe", [P, NC + 1])
        hcw = sb("hcw", [P, CONV, 3])
        NLt, Tm, Tt, X = KL[:, 0], KL[:, 1], sq[:, 1], QL[:, 0]
        R, VN = (dd[:, n, 0:TP].rearrange("p (c n) -> p c n", n=P) for n in range(2))
        Rs, VNs = QL[0:TS, 1, 0:P], QL[0:TS, 1, P:2 * P]
        rt = sb("rt", [P, TS])
        cstash = sb("cstash", [P, 3, XW * (NSEQ + 1)])
        cout = sb("cout", [XW * (NSEQ + 1), 3, P])
        cin = sb("cin", [XW * NSEQ, 3, P])
        gsc = sb("gsc", [H, 4])
        dtb = sb("dtb", [64, 1])

        pj = ctx.enter_context(nc.psum_tensor("pj", [P, 2, 2, 512], F32))
        rr = ctx.enter_context(nc.psum_tensor("rr", [P, 4, 512], F32))

        w_in = [sem(f"weights_loaded{j}") for j in range(RAW)]
        ab_in = sem("ab_loaded")
        w_split = sem("weights_split")
        w_used = sem("weights_used")
        unit_out = sem("unit_evacuated")
        c_in = sem("constants_loaded")
        x_in = [sem(f"x_loaded{n}") for n in range(2)]
        st_in = sem("state_loaded")
        st_out = sem("state_stored")
        y_out = [sem(f"y_stored{n}") for n in range(2)]
        x_done = sem("residual_tile_done")

        def levels(lists):
            return [n for names in lists for n in names]

        VS = dict(
            init=["fill", "vec", "cw", "lb1", "lb2", "lb3", "lb4", "lb5", "lb6"],
            x=["copy"], xs=["copy"],
            norm=[f"{n}{k}" for k in range(KT) for n in ("hi", "lo")],
            hg=(["cols", "neg", "ls", "cd", "nabs", "cmax", "q", "gate", "k", "lf", "b", "bd", "qe", "kd", "d1", "adiag"]
                + levels([([f"d{2 * m}"] if m < LEVELS[-1] else []) + [f"kl{m}"] + ([f"pred{m // 2}"] if m > 1 else [])
                          for m in LEVELS])
                + ["pred64", "S0", "S1", "S2", "S3", "vbig", "sdec", "snew", "on", "og", "lo"]),
            gp=["x", "neg", "ls", "g", "g2", "scan", "dl"],
            gd=(["cols", "nbe", "gsel", "tap1", "tap2", "tap3", "neg", "ls", "qkv", "gate", "qh", "kb", "qg", "dec", "incl",
                 "nl", "nl2", "tt0", "tt1", "vb", "kdt", "kdts"]
                + [f"pred{m}" for m in LEVELS[1:]]
                + ["S0", "r1", "S1", "r2", "S2", "r3", "S3", "sr1", "sr2", "sr3", "vbig", "sdec", "snew", "on", "og", "lo"]),
            up=["s0"] + levels([(f"s{k}", f"lo{k - 1}") for k in range(1, KT)]) + [f"lo{KT - 1}"],
            y=["y"], ys=["y"],
        )
        SS = dict(
            init=["lb1", "lb2", "lb3"],
            norm=[f"sq{k}" for k in range(KT)] + ["ln", "rstd"], normf=[f"sq{k}" for k in range(KT)] + ["ln", "rstd"],
            hg=(["exp", "ln", "sig", "k", "exp2", "ln2", "ebd"] + [f"e{m}" for m in LEVELS]
                + ["vT", "kdT", "kdTs", "oo", "sq", "ln3", "rn", "hi"]),
            gp=["A", "exp", "ln", "be", "el", "eg", "cols"],
            gd=(["cin", "stash", "cout", "tap", "exp", "ln", "sig", "sq", "ln2", "rn", "gb", "bb", "eg", "dec", "tm0"]
                + levels([(f"x{m}", f"tt{m}") for m in LEVELS[1:]])
                + ["vn0", "vn1", "vn2", "vn3", "rs", "vns", "oo", "sq2", "ln3", "rn3", "hi"]),
            up=[f"hi{k}" for k in range(KT)],
            y=["e"], ys=["e"],
        )
        TT = dict(
            init=["vec"], x=["t"], xs=["t"],
            norm=[f"sum{k}" for k in range(KT)], normf=[f"sum{k}" for k in range(KT)],
            hg=["diag"] + [f"lv{m}" for m in LEVELS] + ["vT", "kdT", "smp", "dS", "o", "os", "dSs", "ss"],
            gp=["cols"],
            gd=(["cin", "stash", "ssq", "gb", "kk", "qk", "sm", "t0", "vT", "kT", "vks"]
                + levels([(f"x{m}", f"dt{m}", f"tr{m}") for m in LEVELS[1:]])
                + ["vn0", "dS0", "ks1", "vn1", "dS1", "ks2", "vn2", "dS2", "ks3", "vn3", "dS3", "o", "sks", "srt", "svn",
                   "os", "dSs", "ss"]),
            y=["t"], ys=["t"],
        )
        dt_ready = sem("dt_bias_ready")
        ones_set = sem("ones_set")
        st = {}

        def stage(kind, key):
            if key not in st:
                st[key] = tuple(Steps(sem(f"{e}_{key}"), d[kind]) if kind in d else None
                                for e, d in (("vector", VS), ("scalar", SS), ("tensor", TT)))
            return st[key]

        for kind, key in [("init", "init"), ("x", "x"), ("xs", "xs"), ("norm", "n0"), ("norm", "n1"), ("norm", "n2"),
                          ("norm", "n3"), ("normf", "n4"), ("hg", "hg"), ("gp", "gp"), ("gd", "gd"), ("up", "up0"),
                          ("up", "up1"), ("y", "y"), ("ys", "ys")]:
            stage(kind, key)

        def halves(ap):
            return ap.rearrange("p (a n) -> p a n", a=2)

        def first_half(ap, m):
            return ap.rearrange("p (n two m) -> p n two m", two=2, m=m)[:, :, 0, :]

        def second_half(ap, m):
            return ap.rearrange("p (n two m) -> p n two m", two=2, m=m)[:, :, 1, :]

        def blocks(ap, m):
            return ap.rearrange("p (n m) -> p n m", m=m)

        def width(m):
            return T if m in SLEVELS else TP

        def psum_out(slot):
            return pj[:, slot, :, 0:HALF]

        U_HIN = 0
        U_HOUT = U_HIN + 4 * H
        U_MLP0 = U_HOUT + KT
        U_AB = U_MLP0 + 2 * KT * NGRP
        U_GIN = U_AB + 1
        U_GOUT = U_GIN + 4 * H
        U_MLP1 = U_GOUT + KT
        U_END = U_MLP1 + 2 * KT * NGRP

        def unit_done(u):
            return u + 3

        xrow = [pr[:, :, :].rearrange("p a n -> p (a n)")[:, n * D:(n + 1) * D] for n in range(2)]
        ycol = [ng[:, :, :].rearrange("p a n -> p (a n)")[:, n * D:(n + 1) * D] for n in range(2)]

        block = ctx.enter_context(nc.Block())

        @block.sync
        def _(sp):
            c = 16
            sp.dma_start(cf[:], const_f).then_inc(c_in, c)
            for stage_, part in zip((B, ng), (const_u[:, 0:CU_HALF], const_u[:, CU_HALF:2 * CU_HALF])):
                sp.dma_start(stage_[:].rearrange("p a n -> p (a n)")[:, 0:CU_HALF], part).then_inc(c_in, c)
            rows = xp[:, 0, :]
            for src, r, n in ((norm_mix, V_MIX, 16), (norm_mlp, V_MLP, 16)):
                sp.dma_start(rows[r:r + n, 0:P], src.rearrange("d (k p) -> (d k) p", p=P)).then_inc(c_in, c)
            sp.dma_start(rows[V_FIN:V_FIN + 8, 0:P], norm_final.rearrange("(k p) -> k p", p=P)).then_inc(c_in, c)
            sp.dma_start(rows[V_LB:V_LB + 8, 0:P], hgrn_lb.rearrange("d (k p) -> (d k) p", p=P)).then_inc(c_in, c)
            sp.dma_start(rows[V_HON:V_HON + 1, 0:P], hgrn_out_norm).then_inc(c_in, c)
            sp.dma_start(rows[V_GON:V_GON + 1, 0:P], gdn_out_norm).then_inc(c_in, c)
            sp.dma_start(xp[0:CONV * 3 * H, 1, 0:P],
                         gdn_conv_w[0].rearrange("j (s p) -> (j s) p", p=P)).then_inc(c_in, c)
            sp.dma_start(gsc[:, 0:1], gdn_A_log.rearrange("a h -> h a")).then_inc(c_in, c)
            sp.dma_start(gsc[:, 1:2], gdn_dt_bias.rearrange("a h -> h a")).then_inc(c_in, c)

            xs = stage("x", "x")[2]
            for n in range(NC):
                if n >= 2:
                    sp.wait_ge(xs.sem, n - 1)
                sp.dma_start(xrow[n % 2], x_prompt[0, n * P:(n + 1) * P, :]).then_inc(x_in[n % 2], 16)
            sp.wait_ge(xs.sem, NC - 1)
            sp.dma_start(xrow[0][0:TS], x_sample.rearrange("b t d -> (b t) d")).then_inc(x_in[0], 16)

            def load(U, r, j, src):
                slot = (U + j) % RAW
                if not isinstance(r, int) or r + U + j >= RAW:
                    sp.wait_ge(w_split, r * 2 + (2 * (U + j) - 6))
                sp.dma_start(w_raw[:, slot], src).then_inc(w_in[slot], 16)

            hin = hgrn_w_in[0].rearrange("(k p) n -> p k n", p=P)
            gin = gdn_w_in[0].rearrange("(k p) n -> p k n", p=P)
            for j in range(4):
                load(U_HIN, 0, j, hin[:, :, j * D:j * D + P])
            with sp.Fori(1, H) as h:
                for j in range(4):
                    load(U_HIN, h * 4, j, hin[:, :, ds(h * P + j * D, P)])

            def out_proj(U, w):
                view = w[0].rearrange("(k p) n -> p k n", p=P)
                with sp.Fori(0, 2) as i:
                    for j in range(4):
                        load(U, i * 4, j, view[:, :, ds(i * (4 * P) + j * P, P)])

            def mlp(layer, U):
                up = mlp_w_up[layer].rearrange("(k p) n -> p k n", p=P)
                down = mlp_w_down[layer].rearrange("(g k p) n -> p g k n", p=P, k=KT)
                with sp.Fori(0, NGRP) as g:
                    for j in range(KT):
                        load(U, g * (2 * KT), j, up[:, :, ds(g * D + j * P, P)])
                    for j in range(KT):
                        load(U, g * (2 * KT), KT + j,
                             down[:, ds(g, 1), :, j * P:(j + 1) * P].rearrange("p o k n -> p (o k) n"))

            out_proj(U_HOUT, hgrn_w_out)
            mlp(0, U_MLP0)
            slot = U_AB % RAW
            sp.wait_ge(w_split, 2 * U_AB - 6)
            with nc.allow_non_contiguous_dma(reason="16 columns"):
                for n in range(2):
                    sp.dma_start(w_raw[:, slot, :, 32 * n:32 * n + H],
                                 gin[:, :, 4 * D + n * H:4 * D + (n + 1) * H]).then_inc(w_in[slot], 16)
            with sp.Fori(0, H) as h:
                for j in range(4):
                    load(U_GIN, h * 4, j, gin[:, :, ds(h * P + j * D, P)])
            out_proj(U_GOUT, gdn_w_out)
            mlp(1, U_MLP1)

        @block.gpsimd
        def _(pool):
            nc.gpsimd.memset(ones[:], 1.0).then_inc(ones_set, 1)

            def split(n, j, extra=0):
                u, s = n * 4 + j, j % SPLIT
                loaded, free = fixed(pool, n * 16 + (16 + extra)), fixed(pool, u - 1)
                pool.wait_ge(ones_set, 1)
                pool.wait_ge(w_in[j], loaded)
                if not (isinstance(n, int) and u < SPLIT):
                    pool.wait_ge(w_used, free)
                nc.gpsimd.tensor_copy(w_hi[:, s], w_raw[:, j]).then_inc(w_split, 1)
                pool.wait_ge(w_split, u * 2 + 1)
                nc.gpsimd.tensor_tensor(w_lo[:, s], w_raw[:, j], w_hi[:, s], ALU.subtract).then_inc(w_split, 1)

            for j in range(RAW):
                split(0, j)
            with pool.Fori(1, U_AB // 4) as n:
                for j in range(RAW):
                    split(n, j)
            ab = U_AB % RAW
            with pool.Fori(U_AB // 4, U_END // 4) as n:
                for j in range(RAW):
                    split(n, j, 16 if j == ab else 0)
            for j in range(U_END % 4):
                split(U_END // 4, j, 16 if j == ab else 0)

        @block.tensor
        def _(pe):
            mm = nc.tensor.matmul

            def unit(U, r, j, hi, lo, k_ready=None):
                u, s = r + (U + j), (U + j) % SPLIT
                pe.wait_ge(w_split, u * 2 + 2)
                pe.wait_ge(unit_out, u + 1)
                for k in range(KT):
                    if k_ready:
                        k_ready(k)
                    for a, (w, v) in enumerate(((w_hi, hi), (w_hi, lo), (w_lo, hi))):
                        for b in range(2):
                            last = mm(pj[:, s, b, 0:HALF], w[:, s, k, :], v[:, k, b * HALF:(b + 1) * HALF],
                                      start=(k == 0 and a == 0), stop=(k == KT - 1 and a == 2))
                last.then_inc(w_used, 1)

            def sum_features(bank, src, start=True, stop=True):
                for b in range(2):
                    last = mm(rr[:, bank + b, 0:HALF], ones[:], src[:, b * HALF:(b + 1) * HALF], start=start, stop=stop)
                return last

            def norm(key):
                _, s, t = st[key]
                for k in range(KT):
                    pe.wait_ge(s.sem, s.after(f"sq{k}", 0))
                    t.did(sum_features(0, sq[:, k % 2], k == 0, k == KT - 1), f"sum{k}")

            def tr(out, in_):
                n = in_.shape[0]
                return nc.tensor.transpose(out, in_, cf[0:n, C_EYE:C_EYE + n])

            v, s, t = st["init"]
            pe.wait_ge(c_in, 16 * N_CONST)
            pe.wait_ge(ones_set, 1)
            pe.wait_ge(v.sem, v.after("fill", 0))
            tr(rr[:, 0, 0:V_N], xp[0:V_N, 0, 0:P])
            t.did(tr(rr[:, 1, 0:CONV * 3 * H], xp[0:CONV * 3 * H, 1, 0:P]), "vec")

            v, s, t = st["x"]
            for i in range(NC):
                pe.wait_ge(x_in[i % 2], 16 * (i // 2 + 1))
                if i:
                    pe.wait_ge(v.sem, v.after("copy", i - 1))
                for k in range(KT):
                    last = tr(rr[:, 2 + k // 4, (k % 4) * P:(k % 4 + 1) * P], xrow[i % 2][:, k * P:(k + 1) * P])
                t.did(last, "t")
            pe.wait_ge(x_in[0], 16 * (NC // 2 + 1))
            pe.wait_ge(v.sem, v.after("copy", NC - 1))
            for k in range(KT):
                last = tr(rr[:, 2, k * TS:(k + 1) * TS], xrow[0][0:TS, k * P:(k + 1) * P])
            st["xs"][2].did(last, "t")

            def wait_norm(key):
                v = st[key][0]
                return lambda k: pe.wait_ge(v.sem, v.after(f"lo{k}", 0))

            def hgrn_rec(h):
                v, s, t = st["hg"]
                pe.wait_ge(v.sem, v.after("k", h))
                for c in range(NC):
                    mm(rr[:, 2, c * P:(c + 1) * P], K[:, c * P:(c + 1) * P], Q[:, c * P:(c + 1) * P],
                       start=True, stop=True)
                t.did(mm(rr[0:TS, 3, 0:TS], K[:, TP:T], Q[:, TP:T], start=True, stop=True), "diag")
                for n, m in enumerate(LEVELS):
                    pe.wait_ge(v.sem, v.after(f"kl{m}", h))
                    if n >= 2:
                        pe.wait_ge(v.sem, v.after(f"pred{LEVELS[n - 2]}", h))
                    for c in range(NC):
                        last = mm(rr[:, n % 2, c * 64:(c + 1) * 64], KL[:, n % 2, c * P:(c + 1) * P],
                                  QL[:, n % 2, c * 64:(c + 1) * 64], start=True, stop=True)
                    if m in SLEVELS:
                        last = mm(rr[0:TS, n % 2, TP // 2:T // 2], KL[:, n % 2, TP:T], QL[:, n % 2, TP // 2:T // 2],
                                  start=True, stop=True)
                    t.did(last, f"lv{m}")
                for c in range(NC):
                    last = tr(rr[:, 2, c * P:(c + 1) * P], val[:, c * P:(c + 1) * P])
                t.did(last, "vT")
                for c in range(NC):
                    last = tr(rr[:, 3, c * P:(c + 1) * P], kd[:, c * P:(c + 1) * P])
                t.did(last, "kdT")
                pe.wait_ge(s.sem, s.after("vT", h))
                tr(rr[0:TS, 2, 0:P], val[:, TP:T])
                t.did(tr(rr[0:TS, 2, P:2 * P], kd[:, TP:T]), "smp")
                pe.wait_ge(s.sem, s.after("kdTs", h))
                for c in range(NC):
                    last = mm(rr[:, 2, c * P:(c + 1) * P], kdT[:, c, :], vT[:, c, :], start=True, stop=True)
                t.did(last, "dS")
                pe.wait_ge(v.sem, v.after("pred64", h))
                for c in range(NC):
                    cols = slice(c * P, (c + 1) * P)
                    last = mm(rr[:, 0, cols], vT[:, c, :], A[:, cols], start=True, stop=(c == 0))
                    if c:
                        pe.wait_ge(v.sem, v.after(f"S{c - 1}", h))
                        last = mm(rr[:, 0, cols], Sp[:, c - 1, :], qe[:, cols], start=False, stop=True)
                t.did(last, "o")
                mm(rr[:, 1, 0:TS], vTs[:], A[0:TS, TP:T], start=True, stop=False)
                pe.wait_ge(st_in, h * 16 + 16)
                for b in range(NSEQ):
                    last = mm(rr[:, 1, b * SLEN:(b + 1) * SLEN], S0[:, b, :],
                              qe[:, TP + b * SLEN:TP + (b + 1) * SLEN], start=False, stop=(b == NSEQ - 1))
                t.did(last, "os")
                pe.wait_ge(v.sem, v.after("vbig", h))
                for a in range(2):
                    last = mm(rr[:, 2 + a, :], kdTs[:], vbig[:, 4 * a:4 * a + 4, :].rearrange("p b n -> p (b n)"),
                              start=True, stop=True)
                t.did(last, "dSs")
                pe.wait_ge(s.sem, s.after("sq", h))
                t.did(sum_features(0, sq[:, 0]), "ss")

            def gdn_pre():
                v, s, t = st["gp"]
                pe.wait_ge(v.sem, v.after("dl", 0))
                pe.wait_ge(s.sem, s.after("eg", 0))
                for c in range(NC):
                    tr(rr[:, 2, c * P:(c + 1) * P], gt4[:, c * P:(c + 1) * P])
                t.did(tr(rr[0:TS, 3, 0:P], gt4[:, TP:T]), "cols")

            def gdn_rec(h):
                v, s, t = st["gd"]
                loaded, ready = fixed(pe, h * 32 + (16 * H + 32)), fixed(pe, v.after("cols", h))
                pe.wait_ge(c_in, 16 * N_CONST)
                pe.wait_ge(st_in, loaded)
                pe.wait_ge(v.sem, ready)
                for g in range(3):
                    last = tr(rr[:, 0, g * 32:g * 32 + XW * NSEQ], cin[:, g, :])
                t.did(last, "cin")
                pe.wait_ge(s.sem, s.after("stash", h))
                for g in range(3):
                    last = tr(rr[0:XW * (NSEQ + 1), 1, g * P:(g + 1) * P], cstash[:, g, :])
                t.did(last, "stash")
                pe.wait_ge(s.sem, s.after("sq", h))
                for g in range(2):
                    last = sum_features(2 * g, sq[:, g])
                t.did(last, "ssq")
                pe.wait_ge(s.sem, s.after("ln2", h))
                for g in range(2):
                    for b in range(2):
                        last = mm(rr[:, 2 * g + b, 0:HALF], cf[:, C_IND + g * P:C_IND + (g + 1) * P],
                                  gsel[:, b * HALF:(b + 1) * HALF], start=True, stop=True)
                t.did(last, "gb")
                pe.wait_ge(v.sem, v.after("kb", h))
                for c in range(NC):
                    cols = slice(c * P, (c + 1) * P)
                    last = mm(rr[:, 0, cols], K[:, cols], dd[:, 0, cols], start=True, stop=True)
                t.did(last, "kk")
                for c in range(NC):
                    cols = slice(c * P, (c + 1) * P)
                    last = mm(rr[:, 1, cols], K[:, cols], Q[:, cols], start=True, stop=True)
                t.did(last, "qk")
                mm(rr[0:TS, 2, 0:TS], K[:, TP:T], dd[:, 0, TP:T], start=True, stop=True)
                t.did(mm(rr[0:TS, 2, TS:2 * TS], K[:, TP:T], Q[:, TP:T], start=True, stop=True), "sm")
                pe.wait_ge(v.sem, v.after("tt1", h))
                for c in range(NC):
                    cols = slice(c * P, (c + 1) * P)
                    tr(rr[:, 0, cols], Tt[:, cols])
                t.did(tr(rr[0:TS, 1, 0:TS], Tt[0:TS, TP:T]), "t0")
                for c in range(NC):
                    last = tr(rr[:, 2, c * P:(c + 1) * P], val[:, c * P:(c + 1) * P])
                t.did(last, "vT")
                for c in range(NC):
                    last = tr(rr[:, 3, c * P:(c + 1) * P], K[:, c * P:(c + 1) * P])
                t.did(last, "kT")
                pe.wait_ge(v.sem, v.after("kdt", h))
                t.did(tr(rr[0:TS, 2, 0:P], K[:, TP:T]), "vks")
                pe.wait_ge(s.sem, s.after("tm0", h))
                for n, m in enumerate(LEVELS[1:]):
                    smp = m in SLEVELS
                    if n:
                        pe.wait_ge(s.sem, s.after(f"tt{LEVELS[n]}", h))
                    for c in range(NC):
                        cols = slice(c * P, (c + 1) * P)
                        last = mm(rr[:, 0, c * 64:(c + 1) * 64], NLt[:, cols], first_half(Tm[:, cols], m),
                                  start=True, stop=True)
                    if smp:
                        last = mm(rr[0:TS, 0, TP // 2:T // 2], NLt[0:TS, TP:T], first_half(Tm[0:TS, TP:T], m),
                                  start=True, stop=True)
                    t.did(last, f"x{m}")
                    pe.wait_ge(s.sem, s.after(f"x{m}", h))
                    for c in range(NC):
                        last = mm(rr[:, 1, c * 64:(c + 1) * 64], Tt[:, c * P:(c + 1) * P], X[:, c * 64:(c + 1) * 64],
                                  start=True, stop=True)
                    if smp:
                        last = mm(rr[0:TS, 1, TP // 2:T // 2], Tt[0:TS, TP:T], X[0:TS, TP // 2:T // 2],
                                  start=True, stop=True)
                    t.did(last, f"dt{m}")
                    if n == 0:
                        pe.wait_ge(v.sem, v.after("kdts", h))
                    pe.wait_ge(v.sem, v.after(f"pred{m}", h))
                    for c in range(NC):
                        cols = slice(c * P, (c + 1) * P)
                        last = tr(rr[:, 2, cols], Tm[:, cols])
                    if smp:
                        last = tr(rr[0:TS, 3, 0:TS], Tm[0:TS, TP:T])
                    t.did(last, f"tr{m}")
                pe.wait_ge(s.sem, s.after("tt64", h))
                for c in range(NC):
                    cols = slice(c * P, (c + 1) * P)
                    if c:
                        pe.wait_ge(v.sem, v.after(f"S{c - 1}", h))
                        t.did(mm(rr[:, 0, cols], K[:, cols], Sp[:, c - 1, :], start=True, stop=True), f"ks{c}")
                        pe.wait_ge(v.sem, v.after(f"r{c}", h))
                    t.did(mm(rr[:, 1, cols], Tt[:, cols], R[:, c, :] if c else vT[:, 0, :], start=True, stop=True),
                          f"vn{c}")
                    pe.wait_ge(s.sem, s.after(f"vn{c}", h))
                    t.did(mm(rr[:, 2, cols], kdT[:, c, :], VN[:, c, :], start=True, stop=True), f"dS{c}")
                for c in range(NC):
                    cols = slice(c * P, (c + 1) * P)
                    last = mm(rr[:, 3, cols], VN[:, c, :], A[:, cols], start=True, stop=(c == 0))
                    if c:
                        last = mm(rr[:, 3, cols], Sp[:, c - 1, :], qe[:, cols], start=False, stop=True)
                t.did(last, "o")
                for b in range(NSEQ):
                    last = mm(rr[:, 0, b * SLEN:(b + 1) * SLEN], S0[:, b, :],
                              K[:, TP + b * SLEN:TP + (b + 1) * SLEN], start=True, stop=True)
                t.did(last, "sks")
                pe.wait_ge(v.sem, v.after("sr3", h))
                t.did(tr(rr[0:TS, 1, 0:P], rt[:]), "srt")
                ready = fixed(pe, s.after("rs", h))
                pe.wait_ge(c_in, 16 * N_CONST)
                pe.wait_ge(s.sem, ready)
                t.did(mm(rr[0:TS, 1, P:2 * P], Tt[0:TS, TP:T], Rs[:], start=True, stop=True), "svn")
                pe.wait_ge(s.sem, s.after("vns", h))
                mm(rr[:, 0, 0:TS], VNs[:], A[0:TS, TP:T], start=True, stop=False)
                for b in range(NSEQ):
                    last = mm(rr[:, 0, b * SLEN:(b + 1) * SLEN], S0[:, b, :],
                              qe[:, TP + b * SLEN:TP + (b + 1) * SLEN], start=False, stop=(b == NSEQ - 1))
                t.did(last, "os")
                pe.wait_ge(v.sem, v.after("vbig", h))
                for a in range(2):
                    last = mm(rr[:, 1 + a, :], kdTs[:], vbig[:, 4 * a:4 * a + 4, :].rearrange("p b n -> p (b n)"),
                              start=True, stop=True)
                t.did(last, "dSs")
                pe.wait_ge(s.sem, s.after("sq2", h))
                pe.wait_ge(v.sem, v.after("snew", h))
                t.did(sum_features(2, sq[:, 0]), "ss")

            def out_proj(U, key):
                v = st[key][0]
                with pe.Fori(0, 2) as i:
                    for j in range(4):
                        pe.wait_ge(v.sem, v.after("lo", H - 1))
                        unit(U, i * 4, j, oh, ol)

            def mlp(U, nkey, ukey):
                v = st[ukey][0]
                with pe.Fori(0, NGRP) as g:
                    for j in range(KT):
                        unit(U, g * (2 * KT), j, xh, xl, wait_norm(nkey) if j == 0 else None)
                    for j in range(KT):
                        unit(U, g * (2 * KT), KT + j, oh, ol,
                             (lambda k: pe.wait_ge(v.sem, v.after(f"lo{k}", g))) if j == 0 else None)

            norm("n0")
            unit(U_HIN, 0, 0, xh, xl, wait_norm("n0"))
            for j in range(1, 4):
                unit(U_HIN, 0, j, xh, xl)
            hgrn_rec(0)
            with pe.Fori(1, H) as h:
                for j in range(4):
                    unit(U_HIN, h * 4, j, xh, xl)
                hgrn_rec(h)
            out_proj(U_HOUT, "hg")
            norm("n1")
            mlp(U_MLP0, "n1", "up0")
            norm("n2")
            unit(U_AB, 0, 0, xh, xl, wait_norm("n2"))
            gdn_pre()
            with pe.Fori(0, H) as h:
                for j in range(4):
                    unit(U_GIN, h * 4, j, xh, xl)
                gdn_rec(h)
            out_proj(U_GOUT, "gd")
            norm("n3")
            mlp(U_MLP1, "n3", "up1")
            norm("n4")
            v, s, t = st["y"]
            for i in range(NC):
                pe.wait_ge(v.sem, v.after("y", i))
                if i:
                    pe.wait_ge(s.sem, s.after("e", i - 1))
                for k in range(KT):
                    last = tr(rr[:, 2 + k // 4, (k % 4) * P:(k % 4 + 1) * P], ycol[i % 2][:, k * P:(k + 1) * P])
                t.did(last, "t")
            v2, s2, t2 = st["ys"]
            pe.wait_ge(v2.sem, v2.after("y", 0))
            pe.wait_ge(s.sem, s.after("e", NC - 1))
            for k in range(KT):
                last = tr(rr[0:TS, 2 + k // 4, (k % 4) * P:(k % 4 + 1) * P], ycol[NC % 2][:, k * P:k * P + TS])
            t2.did(last, "t")

        @block.scalar
        def _(act):
            f = nc.scalar.activation
            sem_of = lambda steps, name, i: act.wait_ge(steps.sem, steps.after(name, i))

            v, s, t = st["init"]
            sem_of(v, "lb1", 0)
            s.did(f(lbt[:, 3], lbt[:, 3], ACT.Exp), "lb1")
            sem_of(v, "lb5", 0)
            s.did(f(lbt[:, 1], lbt[:, 1], ACT.Ln, scale=LN_SHIFT), "lb2")
            s.did(f(lbt[:, 2], lbt[:, 0], ACT.Ln), "lb3")

            def norm(key, u_before):
                _, s, t = st[key]
                if u_before is None:
                    act.wait_ge(st["xs"][0].sem, 1)
                else:
                    act.wait_ge(unit_out, unit_done(u_before))
                for k in range(KT):
                    if k >= 2:
                        sem_of(t, f"sum{k - 2}", 0)
                    s.did(f(sq[:, k % 2], xT[:, k], ACT.Square), f"sq{k}")
                sem_of(t, f"sum{KT - 1}", 0)
                s.did(f(halves(rstd[:]), rr[:, 0:2, 0:HALF], ACT.Ln, bias=epsc[:, 0:1], scale=1.0 / D), "ln")
                sem_of(s, "ln", 0)
                s.did(f(rstd[:], rstd[:], ACT.Exp, scale=-0.5), "rstd")

            def load_state(src, h):
                act.dma_start(S0[:], src[0, :, ds(h, 1)].rearrange("b o k v -> k (o b) v")).then_inc(st_in, 16)

            def load_conv(h):
                src = state_conv[0].rearrange("b j (g h p) -> (b j) g h p", g=3, h=H)
                act.dma_start(cin[:], src[:, :, ds(h, 1), :].rearrange("r g o p -> r g (o p)")).then_inc(st_in, 16)

            def store_states(dst_p, dst_s, h):
                act.dma_start(dst_p[0, 0, ds(h, 1)].rearrange("o k v -> k (o v)"), Sp[:, NC - 1]).then_inc(st_out, 16)
                act.dma_start(dst_s[0, :, ds(h, 1)].rearrange("b o k v -> k (o b) v"), Sn[:]).then_inc(st_out, 16)

            def hgrn_head(h, last=False):
                v, s, t = st["hg"]
                sem_of(v, "neg", h)
                s.did(f(ng[:, 0:3, 0:T], ng[:, 0:3, 0:T], ACT.Exp), "exp")
                sem_of(s, "exp", h)
                s.did(f(ng[:, 0:3, 0:T], ng[:, 0:3, 0:T], ACT.Ln, bias=1.0), "ln")
                sem_of(v, "nabs", h)
                s.did(f(ng[:, 0:3:2, 0:T], ng[:, 0:3:2, 0:T], ACT.Exp), "sig")
                s.did(f(K, b1, ACT.Exp), "k")
                s.did(f(b3, b3, ACT.Exp), "exp2")
                sem_of(s, "exp2", h)
                s.did(f(b3, b3, ACT.Ln, bias=1.0), "ln2")
                sem_of(v, "bd", h)
                f(b3, b1, ACT.Exp)
                s.did(f(b4, b2, ACT.Exp), "ebd")
                for n, m in enumerate(LEVELS):
                    sem_of(v, f"d{m}", h)
                    s.did(f(dd[:, n % 2, 0:width(m)], dd[:, n % 2, 0:width(m)], ACT.Exp), f"e{m}")
                sem_of(t, "vT", h)
                s.did(f(vT[:].rearrange("p c n -> p (c n)"), rr[:, 2, :], ACT.Copy), "vT")
                sem_of(t, "kdT", h)
                s.did(f(kdT[:].rearrange("p c n -> p (c n)"), rr[:, 3, :], ACT.Copy), "kdT")
                sem_of(t, "smp", h)
                f(vTs[:], rr[0:TS, 2, 0:P], ACT.Copy)
                s.did(f(kdTs[:], rr[0:TS, 2, P:2 * P], ACT.Copy), "kdTs")
                sem_of(t, "o", h)
                f(oo[:, 0:TP], rr[:, 0, :], ACT.Copy)
                sem_of(t, "os", h)
                s.did(f(oo[:, TP:T], rr[:, 1, 0:TS], ACT.Copy), "oo")
                sem_of(s, "oo", h)
                s.did(f(sq[:, 0], oo[:], ACT.Square), "sq")
                sem_of(t, "ss", h)
                s.did(f(halves(b2), rr[:, 0:2, 0:HALF], ACT.Ln, bias=epsc[:, 0:1], scale=1.0 / P), "ln3")
                sem_of(s, "ln3", h)
                s.did(f(b2, b2, ACT.Exp, scale=-0.5), "rn")
                sem_of(v, "snew", h)
                store_states(hgrn_p, hgrn_s, h)
                if not last:
                    load_state(state_hgrn, h + 1)
                sem_of(v, "og", h)
                s.did(f(oh[:, ds(h, 1)].rearrange("p o n -> p (o n)"), og[:], ACT.Copy), "hi")

            def gdn_pre():
                v, s, t = st["gp"]
                act.wait_ge(c_in, 16 * N_CONST)
                s.did(f(gsc[0:H, 2:3], gsc[0:H, 0:1], ACT.Exp), "A")
                sem_of(v, "neg", 0)
                s.did(f(B[0:64, 1], B[0:64, 1], ACT.Exp), "exp")
                sem_of(s, "exp", 0)
                s.did(f(B[0:64, 1], B[0:64, 1], ACT.Ln, bias=1.0), "ln")
                sem_of(v, "ls", 0)
                s.did(f(gt4[32:64], B[32:64, 2], ACT.Exp), "be")
                sem_of(v, "dl", 0)
                s.did(f(gt4[64:64 + H], B[0:H, 3], ACT.Exp), "el")
                s.did(f(gt4[96:96 + H], gt4[0:H], ACT.Exp), "eg")
                sem_of(t, "cols", 0)
                f(gcol[:, 0:NC].rearrange("p c n -> p (c n)"), rr[:, 2, :], ACT.Copy)
                s.did(f(gcol[0:TS, NC], rr[0:TS, 3, 0:P], ACT.Copy), "cols")

            def padded_samples(row):
                return row[:, :, SB0:XPW].rearrange("p g (b j) -> p g b j", j=SROW)

            def gdn_head(h):
                v, s, t = st["gd"]
                sem_of(t, "cin", h)
                last = f(padded_samples(xp)[:, :, :, 0:XW],
                         rr[:, 0, 0:96].rearrange("p (g x) -> p g x", g=3)[:, :, 0:XW * NSEQ]
                         .rearrange("p g (b j) -> p g b j", j=XW), ACT.Copy)
                s.did(last, "cin")
                act.wait_ge(unit_out, (h * 4 + (U_GIN + 2)) + 3)
                f(cstash[:, :, 0:XW], xp[:, :, TP:TP + XW], ACT.Copy)
                s.did(f(cstash[:, :, XW:].rearrange("p g (b j) -> p g b j", j=XW),
                        padded_samples(xp)[:, :, :, SLEN:SROW], ACT.Copy), "stash")
                sem_of(t, "stash", h)
                act.wait_ge(st_out, h * 64 + 32 * H)
                s.did(f(cout[:].rearrange("r g p -> r (g p)"), rr[0:XW * (NSEQ + 1), 1, 0:3 * P], ACT.Copy), "cout")
                sem_of(v, "cols", h)
                sem_of(s, "cin", h)
                for g in range(3):
                    last = f(pr[:, g, 0:YW], xp[:, g, 0:YW], ACT.Copy, scale=hcw[:, 0, g:g + 1])
                s.did(last, "tap")
                sem_of(v, "neg", h)
                s.did(f(ng[:, :, 0:YW], ng[:, :, 0:YW], ACT.Exp), "exp")
                sem_of(s, "exp", h)
                s.did(f(ng[:, :, 0:YW], ng[:, :, 0:YW], ACT.Ln, bias=1.0), "ln")
                sem_of(v, "ls", h)
                s.did(f(ng[:, :, 0:YW], ng[:, :, 0:YW], ACT.Exp), "sig")
                sem_of(v, "qkv", h)
                s.did(f(sq[:], q3[:, 0:2], ACT.Square), "sq")
                sem_of(t, "ssq", h)
                s.did(f(B[:, 0:2].rearrange("p g (a n) -> p (g a) n", a=2), rr[:, :, 0:HALF], ACT.Ln,
                        bias=epsc[:, 0:1]), "ln2")
                sem_of(s, "ln2", h)
                s.did(f(B[:, 0:2], B[:, 0:2], ACT.Exp, scale=-0.5), "rn")
                sem_of(t, "gb", h)
                s.did(f(halves(b3), rr[:, 0:2, 0:HALF], ACT.Copy), "gb")
                s.did(f(halves(b4), rr[:, 2:4, 0:HALF], ACT.Copy), "bb")
                sem_of(s, "gb", h)
                s.did(f(kd[:], b3, ACT.Exp), "eg")
                sem_of(v, "dec", h)
                f(dd[:, 1, 0:TP], dd[:, 1, 0:TP], ACT.Exp)
                s.did(f(dd[0:TS, 1, TP:T], dd[0:TS, 1, TP:T], ACT.Exp), "dec")
                sem_of(t, "t0", h)
                f(Tm[:, 0:TP], rr[:, 0, :], ACT.Copy)
                s.did(f(Tm[0:TS, TP:T], rr[0:TS, 1, 0:TS], ACT.Copy), "tm0")
                for m in LEVELS[1:]:
                    sem_of(t, f"x{m}", h)
                    last = f(X[:, 0:TP // 2], rr[:, 0, 0:TP // 2], ACT.Copy)
                    if m in SLEVELS:
                        last = f(X[0:TS, TP // 2:T // 2], rr[0:TS, 0, TP // 2:T // 2], ACT.Copy)
                    s.did(last, f"x{m}")
                    sem_of(t, f"tr{m}", h)
                    last = f(Tt[:, 0:TP], rr[:, 2, :], ACT.Copy)
                    if m in SLEVELS:
                        last = f(Tt[0:TS, TP:T], rr[0:TS, 3, 0:TS], ACT.Copy)
                    s.did(last, f"tt{m}")
                for c in range(NC):
                    sem_of(t, f"vn{c}", h)
                    s.did(f(VN[:, c], rr[:, 1, c * P:(c + 1) * P], ACT.Copy), f"vn{c}")
                sem_of(t, "srt", h)
                s.did(f(Rs[:], rr[0:TS, 1, 0:P], ACT.Copy), "rs")
                sem_of(t, "svn", h)
                s.did(f(VNs[:], rr[0:TS, 1, P:2 * P], ACT.Copy), "vns")
                f(oo[:, 0:TP], rr[:, 3, :], ACT.Copy)
                sem_of(t, "os", h)
                s.did(f(oo[:, TP:T], rr[:, 0, 0:TS], ACT.Copy), "oo")
                sem_of(s, "oo", h)
                s.did(f(sq[:, 0], oo[:], ACT.Square), "sq2")
                sem_of(t, "ss", h)
                s.did(f(halves(b2), rr[:, 2:4, 0:HALF], ACT.Ln, bias=epsc[:, 0:1], scale=1.0 / P), "ln3")
                sem_of(s, "ln3", h)
                s.did(f(b2, b2, ACT.Exp, scale=-0.5), "rn3")
                sem_of(v, "snew", h)
                store_states(gdn_p, gdn_s, h)
                for dst, r0, n in ((conv_p, 0, XW), (conv_s, XW, XW * NSEQ)):
                    d = dst[0].rearrange("b j (g h p) -> (b j) g h p", g=3, h=H)[:, :, ds(h, 1), :]
                    act.dma_start(d.rearrange("r g o p -> r g (o p)"), cout[r0:r0 + n]).then_inc(st_out, 16)
                nxt = h + 1
                with_next(act, nxt)
                sem_of(v, "og", h)
                s.did(f(oh[:, ds(h, 1)].rearrange("p o n -> p (o n)"), og[:], ACT.Copy), "hi")

            def mlp(key):
                v, s, _ = st[key]

                with act.Fori(0, NGRP) as g:
                    for k in range(KT):
                        sem_of(v, f"s{k}", g)
                        s.did(f(oh[:, k], B[:, 2 + k % 2], ACT.Copy), f"hi{k}")

            load_state(state_hgrn, 0)
            norm("n0", None)
            hgrn_head(0)
            with act.Fori(1, H - 1) as h:
                hgrn_head(h)
            hgrn_head(H - 1, last=True)
            load_state(state_gdn, 0)
            load_conv(0)

            def with_next(act, nxt):
                load_state(state_gdn, nxt)
                load_conv(nxt)

            norm("n1", U_MLP0 - 1)
            mlp("up0")
            norm("n2", U_AB - 1)
            gdn_pre()
            with act.Fori(0, H - 1) as h:
                gdn_head(h)
            with_next = lambda act, nxt: None
            gdn_head(H - 1)
            norm("n3", U_MLP1 - 1)
            mlp("up1")
            norm("n4", U_END - 1)
            v, s, t = st["y"]
            for i in range(NC):
                sem_of(t, "t", i)
                if i >= 2:
                    act.wait_ge(y_out[i % 2], 16 * (i // 2))
                s.did(f(xrow[i % 2].rearrange("p (a n) -> p a n", a=2), rr[:, 2:4, :], ACT.Copy), "e")
                sem_of(s, "e", i)
                act.dma_start(y_prompt[0, i * P:(i + 1) * P, :], xrow[i % 2]).then_inc(y_out[i % 2], 16)
            v2, s2, t2 = st["ys"]
            sem_of(t2, "t", 0)
            act.wait_ge(y_out[0], 16 * (NC // 2))
            s2.did(f(xrow[NC % 2][0:TS].rearrange("p (a n) -> p a n", a=2), rr[0:TS, 2:4, :], ACT.Copy), "e")
            sem_of(s2, "e", 0)
            act.dma_start(y_sample.rearrange("b t d -> (b t) d"), xrow[NC % 2][0:TS]).then_inc(y_out[0], 16)
            act.wait_ge(y_out[0], 16 * (NC // 2 + 1))
            act.wait_ge(y_out[1], 16 * (NC // 2))
            act.wait_ge(st_out, 32 * H + 64 * H)

        @block.vector
        def _(dve):
            tt, ts, stt, cp = nc.vector.tensor_tensor, nc.vector.tensor_scalar, nc.vector.scalar_tensor_tensor, nc.vector.tensor_copy
            pred = nc.vector.copy_predicated
            dve.wait_ge(c_in, 16 * N_CONST)
            for n, stage_ in enumerate((B, ng)):
                cp(cu[:, n * CU_HALF:(n + 1) * CU_HALF], stage_[:].rearrange("p a n -> p (a n)")[:, 0:CU_HALF])

            def after(steps, name, i):
                dve.wait_ge(steps.sem, steps.after(name, i))

            v, s, t = st["init"]
            nc.vector.memset(epsc[:], EPS).then_inc(unit_out, 2)
            for buf in (KL[:], QL[:], A[:], gt4[:], gcol[:], dtb[:], pr[:, 3, T:XPW]):
                nc.vector.memset(buf, 0.0)
            v.did(nc.vector.memset(zeros[:], 0.0), "fill")
            after(t, "vec", 0)
            v.did(cp(vec[:], rr[:, 0, 0:V_N]), "vec")
            nc.vector.memset(xp[:], 0.0)
            v.did(cp(cw[:].rearrange("p j s -> p (j s)"), rr[:, 1, 0:CONV * 3 * H]), "cw")
            lb = vec[:, V_LB:V_LB + H]
            after(v, "vec", 0)
            v.did(tt(lbt[:, 3], lb, lb, ALU.subtract), "lb1")
            after(s, "lb1", 0)
            v.did(nc.vector.reciprocal(lbt[:, 2], lbt[:, 3]), "lb2")
            after(v, "lb2", 0)
            v.did(tt(lbt[:, 3], lbt[:, 3], lbt[:, 2], ALU.mult), "lb3")
            after(v, "lb3", 0)
            v.did(tt(lbt[:, 3], lbt[:, 3], lbt[:, 3], ALU.subtract), "lb4")
            after(v, "lb4", 0)
            ts(lbt[:, 0], lbt[:, 3], -1.0, 1.0, ALU.mult, ALU.add)
            v.did(ts(lbt[:, 1], lbt[:, 3], LB_FLOOR, None, ALU.max), "lb5")
            after(s, "lb3", 0)
            v.did(ts(lbt[:, 1], lbt[:, 1], float(-np.log(LN_SHIFT)), None, ALU.add), "lb6")

            v, s, t = st["x"]
            for i in range(NC):
                after(t, "t", i)
                v.did(cp(xT[:, :, i * P:(i + 1) * P], rr[:, 2:4, :].rearrange("p a (k n) -> p (a k) n", n=P)), "copy")
            v2, _, t2 = st["xs"]
            after(t2, "t", 0)
            v2.did(cp(xT[:, :, TP:T], rr[:, 2, 0:KT * TS].rearrange("p (k n) -> p k n", n=TS)), "copy")

            def norm(key, wcol, u_before):
                v, _, _ = st[key]
                if u_before is None:
                    after(st["xs"][0], "copy", 0)
                else:
                    dve.wait_ge(unit_out, unit_done(u_before))
                for k in range(KT):
                    w = vec[:, wcol + k:wcol + k + 1]
                    v.did(ts(xh[:, k], xT[:, k], w, None, ALU.mult), f"hi{k}")
                    after(v, f"hi{k}", 0)
                    v.did(stt(out=xl[:, k], in0=xT[:, k], scalar=w, in1=xh[:, k].bitcast(F32),
                              op0=ALU.mult, op1=ALU.subtract), f"lo{k}")

            def computed(U, r, j):
                dve.wait_ge(w_used, r + (U + j + 1))
                return psum_out((U + j) % SPLIT)

            def out_tail(h, v, s, wcol):
                after(s, "rn" if v is st["hg"][0] else "rn3", h)
                v.did(stt(out=og[:], in0=oo[:], scalar=vec[:, wcol:wcol + 1], in1=b2, op0=ALU.mult, op1=ALU.mult), "on")
                after(v, "on", h)
                v.did(tt(og[:], og[:], gate[:], ALU.mult), "og")
                after(s, "hi", h)
                v.did(tt(ol[:, ds(h, 1)].rearrange("p o n -> p (o n)"), og[:],
                         oh[:, ds(h, 1)].rearrange("p o n -> p (o n)"), ALU.subtract), "lo")

            def last_of(ap, m):
                b = blocks(ap, m)
                return b[:, :, m - 1:m].broadcast_to([b.shape[0], b.shape[1], m])

            def less_than_last(out, ap):
                tt(blocks(out[:, 0:TP], P), last_of(ap[:, 0:TP], P), blocks(ap[:, 0:TP], P), ALU.subtract)
                return tt(blocks(out[:, TP:T], SLEN), last_of(ap[:, TP:T], SLEN), blocks(ap[:, TP:T], SLEN), ALU.subtract)

            def over_chunks(ap):
                return ap.unsqueeze(1).broadcast_to([ap.shape[0], NC, P])

            def sample_states(h, v, s, t, vs, decay, bank):
                v.did(tt(vbig[:], vs[:].unsqueeze(1).broadcast_to([TS, NSEQ, P]),
                         cf[0:TS, C_SEQ:C_SEQ + NSEQ].unsqueeze(2).broadcast_to([TS, NSEQ, P]), ALU.mult), "vbig")
                after(t, "os", h)
                v.did(tt(Sn[:], S0[:], blocks(decay[:, TP:T], SLEN)[:, :, SLEN - 1:SLEN].broadcast_to([P, NSEQ, P]),
                         ALU.mult), "sdec")
                after(t, "dSs", h)
                after(v, "sdec", h)
                v.did(tt(Sn[:], Sn[:], rr[:, bank:bank + 2, :].rearrange("p a (b n) -> p (a b) n", n=P), ALU.add), "snew")

            def prompt_state(c, h, v, decay):
                bank = rr[:, 2, c * P:(c + 1) * P]
                if c == 0:
                    v.did(cp(Sp[:, 0], bank), "S0")
                else:
                    after(v, f"S{c - 1}", h)
                    v.did(stt(out=Sp[:, c], in0=Sp[:, c - 1], scalar=decay[:, c * P + P - 1:c * P + P], in1=bank,
                              op0=ALU.mult, op1=ALU.add), f"S{c}")

            def hgrn_head(h):
                v, s, t = st["hg"]
                v.did(cp(hc[:, 0:3], lbt[:, 0:3, ds(h, 1)].rearrange("p r o -> p (r o)")), "cols")
                for j, dst in enumerate((pr[:, 0, 0:T], pr[:, 1, 0:T], val, pr[:, 2, 0:T])):
                    tt(halves(dst), computed(U_HIN, h * 4, j), halves(rstd[:]), ALU.mult).then_inc(unit_out, 1)
                dve.wait_ge(unit_out, h * 4 + (U_HIN + 3) + 3)
                if not isinstance(h, int) or h > 0:
                    dve.wait_ge(st_out, h * 32)
                p3, n3 = pr[:, 0:3, 0:T], ng[:, 0:3, 0:T]
                v.did(stt(out=n3, in0=p3, scalar=-1.0, in1=p3, op0=ALU.mult, op1=ALU.min), "neg")
                after(s, "ln", h)
                v.did(stt(out=n3, in0=p3, scalar=0.0, in1=n3, op0=ALU.min, op1=ALU.subtract), "ls")
                after(v, "ls", h)
                tt(b1, ng[:, 1, 0:T], pr[:, 1, 0:T], ALU.subtract)
                v.did(ts(b2, ng[:, 1, 0:T], hc[:, 2:3], hc[:, 1:2], ALU.add, ALU.subtract), "cd")
                after(v, "cd", h)
                v.did(stt(out=b3, in0=b2, scalar=-1.0, in1=b2, op0=ALU.mult, op1=ALU.min), "nabs")
                v.did(ts(b4, ng[:, 1, 0:T], hc[:, 2:3], hc[:, 1:2], ALU.add, ALU.max), "cmax")
                after(s, "sig", h)
                v.did(tt(Q, pr[:, 0, 0:T], ng[:, 0, 0:T], ALU.mult), "q")
                v.did(tt(gate[:], pr[:, 2, 0:T], ng[:, 2, 0:T], ALU.mult), "gate")
                after(s, "k", h)
                v.did(ts(K, K, hc[:, 0:1], None, ALU.mult), "k")
                after(s, "ln2", h)
                after(v, "cmax", h)
                v.did(tt(b4, b4, b3, ALU.add), "lf")
                after(v, "lf", h)
                v.did(nc.vector.tensor_tensor_scan(b1, reset, b4, 0.0, ALU.mult, ALU.add), "b")
                after(v, "b", h)
                v.did(less_than_last(b2, b1), "bd")
                after(s, "ebd", h)
                v.did(tt(qe[:], Q, b3, ALU.mult), "qe")
                v.did(tt(kd[:], K, b4, ALU.mult), "kd")

                def differences(n, m):
                    w = width(m)
                    mid = first_half(b1[:, 0:w], m)[:, :, m - 1:m].broadcast_to([P, w // (2 * m), m])
                    if n >= 2:
                        after(v, f"kl{LEVELS[n - 2]}", h)
                    tt(second_half(dd[:, n % 2, 0:w], m), second_half(b1[:, 0:w], m), mid, ALU.subtract)
                    v.did(tt(first_half(dd[:, n % 2, 0:w], m), mid, first_half(b1[:, 0:w], m), ALU.subtract), f"d{m}")

                def keep(n, m):
                    ready, kept = fixed(dve, t.after(f"lv{m}", h)), fixed(dve, v.after(f"pred{m // 2}" if n else "adiag", h))
                    dve.wait_ge(c_in, 16 * N_CONST)
                    dve.wait_ge(t.sem, ready)
                    dve.wait_ge(v.sem, kept)
                    last = pred(second_half(A[:, 0:TP], m), blocks(mask[:, 0, n, 0:TP // 2], m),
                                blocks(rr[:, n % 2, 0:TP // 2], m))
                    if m in SLEVELS:
                        last = pred(second_half(A[0:TS, TP:T], m), blocks(mask[0:TS, 0, n, TP // 2:T // 2], m),
                                    blocks(rr[0:TS, n % 2, TP // 2:T // 2], m))
                    v.did(last, f"pred{m}")

                differences(0, 1)
                after(t, "diag", h)
                tt(blocks(A[:, 0:TP], P), blocks(rr[:, 2, :], P), over_chunks(eye), ALU.mult)
                v.did(tt(A[0:TS, TP:T], rr[0:TS, 3, 0:TS], cf[0:TS, C_EYE:C_EYE + TS], ALU.mult), "adiag")
                after(v, "adiag", h)
                for n, m in enumerate(LEVELS):
                    w = width(m)
                    if m < LEVELS[-1]:
                        differences(n + 1, 2 * m)
                    after(s, f"e{m}", h)
                    if n >= 2:
                        after(t, f"lv{LEVELS[n - 2]}", h)
                    tt(blocks(QL[:, n % 2, 0:w // 2], m), second_half(Q[:, 0:w], m), second_half(dd[:, n % 2, 0:w], m), ALU.mult)
                    v.did(tt(first_half(KL[:, n % 2, 0:w], m), first_half(K[:, 0:w], m), first_half(dd[:, n % 2, 0:w], m),
                             ALU.mult), f"kl{m}")
                    if n:
                        keep(n - 1, LEVELS[n - 1])
                keep(len(LEVELS) - 1, LEVELS[-1])
                after(t, "dS", h)
                for c in range(NC):
                    prompt_state(c, h, v, b3)
                after(s, "kdTs", h)
                sample_states(h, v, s, t, vTs, b3, 2)
                out_tail(h, v, s, V_HON)

            def gdn_pre():
                v, s, t = st["gp"]
                cp(dtb[0:H], gsc[0:H, 1:2]).then_inc(dt_ready, 1)
                b = [B[0:64, n] for n in range(4)]
                tt(halves(b[0]), computed(U_AB, 0, 0)[0:64], halves(rstd[0:64]), ALU.mult).then_inc(unit_out, 1)
                dve.wait_ge(unit_out, unit_done(U_AB))
                dve.wait_ge(dt_ready, 1)
                v.did(ts(b[0], b[0], dtb[:, 0:1], None, ALU.add), "x")
                after(v, "x", 0)
                v.did(stt(out=b[1], in0=b[0], scalar=-1.0, in1=b[0], op0=ALU.mult, op1=ALU.min), "neg")
                after(s, "ln", 0)
                v.did(stt(out=b[2], in0=b[0], scalar=0.0, in1=b[1], op0=ALU.min, op1=ALU.subtract), "ls")
                v.did(stt(out=b[3][0:H], in0=b[0][0:H], scalar=0.0, in1=b[1][0:H], op0=ALU.max, op1=ALU.add), "g")
                after(v, "g", 0)
                v.did(ts(b[3][0:H], b[3][0:H], gsc[:, 2:3], -1.0, ALU.mult, ALU.mult), "g2")
                after(v, "g2", 0)
                v.did(nc.vector.tensor_tensor_scan(gt4[0:H], reset[0:H], b[3][0:H], 0.0, ALU.mult, ALU.add), "scan")
                after(v, "scan", 0)
                v.did(less_than_last(b[3][0:H], gt4[0:H]), "dl")

            def gdn_head(h):
                v, s, t = st["gd"]
                cp(hc[:, 4:5], cf[:, ds(h + C_HSEL, 1)])
                cp(hcw[:], cw[:].rearrange("p j (g x) -> p j g x", g=3)[:, :, :, ds(h, 1)].rearrange("p j g o -> p j (g o)"))
                v.did(cp(gcols[:], gcol[:].rearrange("p c (r x) -> p c r x", x=32)[:, :, :, ds(h, 1)]
                         .rearrange("p c r o -> p c (r o)")), "cols")
                after(v, "cols", h)
                v.did(stt(out=nbe[:], in0=gcols[:, :, 1], scalar=-1.0, in1=gcols[:, :, 3], op0=ALU.mult, op1=ALU.mult), "nbe")
                v.did(ts(gsel[:], gt4[:], hc[:, 4:5], None, ALU.mult), "gsel")
                for j in range(3):
                    ps = computed(U_GIN, h * 4, j)
                    cut = TP - HALF
                    tt(xp[:, j, XW:XW + HALF], ps[:, 0], rstd[:, 0:HALF], ALU.mult)
                    tt(xp[:, j, XW + HALF:XW + TP], ps[:, 1, 0:cut], rstd[:, HALF:TP], ALU.mult)
                    tt(blocks(xp[:, j, SB0:XPW], SROW)[:, :, XW:SROW], blocks(ps[:, 1, cut:HALF], SLEN),
                       blocks(rstd[:, TP:T], SLEN), ALU.mult).then_inc(unit_out, 1)
                tt(halves(pr[:, 3, 0:T]), computed(U_GIN, h * 4, 3), halves(rstd[:]), ALU.mult).then_inc(unit_out, 1)
                dve.wait_ge(unit_out, h * 4 + (U_GIN + 3) + 3)
                after(s, "tap", h)
                for j in range(1, CONV):
                    if j > 1:
                        after(v, f"tap{j - 1}", h)
                    for g in range(3):
                        last = stt(out=pr[:, g, 0:YW], in0=xp[:, g, j:j + YW], scalar=hcw[:, j, g:g + 1],
                                   in1=pr[:, g, 0:YW], op0=ALU.mult, op1=ALU.add)
                    v.did(last, f"tap{j}")
                after(v, "tap3", h)
                dve.wait_ge(st_out, h * 64 + 32 * H)
                p4, n4 = pr[:, :, 0:YW], ng[:, :, 0:YW]
                v.did(stt(out=n4, in0=p4, scalar=-1.0, in1=p4, op0=ALU.mult, op1=ALU.min), "neg")
                after(s, "ln", h)
                v.did(stt(out=n4, in0=p4, scalar=0.0, in1=n4, op0=ALU.min, op1=ALU.subtract), "ls")
                after(s, "sig", h)
                tt(q3[:, :, 0:TP], pr[:, 0:3, 0:TP], ng[:, 0:3, 0:TP], ALU.mult)

                def conv_samples(x):
                    return x[:, 0:3, SB0:XPW].rearrange("p g (b j) -> p g b j", j=SROW)[:, :, :, 0:SLEN]

                for g in range(3):
                    last = tt(blocks(q3[:, g, TP:T], SLEN), blocks(pr[:, g, SB0:XPW], SROW)[:, :, 0:SLEN],
                              blocks(ng[:, g, SB0:XPW], SROW)[:, :, 0:SLEN], ALU.mult)
                v.did(last, "qkv")
                v.did(tt(gate[:], pr[:, 3, 0:T], ng[:, 3, 0:T], ALU.mult), "gate")
                after(s, "rn", h)
                tt(K, K, b2, ALU.mult)
                v.did(stt(out=Q, in0=Q, scalar=float(P) ** -0.5, in1=b1, op0=ALU.mult, op1=ALU.mult), "qh")
                after(s, "eg", h)
                after(v, "qh", h)
                v.did(tt(dd[:, 0], K, b4, ALU.mult), "kb")
                v.did(tt(qe[:], Q, kd[:], ALU.mult), "qg")
                for c in range(NC):
                    cols = slice(c * P, (c + 1) * P)
                    ts(dd[:, 1, cols], b3[:, cols], gcols[:, c, 0:1], 0.0, ALU.subtract, ALU.min)
                v.did(ts(dd[0:TS, 1, TP:T], b3[0:TS, TP:T], gcols[0:TS, NC, 0:1], 0.0, ALU.subtract, ALU.min), "dec")
                after(s, "dec", h)
                dec, decs = dd[:, 1, 0:TP], dd[0:TS, 1, TP:T]
                tt(blocks(dec, P), blocks(dec, P), over_chunks(cf[:, C_INCL:C_INCL + P]), ALU.mult)
                v.did(tt(decs, decs, cf[0:TS, C_INCLS:C_INCLS + TS], ALU.mult), "incl")
                after(v, "incl", h)
                after(t, "sm", h)
                tt(A[:, 0:TP], rr[:, 1, :], dec, ALU.mult)
                tt(A[0:TS, TP:T], rr[0:TS, 2, TS:2 * TS], decs, ALU.mult)
                tt(NLt[:, 0:TP], rr[:, 0, :], dec, ALU.mult)
                v.did(tt(NLt[0:TS, TP:T], rr[0:TS, 2, 0:TS], decs, ALU.mult), "nl")
                after(v, "nl", h)
                tt(blocks(NLt[:, 0:TP], P), blocks(NLt[:, 0:TP], P), over_chunks(cf[:, C_NSTR:C_NSTR + P]), ALU.mult)
                v.did(tt(NLt[0:TS, TP:T], NLt[0:TS, TP:T], cf[0:TS, C_NSTRS:C_NSTRS + TS], ALU.mult), "nl2")
                cp(blocks(Tt[:, 0:TP], P), over_chunks(eye))
                v.did(cp(Tt[0:TS, TP:T], cf[0:TS, C_EYE:C_EYE + TS]), "tt0")
                ready = fixed(dve, v.after("tt0", h))
                dve.wait_ge(c_in, 16 * N_CONST)
                dve.wait_ge(v.sem, ready)
                pred(second_half(Tt[:, 0:TP], 1), blocks(mask[:, 0, 0, 0:TP // 2], 1), second_half(NLt[:, 0:TP], 1))
                v.did(pred(second_half(Tt[0:TS, TP:T], 1), blocks(mask[0:TS, 0, 0, TP // 2:T // 2], 1),
                           second_half(NLt[0:TS, TP:T], 1)), "tt1")
                after(t, "vT", h)
                v.did(tt(vT[:], blocks(rr[:, 2, :], P), gcols[:, 0:NC, 1:2].broadcast_to([P, NC, P]), ALU.mult), "vb")
                after(t, "kT", h)
                v.did(tt(kdT[:], blocks(rr[:, 3, :], P), gcols[:, 0:NC, 2:3].broadcast_to([P, NC, P]), ALU.mult), "kdt")
                after(t, "vks", h)
                v.did(ts(kdTs[:], rr[0:TS, 2, 0:P], gcols[0:TS, NC, 2:3], None, ALU.mult), "kdts")
                for n, m in enumerate(LEVELS[1:], 1):
                    if n == 1:
                        after(s, "tm0", h)
                    ready = fixed(dve, t.after(f"dt{m}", h))
                    dve.wait_ge(c_in, 16 * N_CONST)
                    dve.wait_ge(t.sem, ready)
                    last = pred(first_half(Tm[:, 0:TP], m), blocks(mask[:, 1, n, 0:TP // 2], m), blocks(rr[:, 1, 0:TP // 2], m))
                    if m in SLEVELS:
                        last = pred(first_half(Tm[0:TS, TP:T], m), blocks(mask[0:TS, 1, n, TP // 2:T // 2], m),
                                    blocks(rr[0:TS, 1, TP // 2:T // 2], m))
                    v.did(last, f"pred{m}")
                for c in range(NC):
                    if c:
                        after(t, f"ks{c}", h)
                        v.did(stt(out=R[:, c], in0=rr[:, 0, c * P:(c + 1) * P], scalar=nbe[:, c:c + 1], in1=vT[:, c],
                                  op0=ALU.mult, op1=ALU.add), f"r{c}")
                    after(t, f"dS{c}", h)
                    prompt_state(c, h, v, kd)
                after(t, "sks", h)
                v.did(tt(rt[:], rr[:, 0, 0:TS], kd[:, TP:T], ALU.mult), "sr1")
                after(v, "sr1", h)
                v.did(tt(rt[:], val[:, TP:T], rt[:], ALU.subtract), "sr2")
                after(v, "sr2", h)
                v.did(tt(rt[:], rt[:], b4[:, TP:T], ALU.mult), "sr3")
                after(s, "vns", h)
                sample_states(h, v, s, t, VNs, kd, 1)
                out_tail(h, v, s, V_GON)

            def out_proj(U):
                with dve.Fori(0, 2) as i:
                    for j in range(4):
                        x = xT[:, ds(i * 4 + j, 1)].rearrange("p o (a n) -> p (o a) n", a=2)
                        tt(x, x, computed(U, i * 4, j), ALU.add).then_inc(unit_out, 1)

            def mlp(U, nkey, key):
                v, s, _ = st[key]
                after(st[nkey][1], "rstd", 0)
                with dve.Fori(0, NGRP) as g:
                    r = g * (2 * KT)

                    def rest(k):
                        after(s, f"hi{k}", g)
                        v.did(tt(ol[:, k], B[:, 2 + k % 2], oh[:, k], ALU.subtract), f"lo{k}")

                    for k in range(KT):
                        tt(halves(B[:, k % 2]), computed(U, r, k), halves(rstd[:]), ALU.mult).then_inc(unit_out, 1)
                        dve.wait_ge(unit_out, r + (U + k + 3))
                        v.did(stt(out=B[:, 2 + k % 2], in0=B[:, k % 2], scalar=0.0, in1=B[:, k % 2],
                                  op0=ALU.max, op1=ALU.mult), f"s{k}")
                        if k:
                            rest(k - 1)
                    rest(KT - 1)
                    for k in range(KT):
                        tt(halves(xT[:, k]), halves(xT[:, k]), computed(U, r, KT + k), ALU.add).then_inc(unit_out, 1)

            norm("n0", V_MIX, None)
            after(st["n0"][1], "rstd", 0)
            hgrn_head(0)
            with dve.Fori(1, H) as h:
                hgrn_head(h)
            out_proj(U_HOUT)
            norm("n1", V_MLP, U_MLP0 - 1)
            mlp(U_MLP0, "n1", "up0")
            norm("n2", V_MIX + KT, U_AB - 1)
            after(st["n2"][1], "rstd", 0)
            gdn_pre()
            after(st["gp"][1], "cols", 0)
            with dve.Fori(0, H) as h:
                gdn_head(h)
            out_proj(U_GOUT)
            norm("n3", V_MLP + KT, U_MLP1 - 1)
            mlp(U_MLP1, "n3", "up1")
            after(st["n4"][1], "rstd", 0)
            dve.wait_ge(st_out, (32 + 64) * H)

            def result(i, cols, steps):
                n = cols.stop - cols.start
                for k in range(KT):
                    last = stt(out=ycol[i % 2][:, k * P:k * P + n], in0=xT[:, k, cols], scalar=vec[:, V_FIN + k:V_FIN + k + 1],
                               in1=rstd[:, cols], op0=ALU.mult, op1=ALU.mult)
                steps.did(last, "y")

            v, s, t = st["y"]
            for i in range(NC):
                if i >= 2:
                    after(t, "t", i - 2)
                result(i, slice(i * P, (i + 1) * P), v)
            after(t, "t", NC - 2)
            result(NC, slice(TP, T), st["ys"][0])


_INS = ['x_prompt', 'x_sample', 'state_hgrn', 'state_gdn', 'state_gdn_conv', 'norm_mix', 'norm_mlp', 'norm_final',
        'hgrn_w_in', 'hgrn_lb', 'hgrn_out_norm', 'hgrn_w_out', 'gdn_w_in', 'gdn_conv_w', 'gdn_A_log', 'gdn_dt_bias',
        'gdn_out_norm', 'gdn_w_out', 'mlp_w_up', 'mlp_w_down']
_OUTS = [(1, TP, D), (NSEQ, SLEN, D), (1, 1, H, P, P), (1, NSEQ, H, P, P), (1, 1, H, P, P), (1, NSEQ, H, P, P),
         (1, 1, XW, 3 * D), (1, NSEQ, XW, 3 * D)]


def kernel(**inputs):
    import concourse.bacc as _bacc
    from concourse.bass_utils import run_bass_kernel_spmd as _run

    nc = _bacc.Bacc("TRN2", target_bir_lowering=False, num_devices=1)
    arrays, args = {}, []
    named = [(name, np.ascontiguousarray(inputs[name])) for name in _INS]
    named += list(zip(("const_f", "const_u"), shape_constants()))
    for name, a in named:
        arrays[f"in_{name}_dram"] = a
        args.append(nc.dram_tensor(f"in_{name}_dram", a.shape, mybir.dt.from_np(a.dtype), kind="ExternalInput").ap())
    for i, shape in enumerate(_OUTS):
        args.append(nc.dram_tensor(f"out_{i}_dram", shape, F32, kind="ExternalOutput").ap())
    build(nc, *args)
    r = _run(nc, [arrays], core_ids=[0])
    return tuple(r.results[0][f"out_{i}_dram"] for i in range(len(_OUTS)))
```

```python
from contextlib import ExitStack

import numpy as np

import concourse.bass as bass
from concourse import mybir

F32 = mybir.dt.float32
F32R = mybir.dt.float32r
U8 = mybir.dt.uint8
ALU = mybir.AluOpType
ACT = mybir.ActivationFunctionType
ds = bass.ds

P = 128
D = 1024
KT = D // P
TP = 512
NSEQ, SLEN = 8, 4
TS = NSEQ * SLEN
T = TP + TS
HALF = T // 2
NC = TP // P
H = 8
FF = 4 * D
NGRP = FF // D
EPS = 1e-6
LB_FLOOR = 1e-30
LN_SHIFT = 2.0 ** 60
CONV = 4
XW = CONV - 1
SB0 = XW + TP
SROW = XW + SLEN
XPW = SB0 + NSEQ * SROW
YW = XPW - XW
LEVELS = [1, 2, 4, 8, 16, 32, 64]
SLEVELS = [m for m in LEVELS if 2 * m <= SLEN]
RAW, SPLIT = 4, 2

V_MIX, V_MLP, V_FIN, V_LB, V_HON, V_GON, V_CONV = 0, 16, 32, 40, 48, 49, 50
V_N = V_CONV

C_EYE, C_INCL, C_NSTR, C_IND, C_RESET, C_SEQ, C_INCLS, C_NSTRS, C_HSEL = 0, 128, 256, 384, 640, 1184, 1192, 1224, 1256
C_W = C_HSEL + H
CU_HALF = len(LEVELS) * (T // 2)

WS_ROWS = 22
HGRN_ORDER = [1, 0, 3, 2]
GDN_ORDER = [1, 0, 2, 3]
Q_ROW, K_ROW, V_ROW = 0, 1, 2
GDN_SLOTS = ["L1", "L2", "L3", "L4", "L5", "L6", "C0", "C1", "C2", "C3"]

SKS, OS, SRT = 288, 320, 352
SVN = 288
RS, VNS = T // 2, T // 2 + P


def shape_constants():
    cf = np.zeros((P, C_W), np.float32)
    p = np.arange(P)
    cf[:, C_EYE:C_EYE + P] = np.eye(P)
    cf[:, C_INCL:C_INCL + P] = p[None, :] >= p[:, None]
    cf[:, C_NSTR:C_NSTR + P] = -(p[None, :] > p[:, None]).astype(np.float32)
    cf[0:32, C_IND:C_IND + P] = 1
    cf[32:64, C_IND + P:C_IND + 2 * P] = 1
    t = np.arange(T)
    first = np.where(t < TP, t % P == 0, (t - TP) % SLEN == 0)
    cf[:, C_RESET:C_RESET + T] = ~first
    s = np.arange(TS)
    cf[:TS, C_SEQ:C_SEQ + NSEQ] = s[:, None] // SLEN == np.arange(NSEQ)[None, :]
    same = s[:, None] // SLEN == s[None, :] // SLEN
    cf[:TS, C_INCLS:C_INCLS + TS] = same & (s[None, :] >= s[:, None])
    cf[:TS, C_NSTRS:C_NSTRS + TS] = -(same & (s[None, :] > s[:, None])).astype(np.float32)
    cf[:, C_HSEL:C_HSEL + H] = p[:, None] % 32 == np.arange(H)[None, :]
    cu = np.zeros((P, 2, len(LEVELS), T // 2), np.float32)
    for n, m in enumerate(LEVELS):
        c = np.arange(T // 2)
        blk, local = c // m, np.where(c < TP // 2, (c // m) % (P // (2 * m)), (c - TP // 2) // m)
        rb, rh = p // (2 * m), (p // m) % 2
        hit = rb[:, None] == local[None, :]
        cu[:, 0, n] = hit & (rh[:, None] == 0)
        cu[:, 1, n] = hit & (rh[:, None] == 1)
    return cf, cu.reshape(P, -1)


N_CONST = 12


class Steps:

    def __init__(self, sem, names):
        self.sem, self.names, self.at = sem, names, 0

    def did(self, instruction, name):
        assert self.names[self.at % len(self.names)] == name, (self.names[self.at % len(self.names)], name)
        self.at += 1
        instruction.then_inc(self.sem, 1)

    def after(self, name, i):
        return i * len(self.names) + (self.names.index(name) + 1)


def fixed(eng, value):
    return value if isinstance(value, int) else eng.to_reg(value)


def build(nc, x_prompt, x_sample, state_hgrn, state_gdn, state_conv, norm_mix, norm_mlp, norm_final, hgrn_w_in,
          hgrn_lb, hgrn_out_norm, hgrn_w_out, gdn_w_in, gdn_conv_w, gdn_A_log, gdn_dt_bias, gdn_out_norm, gdn_w_out,
          mlp_w_up, mlp_w_down, const_f, const_u, y_prompt, y_sample, hgrn_p, hgrn_s, gdn_p, gdn_s, conv_p, conv_s):
    with ExitStack() as ctx:
        def sb(name, shape, dt=F32):
            return ctx.enter_context(nc.sbuf_tensor(name, shape, dt))

        def sem(name):
            return ctx.enter_context(nc.semaphore(name))

        xT = sb("xT", [P, KT, T])
        xh = sb("xh", [P, KT, T], F32R)
        xl = sb("xl", [P, KT, T], F32R)
        oh = sb("oh", [P, KT, T], F32R)
        ol = sb("ol", [P, KT, T], F32R)
        w_raw = sb("w_raw", [P, RAW, KT, P])
        w_hi = sb("w_hi", [P, SPLIT, KT, P], F32R)
        w_lo = sb("w_lo", [P, SPLIT, KT, P], F32R)
        cf = sb("cf", [P, C_W])
        cu = sb("cu", [P, 2 * len(LEVELS) * (T // 2)], U8)
        vec = sb("vec", [P, V_N])
        cw = sb("cw", [P, CONV, 3 * H])
        hc = sb("hc", [P, 16])
        lbt = sb("lbt", [P, 4, H])
        ones = sb("ones", [P, P])
        epsc = sb("epsc", [P, 2])
        zeros = sb("zeros", [P, 1])
        rstd = sb("rstd", [P, T])
        eye = cf[:, C_EYE:C_EYE + P]
        reset = cf[:, C_RESET:C_RESET + T]
        mask = cu[:, :].rearrange("p (a l n) -> p a l n", a=2, l=len(LEVELS))

        ws = sb("ws", [P, WS_ROWS, T])

        def rows(names):
            at, out = 0, {}
            for entry in names:
                name, n = entry if isinstance(entry, tuple) else (entry, 1)
                out[name] = ws[:, at] if n == 1 else ws[:, at:at + n]
                at += n
            assert at <= WS_ROWS
            return out

        xrow = [ws[:, 0:4].rearrange("p a n -> p (a n)")[:, n * D:(n + 1) * D] for n in range(2)]
        ycol = [ws[:, 4:8].rearrange("p a n -> p (a n)")[:, n * D:(n + 1) * D] for n in range(2)]
        cstage = [ws[:, n:n + 4].rearrange("p a n -> p (a n)")[:, 0:CU_HALF] for n in (8, 12)]
        sq = ws[:, 16:18]
        B = ws[:, 0:4]

        pr = sb("pr", [P, 3, XPW])
        ng = sb("ng", [P, 3, XPW])
        xp = sb("xp", [P, 2, XPW])
        hg = rows(["Q", "K", "val", "gate", "b", "bd", "eb", "oo", "qe", "kd", "QL", "A", "sq", ("dd", 2), ("KL", 2),
                   "vT", "kdT", ("vbig", 2)])
        gd = rows(["nQ", "nK", "nV", "work", "G", "beta", "eG", "dec",
                   "K", "qe", "gate", "A", "NL", "Tm", "Tt", "X", "kdT", "vT", "VN", "oo", "sq", "spare"])
        QL = hg["QL"].rearrange("p (a n) -> p a n", a=2)
        gd_vbig = [gd[n][0:TS, 0:4 * P] for n in ("Tm", "spare")]
        vTs = sb("vTs", [TS, P])
        kdTs = sb("kdTs", [TS, P])
        Sp = sb("Sp", [P, NC, P])
        S0 = sb("S0", [P, NSEQ, P])
        gt4 = sb("gt4", [P, T])
        gcol = sb("gcol", [P, NC + 1, 4 * H])
        gnext = sb("gnext", [P, NC + 1])
        gcols = sb("gcols", [P, NC + 1, 4])
        nbe = sb("nbe", [P, NC + 1])
        eGs = sb("eGs", [P, NC + TS])
        betas = sb("betas", [P, TS])
        hcw = sb("hcw", [P, CONV, 3])
        rt = sb("rt", [P, TS])
        hist = sb("hist", [P, 3, XW * NSEQ])
        cstash = sb("cstash", [P, 3, XW * (NSEQ + 1)])
        cout = sb("cout", [XW * (NSEQ + 1), 3, P])
        cin = sb("cin", [XW * NSEQ, 3, P])
        gsc = sb("gsc", [H, 4])
        dtb = sb("dtb", [64, 1])

        pj = ctx.enter_context(nc.psum_tensor("pj", [P, 2, 2, 512], F32))
        rr = ctx.enter_context(nc.psum_tensor("rr", [P, 4, 512], F32))

        w_in = [sem(f"weights_loaded{j}") for j in range(RAW)]
        ab_in = sem("ab_loaded")
        w_split = sem("weights_split")
        w_used = sem("weights_used")
        unit_out = sem("unit_evacuated")
        c_in = sem("constants_loaded")
        x_in = [sem(f"x_loaded{n}") for n in range(2)]
        st_in = sem("state_loaded")
        st_out = sem("state_stored")
        cv_in = sem("conv_rows_loaded")
        cv_out = sem("conv_rows_stored")
        y_out = [sem(f"y_stored{n}") for n in range(2)]
        x_done = sem("residual_tile_done")

        def levels(lists):
            return [n for names in lists for n in names]

        VS = dict(
            init=["masks", "fill", "vec", "cw", "lb1", "lb2", "lb3", "lb4", "lb5", "lb6"],
            x=["copy"], xs=["copy"],
            norm=[f"{n}{k}" for k in range(KT) for n in ("hi", "lo")],
            ha=["cols", "fneg", "fls", "fb", "cd", "nabs", "cmax", "qneg", "qls", "lf", "gneg", "gls", "Q", "K", "scan",
                "bd", "gate"],
            hr=["qe", "kd", "d1", "adiag", "d2", "kl1", "d4", "kl2", "pred1", "d8", "kl4", "pred2", "d16", "kl8", "pred4",
                "d32", "kl16", "pred8", "S0", "S1", "S2", "S3", "d64", "kl32", "pred16", "vbig", "sdec", "kl64", "pred32",
                "snew", "pred64", "on", "og", "lo"],
            gp=["x", "neg", "ls", "g", "g2", "scan", "dl"],
            ga=["cols", "gsel", "k1", "k2", "k3", "kneg", "dec", "kls", "q1", "q2", "q3", "qneg", "ks", "qls", "kn", "kb",
                "v1", "v2", "v3", "vneg", "qs", "kkd", "vls", "vs", "qn", "nl", "qkd", "zneg", "zls", "tt0", "tt1", "A",
                "qe", "cols2", "nbe", "gate"],
            gr=["pred2", "vb", "pred4", "kdt", "kdts", "sr1", "sr2", "sr3", "pred8", "pred16", "pred32", "pred64",
                "S0", "vbig", "sdec", "r1", "S1", "r2", "S2", "r3", "S3", "sn0", "sn1", "on", "og", "lo"],
            up=["s0"] + levels([(f"s{k}", f"lo{k - 1}") for k in range(1, KT)]) + [f"lo{KT - 1}"],
            y=["y"], ys=["y"],
        )
        SS = dict(
            init=["lb1", "lb2", "lb3"],
            norm=[f"sq{k}" for k in range(KT)] + ["ln", "rstd"], normf=[f"sq{k}" for k in range(KT)] + ["ln", "rstd"],
            ha=["fexp", "fln", "kexp", "cexp", "cln", "qexp", "qln", "qsig", "gexp", "gln", "gsig", "ebd"],
            hr=["e1", "e2", "e4", "vT", "kdT", "e8", "kdTs", "e16", "e32", "os", "e64", "oo", "sq", "ln", "rn", "hi"],
            gp=["A", "exp", "ln", "be", "el", "eg", "cols"],
            ga=["hist", "past", "ktap", "G", "kexp", "kln", "bb", "eG", "qtap", "vhist", "dec", "ksig", "sqk", "qexp", "qln", "lnk",
                "rnk", "vtap", "qsig", "vexp", "vln", "sqq", "vsig", "lnq", "rnq", "zexp", "zln", "cout", "K", "tm0", "zsig"],
            gr=["x2", "tt2", "x4", "tt4", "x8", "tt8", "x16", "tt16", "rs", "x32", "tt32", "vns", "x64", "tt64", "os",
                "vn0", "vn1", "vn2", "vn3", "oo", "sq", "ln", "rn", "hi"],
            up=[f"hi{k}" for k in range(KT)],
            y=["e"], ys=["e"],
        )
        TT = dict(
            init=["vec"], x=["t"], xs=["t"],
            norm=[f"sum{k}" for k in range(KT)], normf=[f"sum{k}" for k in range(KT)],
            hr=["diag", "lv1", "lv2", "vT", "kdT", "lv4", "smp", "lv8", "dS", "lv16", "os", "lv32", "dSs", "lv64", "o", "ss"],
            gp=["cols"],
            ga=["cin", "gb", "bb", "ssk", "kk", "ssq", "qk", "stash", "t0"],
            gr=["x2", "dt2", "tr2", "vT", "x4", "dt4", "tr4", "sks", "x8", "dt8", "tr8", "x16", "dt16", "tr16",
                "srt", "x32", "dt32", "tr32", "svn", "x64", "dt64", "tr64", "os",
                "vn0", "dS0", "ks1", "vn1", "dS1", "ks2", "vn2", "dS2", "ks3", "vn3", "dS3", "o", "dSs0", "dSs1", "ss"],
            y=["t"], ys=["t"],
        )
        dt_ready = sem("dt_bias_ready")
        ones_set = sem("ones_set")
        st = {}

        def stage(kind, key):
            if key not in st:
                st[key] = tuple(Steps(sem(f"{e}_{key}"), d[kind]) if kind in d else None
                                for e, d in (("vector", VS), ("scalar", SS), ("tensor", TT)))
            return st[key]

        for kind, key in [("init", "init"), ("x", "x"), ("xs", "xs"), ("norm", "n0"), ("norm", "n1"), ("norm", "n2"),
                          ("norm", "n3"), ("normf", "n4"), ("ha", "ha"), ("hr", "hr"), ("gp", "gp"), ("ga", "ga"),
                          ("gr", "gr"), ("up", "up0"),
                          ("up", "up1"), ("y", "y"), ("ys", "ys")]:
            stage(kind, key)

        def halves(ap):
            return ap.rearrange("p (a n) -> p a n", a=2)

        def first_half(ap, m):
            return ap.rearrange("p (n two m) -> p n two m", two=2, m=m)[:, :, 0, :]

        def second_half(ap, m):
            return ap.rearrange("p (n two m) -> p n two m", two=2, m=m)[:, :, 1, :]

        def blocks(ap, m):
            return ap.rearrange("p (n m) -> p n m", m=m)

        def width(m):
            return T if m in SLEVELS else TP

        def psum_out(slot):
            return pj[:, slot, :, 0:HALF]

        U_HIN = 0
        U_HOUT = U_HIN + 4 * H
        U_MLP0 = U_HOUT + KT
        U_AB = U_MLP0 + 2 * KT * NGRP
        U_GIN = U_AB + 1
        U_GOUT = U_GIN + 4 * H
        U_MLP1 = U_GOUT + KT
        U_END = U_MLP1 + 2 * KT * NGRP

        def unit_done(u):
            return u + 3

        block = ctx.enter_context(nc.Block())

        @block.sync
        def _(sp):
            c = 16
            sp.dma_start(cf[:], const_f).then_inc(c_in, c)
            for stage_, part in zip(cstage, (const_u[:, 0:CU_HALF], const_u[:, CU_HALF:2 * CU_HALF])):
                sp.dma_start(stage_, part).then_inc(c_in, c)
            rows = xp[:, 0, :]
            for src, r, n in ((norm_mix, V_MIX, 16), (norm_mlp, V_MLP, 16)):
                sp.dma_start(rows[r:r + n, 0:P], src.rearrange("d (k p) -> (d k) p", p=P)).then_inc(c_in, c)
            sp.dma_start(rows[V_FIN:V_FIN + 8, 0:P], norm_final.rearrange("(k p) -> k p", p=P)).then_inc(c_in, c)
            sp.dma_start(rows[V_LB:V_LB + 8, 0:P], hgrn_lb.rearrange("d (k p) -> (d k) p", p=P)).then_inc(c_in, c)
            sp.dma_start(rows[V_HON:V_HON + 1, 0:P], hgrn_out_norm).then_inc(c_in, c)
            sp.dma_start(rows[V_GON:V_GON + 1, 0:P], gdn_out_norm).then_inc(c_in, c)
            sp.dma_start(xp[0:CONV * 3 * H, 1, 0:P],
                         gdn_conv_w[0].rearrange("j (s p) -> (j s) p", p=P)).then_inc(c_in, c)
            sp.dma_start(gsc[:, 0:1], gdn_A_log.rearrange("a h -> h a")).then_inc(c_in, c)
            sp.dma_start(gsc[:, 1:2], gdn_dt_bias.rearrange("a h -> h a")).then_inc(c_in, c)

            xs = stage("x", "x")[2]
            for n in range(NC):
                if n >= 2:
                    sp.wait_ge(xs.sem, n - 1)
                sp.dma_start(xrow[n % 2], x_prompt[0, n * P:(n + 1) * P, :]).then_inc(x_in[n % 2], 16)
            sp.wait_ge(xs.sem, NC - 1)
            sp.dma_start(xrow[0][0:TS], x_sample.rearrange("b t d -> (b t) d")).then_inc(x_in[0], 16)

            def load(U, r, j, src):
                slot = (U + j) % RAW
                if not isinstance(r, int) or r + U + j >= RAW:
                    free = fixed(sp, r * 2 + (2 * (U + j) - 6))
                    sp.wait_ge(x_in[0], 16)
                    sp.wait_ge(w_split, free)
                sp.dma_start(w_raw[:, slot], src).then_inc(w_in[slot], 16)

            hin = hgrn_w_in[0].rearrange("(k p) n -> p k n", p=P)
            gin = gdn_w_in[0].rearrange("(k p) n -> p k n", p=P)
            for j in range(4):
                load(U_HIN, 0, j, hin[:, :, HGRN_ORDER[j] * D:HGRN_ORDER[j] * D + P])
            with sp.Fori(1, H) as h:
                for j in range(4):
                    load(U_HIN, h * 4, j, hin[:, :, ds(h * P + HGRN_ORDER[j] * D, P)])

            def out_proj(U, w):
                view = w[0].rearrange("(k p) n -> p k n", p=P)
                with sp.Fori(0, 2) as i:
                    for j in range(4):
                        load(U, i * 4, j, view[:, :, ds(i * (4 * P) + j * P, P)])

            def mlp(layer, U):
                up = mlp_w_up[layer].rearrange("(k p) n -> p k n", p=P)
                down = mlp_w_down[layer].rearrange("(g k p) n -> p g k n", p=P, k=KT)
                with sp.Fori(0, NGRP) as g:
                    for j in range(KT):
                        load(U, g * (2 * KT), j, up[:, :, ds(g * D + j * P, P)])
                    for j in range(KT):
                        load(U, g * (2 * KT), KT + j,
                             down[:, ds(g, 1), :, j * P:(j + 1) * P].rearrange("p o k n -> p (o k) n"))

            out_proj(U_HOUT, hgrn_w_out)
            mlp(0, U_MLP0)
            slot = U_AB % RAW
            sp.wait_ge(w_split, 2 * U_AB - 6)
            with nc.allow_non_contiguous_dma(reason="16 columns"):
                for n in range(2):
                    sp.dma_start(w_raw[:, slot, :, 32 * n:32 * n + H],
                                 gin[:, :, 4 * D + n * H:4 * D + (n + 1) * H]).then_inc(w_in[slot], 16)
            with sp.Fori(0, H) as h:
                for j in range(4):
                    load(U_GIN, h * 4, j, gin[:, :, ds(h * P + GDN_ORDER[j] * D, P)])
            out_proj(U_GOUT, gdn_w_out)
            mlp(1, U_MLP1)

        @block.gpsimd
        def _(pool):
            nc.gpsimd.memset(ones[:], 1.0).then_inc(ones_set, 1)

            def split(n, j, extra=0):
                u, s = n * 4 + j, j % SPLIT
                loaded, free = fixed(pool, n * 16 + (16 + extra)), fixed(pool, u - 1)
                pool.wait_ge(ones_set, 1)
                pool.wait_ge(w_in[j], loaded)
                if not (isinstance(n, int) and u < SPLIT):
                    pool.wait_ge(w_used, free)
                nc.gpsimd.tensor_scalar(w_hi[:, s], w_raw[:, j], 1.0, 1.0, ALU.mult, ALU.mult).then_inc(w_split, 1)
                pool.wait_ge(w_split, u * 2 + 1)
                nc.gpsimd.tensor_tensor(w_lo[:, s], w_raw[:, j], w_hi[:, s], ALU.subtract).then_inc(w_split, 1)

            for j in range(RAW):
                split(0, j)
            with pool.Fori(1, U_AB // 4) as n:
                for j in range(RAW):
                    split(n, j)
            ab = U_AB % RAW
            with pool.Fori(U_AB // 4, U_END // 4) as n:
                for j in range(RAW):
                    split(n, j, 16 if j == ab else 0)
            for j in range(U_END % 4):
                split(U_END // 4, j, 16 if j == ab else 0)

        @block.tensor
        def _(pe):
            mm = nc.tensor.matmul

            def tiles(U, r, j, hi, lo, k0, k1, k_ready=None):
                u, s = r + (U + j), (U + j) % SPLIT
                if k0 == 0:
                    pe.wait_ge(w_split, u * 2 + 2)
                    pe.wait_ge(unit_out, u + 1)
                for k in range(k0, k1):
                    if k_ready:
                        k_ready(k)
                    for a, (w, v) in enumerate(((w_hi, hi), (w_hi, lo), (w_lo, hi))):
                        for b in range(2):
                            last = mm(pj[:, s, b, 0:HALF], w[:, s, k, :], v[:, k, b * HALF:(b + 1) * HALF],
                                      start=(k == 0 and a == 0), stop=(k == KT - 1 and a == 2))
                if k1 == KT:
                    last.then_inc(w_used, 1)

            def unit(U, r, j, hi, lo, k_ready=None):
                tiles(U, r, j, hi, lo, 0, KT, k_ready)

            def head_projections(U, h):
                done = [0]

                def more(n):
                    for i in range(done[0], min(done[0] + n, 4 * KT)):
                        tiles(U, h * 4, i // KT, xh, xl, i % KT, i % KT + 1)
                    done[0] += n
                return more

            def sum_features(bank, src, start=True, stop=True):
                for b in range(2):
                    last = mm(rr[:, bank + b, 0:HALF], ones[:], src[:, b * HALF:(b + 1) * HALF], start=start, stop=stop)
                return last

            def norm(key):
                _, s, t = st[key]
                for k in range(KT):
                    pe.wait_ge(s.sem, s.after(f"sq{k}", 0))
                    t.did(sum_features(0, sq[:, k % 2], k == 0, k == KT - 1), f"sum{k}")

            def tr(out, in_):
                n = in_.shape[0]
                return nc.tensor.transpose(out, in_, cf[0:n, C_EYE:C_EYE + n])

            v, s, t = st["init"]
            pe.wait_ge(c_in, 16 * N_CONST)
            pe.wait_ge(ones_set, 1)
            pe.wait_ge(v.sem, v.after("fill", 0))
            tr(rr[:, 0, 0:V_N], xp[0:V_N, 0, 0:P])
            t.did(tr(rr[:, 1, 0:CONV * 3 * H], xp[0:CONV * 3 * H, 1, 0:P]), "vec")

            v, s, t = st["x"]
            for i in range(NC):
                pe.wait_ge(x_in[i % 2], 16 * (i // 2 + 1))
                if i:
                    pe.wait_ge(v.sem, v.after("copy", i - 1))
                for k in range(KT):
                    last = tr(rr[:, 2 + k // 4, (k % 4) * P:(k % 4 + 1) * P], xrow[i % 2][:, k * P:(k + 1) * P])
                t.did(last, "t")
            pe.wait_ge(x_in[0], 16 * (NC // 2 + 1))
            pe.wait_ge(v.sem, v.after("copy", NC - 1))
            for k in range(KT):
                last = tr(rr[:, 2, k * TS:(k + 1) * TS], xrow[0][0:TS, k * P:(k + 1) * P])
            st["xs"][2].did(last, "t")

            def wait_norm(key):
                v = st[key][0]
                return lambda k: pe.wait_ge(v.sem, v.after(f"lo{k}", 0))

            def hgrn_rec(h, more):
                (v, s, t), va = st["hr"], st["ha"][0]
                Q, K, val, qe, kd, A, KL, vT, kdT = (hg[n] for n in ("Q", "K", "val", "qe", "kd", "A", "KL", "vT", "kdT"))

                def level(n, tiles):
                    m = LEVELS[n]
                    more(tiles)
                    pe.wait_ge(v.sem, v.after(f"kl{m}", h))
                    if n >= 2:
                        pe.wait_ge(v.sem, v.after(f"pred{LEVELS[n - 2]}", h))
                    for c in range(NC):
                        last = mm(rr[:, n % 2, c * 64:(c + 1) * 64], KL[:, n % 2, c * P:(c + 1) * P],
                                  QL[:, n % 2, c * 64:(c + 1) * 64], start=True, stop=True)
                    if m in SLEVELS:
                        last = mm(rr[0:TS, n % 2, TP // 2:T // 2], KL[:, n % 2, TP:T], QL[:, n % 2, TP // 2:T // 2],
                                  start=True, stop=True)
                    t.did(last, f"lv{m}")

                pe.wait_ge(va.sem, va.after("K", h))
                pe.wait_ge(st["ha"][1].sem, st["ha"][1].after("ebd", h))
                for c in range(NC):
                    cols = slice(c * P, (c + 1) * P)
                    mm(rr[:, 2, cols], K[:, cols], Q[:, cols], start=True, stop=True)
                t.did(mm(rr[0:TS, 3, 0:TS], K[:, TP:T], Q[:, TP:T], start=True, stop=True), "diag")
                level(0, 6)
                level(1, 3)
                pe.wait_ge(v.sem, v.after("adiag", h))
                for c in range(NC):
                    last = tr(rr[:, 2, c * P:(c + 1) * P], val[:, c * P:(c + 1) * P])
                t.did(last, "vT")
                for c in range(NC):
                    last = tr(rr[:, 3, c * P:(c + 1) * P], kd[:, c * P:(c + 1) * P])
                t.did(last, "kdT")
                level(2, 3)
                taken = fixed(pe, s.after("vT", h))
                pe.wait_ge(c_in, 16 * N_CONST)
                pe.wait_ge(s.sem, taken)
                tr(rr[0:TS, 2, 0:P], val[:, TP:T])
                t.did(tr(rr[0:TS, 2, P:2 * P], kd[:, TP:T]), "smp")
                level(3, 3)
                pe.wait_ge(s.sem, s.after("kdTs", h))
                for c in range(NC):
                    last = mm(rr[:, 2, c * P:(c + 1) * P], kdT[:, c * P:(c + 1) * P], vT[:, c * P:(c + 1) * P],
                              start=True, stop=True)
                t.did(last, "dS")
                level(4, 3)
                pe.wait_ge(st_in, h * 16 + 16)
                mm(rr[:, 3, 0:TS], vTs[:], A[0:TS, TP:T], start=True, stop=False)
                for b in range(NSEQ):
                    last = mm(rr[:, 3, b * SLEN:(b + 1) * SLEN], S0[:, b, :],
                              qe[:, TP + b * SLEN:TP + (b + 1) * SLEN], start=False, stop=(b == NSEQ - 1))
                t.did(last, "os")
                level(5, 3)
                pe.wait_ge(v.sem, v.after("vbig", h))
                pe.wait_ge(s.sem, s.after("os", h))
                for a in range(2):
                    last = mm(rr[:, 2 + a, :], kdTs[:], hg["vbig"][0:TS, a, 0:4 * P], start=True, stop=True)
                t.did(last, "dSs")
                level(6, 3)
                more(4)
                pe.wait_ge(v.sem, v.after("pred64", h))
                for c in range(NC):
                    cols = slice(c * P, (c + 1) * P)
                    last = mm(rr[:, 1, cols], vT[:, cols], A[:, cols], start=True, stop=(c == 0))
                    if c:
                        last = mm(rr[:, 1, cols], Sp[:, c - 1, :], qe[:, cols], start=False, stop=True)
                t.did(last, "o")
                more(4)
                pe.wait_ge(s.sem, s.after("sq", h))
                t.did(sum_features(2, hg["sq"]), "ss")

            def gdn_pre():
                v, s, t = st["gp"]
                pe.wait_ge(v.sem, v.after("dl", 0))
                pe.wait_ge(s.sem, s.after("eg", 0))
                for c in range(NC):
                    tr(rr[:, 2, c * P:(c + 1) * P], gt4[:, c * P:(c + 1) * P])
                t.did(tr(rr[0:TS, 3, 0:P], gt4[:, TP:T]), "cols")

            def held(*waits):
                values = [(steps.sem, fixed(pe, steps.after(name, h))) for steps, name, h in waits]
                pe.wait_ge(c_in, 16 * N_CONST)
                for sem_, value in values:
                    pe.wait_ge(sem_, value)

            def gdn_prepare(slot, h):
                v, s, t = st["ga"]
                nQ, nK, work = gd["nQ"], gd["nK"], gd["work"]
                if slot == "L1":
                    loaded = fixed(pe, h * 16 + 16)
                    pe.wait_ge(c_in, 16 * N_CONST)
                    pe.wait_ge(cv_in, loaded)
                    for g in range(3):
                        last = tr(rr[:, 3, SVN + g * 32:SVN + g * 32 + XW * NSEQ], cin[:, g, :])
                    t.did(last, "cin")
                if slot in ("L3", "L4"):
                    g, name = (0, "gb") if slot == "L3" else (1, "bb")
                    pe.wait_ge(s.sem, s.after("G" if g else "hist", h))
                    pe.wait_ge(v.sem, v.after("gsel", h))
                    for b in range(2):
                        last = mm(rr[:, 2 + b, 0:HALF], cf[:, C_IND + g * P:C_IND + (g + 1) * P],
                                  work[:, b * HALF:(b + 1) * HALF], start=True, stop=True)
                    t.did(last, name)
                if slot == "L6":
                    pe.wait_ge(s.sem, s.after("sqk", h))
                    t.did(sum_features(2, work), "ssk")
                if slot == "C0":
                    pe.wait_ge(v.sem, v.after("kb", h))
                    for c in range(NC):
                        cols = slice(c * P, (c + 1) * P)
                        mm(rr[:, 2 + c // 2, c % 2 * P:(c % 2 + 1) * P], nK[:, cols], work[:, cols], start=True, stop=True)
                    t.did(mm(rr[0:TS, 2, 2 * P:2 * P + TS], nK[:, TP:T], work[:, TP:T], start=True, stop=True), "kk")
                if slot == "C1":
                    pe.wait_ge(s.sem, s.after("sqq", h))
                    pe.wait_ge(v.sem, v.after("kkd", h))
                    t.did(sum_features(2, gd["G"]), "ssq")
                if slot == "C2":
                    pe.wait_ge(v.sem, v.after("qn", h))
                    for c in range(NC):
                        cols = slice(c * P, (c + 1) * P)
                        mm(rr[:, 2 + c // 2, c % 2 * P:(c % 2 + 1) * P], nK[:, cols], nQ[:, cols], start=True, stop=True)
                    t.did(mm(rr[0:TS, 3, 2 * P:2 * P + TS], nK[:, TP:T], nQ[:, TP:T], start=True, stop=True), "qk")
                if slot == "C3":
                    held((v, "qkd", h))
                    for g in range(3):
                        n = XW * (NSEQ + 1)
                        last = tr(rr[0:n, 2 + g // 2, g % 2 * P:(g % 2 + 1) * P], cstash[:, g, :])
                    t.did(last, "stash")

            def gdn_first_inverse(h, *bank_left):
                v, s, t = st["ga"]
                Tt = gd["Tt"]
                pe.wait_ge(v.sem, v.after("tt1", h))
                for c in range(NC):
                    cols = slice(c * P, (c + 1) * P)
                    tr(rr[:, 1, cols], Tt[:, cols])
                held((v, "tt1", h), *bank_left)
                t.did(tr(rr[0:TS, 2, 0:TS], Tt[0:TS, TP:T]), "t0")

            def gdn_rec(h, nxt, more):
                (v, s, t), (va, sa, ta) = st["gr"], st["ga"]
                K, qe, A, NL, Tm, Tt, X, kdT, vT, VN = (gd[n] for n in ("K", "qe", "A", "NL", "Tm", "Tt", "X", "kdT",
                                                                        "vT", "VN"))

                for n, m in enumerate(LEVELS[1:]):
                    smp = m in SLEVELS
                    more(6 if n == 0 else 1)
                    if n == 0:
                        pe.wait_ge(sa.sem, sa.after("tm0", h))
                        pe.wait_ge(va.sem, va.after("qe", h))
                    else:
                        pe.wait_ge(s.sem, s.after(f"tt{LEVELS[n]}", h))
                    for c in range(NC):
                        cols = slice(c * P, (c + 1) * P)
                        last = mm(rr[:, 0, c * 64:(c + 1) * 64], NL[:, cols], first_half(Tm[:, cols], m),
                                  start=True, stop=True)
                    if smp:
                        last = mm(rr[0:TS, 1, 0:TS // 2], NL[0:TS, TP:T], first_half(Tm[0:TS, TP:T], m),
                                  start=True, stop=True)
                    t.did(last, f"x{m}")
                    more(2)
                    pe.wait_ge(s.sem, s.after(f"x{m}", h))
                    for c in range(NC):
                        last = mm(rr[:, 0, 256 + c * 64:256 + (c + 1) * 64], Tt[:, c * P:(c + 1) * P],
                                  X[:, c * 64:(c + 1) * 64], start=True, stop=True)
                    if smp:
                        last = mm(rr[0:TS, 1, TS // 2:TS], Tt[0:TS, TP:T], X[0:TS, TP // 2:T // 2],
                                  start=True, stop=True)
                    t.did(last, f"dt{m}")
                    more(2)
                    pe.wait_ge(v.sem, v.after(f"pred{m}", h))
                    for c in range(NC):
                        cols = slice(c * P, (c + 1) * P)
                        last = tr(rr[:, 1, cols], Tm[:, cols])
                    if smp:
                        last = tr(rr[0:TS, 0, 0:TS], Tm[0:TS, TP:T])
                    t.did(last, f"tr{m}")
                    if m == 2:
                        pe.wait_ge(va.sem, va.after("gate", h))
                        for c in range(NC):
                            last = tr(rr[:, 2 + c // 2, c % 2 * P:(c % 2 + 1) * P], gd["nV"][:, c * P:(c + 1) * P])
                        t.did(last, "vT")
                    if m == 4:
                        pe.wait_ge(v.sem, v.after("vb", h))
                        if nxt is not None:
                            pe.wait_ge(sa.sem, sa.after("hist", nxt))
                        for c in range(NC):
                            tr(rr[:, 2 + c // 2, c % 2 * P:(c % 2 + 1) * P], K[:, c * P:(c + 1) * P])
                        tr(rr[0:TS, 2, SRT:SRT + P], K[:, TP:T])
                        pe.wait_ge(st_in, h * 16 + 16 * (H + 1))
                        for b in range(NSEQ):
                            last = mm(rr[:, 2, SKS + b * SLEN:SKS + (b + 1) * SLEN], S0[:, b, :],
                                      K[:, TP + b * SLEN:TP + (b + 1) * SLEN], start=True, stop=True)
                        t.did(last, "sks")
                    if m == 8:
                        pe.wait_ge(v.sem, v.after("sr1", h))
                    if m == 16:
                        held((v, "sr3", h), *([] if nxt is None else [(sa, "G", nxt)]))
                        t.did(tr(rr[0:TS, 2, SRT:SRT + P], rt[:]), "srt")
                    if m == 32:
                        held((s, "rs", h), *([] if nxt is None else [(sa, "bb", nxt)]))
                        t.did(mm(rr[0:TS, 3, SVN:SVN + P], Tt[0:TS, TP:T], X[0:TS, RS:RS + P], start=True, stop=True), "svn")
                    if m == 64:
                        pe.wait_ge(s.sem, s.after("vns", h))
                        mm(rr[:, 2, OS:OS + TS], X[0:TS, VNS:VNS + P], A[0:TS, TP:T], start=True, stop=False)
                        for b in range(NSEQ):
                            last = mm(rr[:, 2, OS + b * SLEN:OS + (b + 1) * SLEN], S0[:, b, :],
                                      qe[:, TP + b * SLEN:TP + (b + 1) * SLEN], start=False, stop=(b == NSEQ - 1))
                        t.did(last, "os")
                    if nxt is not None:
                        if m == 2:
                            pe.wait_ge(v.sem, v.after("vb", h))
                        gdn_prepare(f"L{n + 1}", nxt)
                pe.wait_ge(s.sem, s.after("tt64", h))
                for c in range(NC):
                    cols = slice(c * P, (c + 1) * P)
                    if c:
                        pe.wait_ge(v.sem, v.after(f"S{c - 1}", h))
                        t.did(mm(rr[:, 0, 0:P], K[:, cols], Sp[:, c - 1, :], start=True, stop=True), f"ks{c}")
                        pe.wait_ge(v.sem, v.after(f"r{c}", h))
                    t.did(mm(rr[:, 0, P:2 * P], Tt[:, cols], vT[:, cols], start=True, stop=True), f"vn{c}")
                    pe.wait_ge(s.sem, s.after(f"vn{c}", h))
                    t.did(mm(rr[:, 0, 2 * P:3 * P], kdT[:, cols], VN[:, cols], start=True, stop=True), f"dS{c}")
                    last = mm(rr[:, 1, cols], VN[:, cols], A[:, cols], start=True, stop=(c == 0))
                    if c:
                        last = mm(rr[:, 1, cols], Sp[:, c - 1, :], qe[:, cols], start=False, stop=True)
                    if c == NC - 1:
                        t.did(last, "o")
                    if nxt is not None:
                        if c == 0:
                            pe.wait_ge(s.sem, s.after("os", h))
                        gdn_prepare(f"C{c}", nxt)
                pe.wait_ge(v.sem, v.after("S3", h))
                t.did(mm(rr[:, 0, :], kdTs[:], gd_vbig[0], start=True, stop=True), "dSs0")
                if nxt is not None:
                    pe.wait_ge(s.sem, s.after("oo", h))
                    gdn_first_inverse(nxt, (sa, "cout", nxt))
                pe.wait_ge(v.sem, v.after("sn0", h))
                t.did(mm(rr[:, 0, :], kdTs[:], gd_vbig[1], start=True, stop=True), "dSs1")
                pe.wait_ge(s.sem, s.after("sq", h))
                if nxt is not None:
                    pe.wait_ge(sa.sem, sa.after("tm0", nxt))
                t.did(sum_features(2, gd["sq"]), "ss")
            def out_proj(U, key):
                v = st[key][0]
                with pe.Fori(0, 2) as i:
                    for j in range(4):
                        pe.wait_ge(v.sem, v.after("lo", H - 1))
                        unit(U, i * 4, j, oh, ol)

            def mlp(U, nkey, ukey):
                v = st[ukey][0]
                with pe.Fori(0, NGRP) as g:
                    for j in range(KT):
                        unit(U, g * (2 * KT), j, xh, xl, wait_norm(nkey) if j == 0 else None)
                    for j in range(KT):
                        unit(U, g * (2 * KT), KT + j, oh, ol,
                             (lambda k: pe.wait_ge(v.sem, v.after(f"lo{k}", g))) if j == 0 else None)

            norm("n0")
            unit(U_HIN, 0, 0, xh, xl, wait_norm("n0"))
            for j in range(1, 4):
                unit(U_HIN, 0, j, xh, xl)
            with pe.Fori(0, H - 1) as h:
                hgrn_rec(h, head_projections(U_HIN, h + 1))
            hgrn_rec(H - 1, lambda n: None)
            out_proj(U_HOUT, "hr")
            norm("n1")
            mlp(U_MLP0, "n1", "up0")
            norm("n2")
            unit(U_AB, 0, 0, xh, xl, wait_norm("n2"))
            gdn_pre()
            more = head_projections(U_GIN, 0)
            pe.wait_ge(st["gp"][1].sem, st["gp"][1].after("cols", 0))
            for slot in GDN_SLOTS:
                more(11 if slot == "L1" else 5)
                gdn_prepare(slot, 0)
            gdn_first_inverse(0, (st["ga"][1], "cout", 0))
            with pe.Fori(0, H - 1) as h:
                gdn_rec(h, h + 1, head_projections(U_GIN, h + 1))
            gdn_rec(H - 1, None, lambda n: None)
            out_proj(U_GOUT, "gr")
            norm("n3")
            mlp(U_MLP1, "n3", "up1")
            norm("n4")
            v, s, t = st["y"]
            for i in range(NC):
                pe.wait_ge(v.sem, v.after("y", i))
                if i:
                    pe.wait_ge(s.sem, s.after("e", i - 1))
                for k in range(KT):
                    last = tr(rr[:, 2 + k // 4, (k % 4) * P:(k % 4 + 1) * P], ycol[i % 2][:, k * P:(k + 1) * P])
                t.did(last, "t")
            v2, s2, t2 = st["ys"]
            pe.wait_ge(v2.sem, v2.after("y", 0))
            pe.wait_ge(s.sem, s.after("e", NC - 1))
            for k in range(KT):
                last = tr(rr[0:TS, 2 + k // 4, (k % 4) * P:(k % 4 + 1) * P], ycol[NC % 2][:, k * P:k * P + TS])
            t2.did(last, "t")

        @block.scalar
        def _(act):
            f = nc.scalar.activation
            nc.scalar.preload_act_table_set("natural_log_exp_and_others")
            sem_of = lambda steps, name, i: act.wait_ge(steps.sem, steps.after(name, i))

            v, s, t = st["init"]
            sem_of(v, "lb1", 0)
            s.did(f(lbt[:, 3], lbt[:, 3], ACT.Exp), "lb1")
            sem_of(v, "lb5", 0)
            s.did(f(lbt[:, 1], lbt[:, 1], ACT.Ln, scale=LN_SHIFT), "lb2")
            s.did(f(lbt[:, 2], lbt[:, 0], ACT.Ln), "lb3")

            def norm(key, u_before):
                _, s, t = st[key]
                if u_before is None:
                    act.wait_ge(st["xs"][0].sem, 1)
                else:
                    act.wait_ge(unit_out, unit_done(u_before))
                for k in range(KT):
                    if k >= 2:
                        sem_of(t, f"sum{k - 2}", 0)
                    s.did(f(sq[:, k % 2], xT[:, k], ACT.Square), f"sq{k}")
                sem_of(t, f"sum{KT - 1}", 0)
                s.did(f(halves(rstd[:]), rr[:, 0:2, 0:HALF], ACT.Ln, bias=epsc[:, 0:1], scale=1.0 / D), "ln")
                sem_of(s, "ln", 0)
                s.did(f(rstd[:], rstd[:], ACT.Exp, scale=-0.5), "rstd")

            def load_state(src, h):
                act.dma_start(S0[:], src[0, :, ds(h, 1)].rearrange("b o k v -> k (o b) v")).then_inc(st_in, 16)

            def store_states(dst_p, dst_s, h):
                act.dma_start(dst_p[0, 0, ds(h, 1)].rearrange("o k v -> k (o v)"), Sp[:, NC - 1]).then_inc(st_out, 16)
                act.dma_start(dst_s[0, :, ds(h, 1)].rearrange("b o k v -> k (o b) v"), S0[:]).then_inc(st_out, 16)

            def hgrn_prepare(slot, h):
                v, s, t = st["ha"]
                T1 = xp[:, 0, XW:XW + T]
                if slot == 3:
                    sem_of(v, "fneg", h)
                    s.did(f(ng[:, 1, 0:T], ng[:, 1, 0:T], ACT.Exp), "fexp")
                    sem_of(s, "fexp", h)
                    s.did(f(ng[:, 1, 0:T], ng[:, 1, 0:T], ACT.Ln, bias=1.0), "fln")
                if slot == 4:
                    sem_of(v, "nabs", h)
                    s.did(f(pr[:, 1, 0:T], pr[:, 1, 0:T], ACT.Exp), "kexp")
                    s.did(f(T1, T1, ACT.Exp), "cexp")
                    sem_of(s, "cexp", h)
                    s.did(f(T1, T1, ACT.Ln, bias=1.0), "cln")
                if slot == 5:
                    sem_of(v, "qneg", h)
                    s.did(f(ng[:, 0, 0:T], ng[:, 0, 0:T], ACT.Exp), "qexp")
                    sem_of(s, "qexp", h)
                    s.did(f(ng[:, 0, 0:T], ng[:, 0, 0:T], ACT.Ln, bias=1.0), "qln")
                if slot == 6:
                    sem_of(v, "qls", h)
                    s.did(f(ng[:, 0, 0:T], ng[:, 0, 0:T], ACT.Exp), "qsig")
                if slot == 7:
                    sem_of(v, "gneg", h)
                    s.did(f(ng[:, 2, 0:T], ng[:, 2, 0:T], ACT.Exp), "gexp")
                    sem_of(s, "gexp", h)
                    s.did(f(ng[:, 2, 0:T], ng[:, 2, 0:T], ACT.Ln, bias=1.0), "gln")
                if slot == 8:
                    sem_of(v, "gls", h)
                    s.did(f(ng[:, 2, 0:T], ng[:, 2, 0:T], ACT.Exp), "gsig")
                if slot == 9:
                    sem_of(v, "bd", h)
                    f(hg["eb"], hg["b"], ACT.Exp)
                    s.did(f(hg["bd"], hg["bd"], ACT.Exp), "ebd")

            def hgrn_head(h, nxt):
                v, s, t = st["hr"]
                dd, oo, vT, kdT, sqr = hg["dd"], hg["oo"], hg["vT"], hg["kdT"], hg["sq"]
                for n, m in enumerate(LEVELS):
                    sem_of(v, f"d{m}", h)
                    s.did(f(dd[:, n % 2, 0:width(m)], dd[:, n % 2, 0:width(m)], ACT.Exp), f"e{m}")
                    if m == 4:
                        sem_of(t, "vT", h)
                        s.did(f(vT[:, 0:TP], rr[:, 2, :], ACT.Copy), "vT")
                        sem_of(t, "kdT", h)
                        s.did(f(kdT[:, 0:TP], rr[:, 3, :], ACT.Copy), "kdT")
                    if m == 8:
                        sem_of(t, "smp", h)
                        f(vTs[:], rr[0:TS, 2, 0:P], ACT.Copy)
                        s.did(f(kdTs[:], rr[0:TS, 2, P:2 * P], ACT.Copy), "kdTs")
                    if m == 32:
                        sem_of(t, "os", h)
                        s.did(f(oo[:, TP:T], rr[:, 3, 0:TS], ACT.Copy), "os")
                    if nxt is not None:
                        hgrn_prepare(n, nxt)
                if nxt is not None:
                    hgrn_prepare(7, nxt)
                sem_of(t, "o", h)
                s.did(f(oo[:, 0:TP], rr[:, 1, :], ACT.Copy), "oo")
                sem_of(s, "oo", h)
                s.did(f(sqr, oo, ACT.Square), "sq")
                sem_of(v, "snew", h)
                store_states(hgrn_p, hgrn_s, h)
                if nxt is not None:
                    hgrn_prepare(8, nxt)
                sem_of(t, "ss", h)
                s.did(f(halves(sqr), rr[:, 2:4, 0:HALF], ACT.Ln, bias=epsc[:, 0:1], scale=1.0 / P), "ln")
                sem_of(s, "ln", h)
                s.did(f(sqr, sqr, ACT.Exp, scale=-0.5), "rn")
                if nxt is not None:
                    hgrn_prepare(9, nxt)
                sem_of(v, "og", h)
                s.did(f(oh[:, ds(h, 1)].rearrange("p o n -> p (o n)"), oo, ACT.Copy), "hi")
                if nxt is not None:
                    act.wait_ge(st_out, h * 32 + 32)
                    load_state(state_hgrn, nxt)

            def gdn_pre():
                v, s, t = st["gp"]
                act.wait_ge(c_in, 16 * N_CONST)
                s.did(f(gsc[0:H, 2:3], gsc[0:H, 0:1], ACT.Exp), "A")
                sem_of(v, "neg", 0)
                s.did(f(B[0:64, 1], B[0:64, 1], ACT.Exp), "exp")
                sem_of(s, "exp", 0)
                s.did(f(B[0:64, 1], B[0:64, 1], ACT.Ln, bias=1.0), "ln")
                sem_of(v, "ls", 0)
                s.did(f(gt4[32:64], B[32:64, 2], ACT.Exp), "be")
                sem_of(v, "dl", 0)
                s.did(f(gt4[64:64 + H], B[0:H, 3], ACT.Exp), "el")
                s.did(f(gt4[96:96 + H], gt4[0:H], ACT.Exp), "eg")
                sem_of(t, "cols", 0)
                f(gcol[:, 0:NC].rearrange("p c (r x) -> p (c r) x", x=H), blocks(rr[:, 2, :], 32)[:, :, 0:H], ACT.Copy)
                s.did(f(blocks(gcol[0:TS, NC], H), blocks(rr[0:TS, 3, 0:P], 32)[:, :, 0:H], ACT.Copy), "cols")

            def sample_rows(slot):
                return blocks(xp[:, slot, SB0:XPW], SROW)

            def put_history(slot, g):
                return f(sample_rows(slot)[:, :, 0:XW], blocks(hist[:, g, :], XW), ACT.Copy)

            def first_tap(name, slot, g, h, past="past"):
                v, s, t = st["ga"]
                sem_of(s, past, h)
                act.wait_ge(unit_out, (h * 4 + (U_GIN + GDN_ORDER.index(g))) + 3)
                f(cstash[:, g, 0:XW], xp[:, slot, TP:TP + XW], ACT.Copy)
                f(blocks(cstash[:, g, XW:], XW), sample_rows(slot)[:, :, SLEN:SROW], ACT.Copy)
                s.did(f(pr[:, slot, 0:YW], xp[:, slot, 0:YW], ACT.Copy, scale=hcw[:, 0, g:g + 1]), name)

            def soft(row, w, exp, ln):
                s = st["ga"][1]
                s.did(f(ng[:, row, 0:w], ng[:, row, 0:w], ACT.Exp), exp[0])
                sem_of(s, *exp)
                s.did(f(ng[:, row, 0:w], ng[:, row, 0:w], ACT.Ln, bias=1.0), ln)

            def norm_scale(row, ln, rn, h):
                s = st["ga"][1]
                s.did(f(halves(row), rr[:, 2:4, 0:HALF], ACT.Ln, bias=epsc[:, 0:1]), ln)
                sem_of(s, ln, h)
                s.did(f(row, row, ACT.Exp, scale=-0.5), rn)

            def gdn_prepare(slot, h):
                v, s, t = st["ga"]
                work, G, dec = gd["work"], gd["G"], gd["dec"]
                if slot == "L1":
                    sem_of(t, "cin", h)
                    last = f(hist[:], rr[:, 3, SVN:SVN + 96].rearrange("p (g x) -> p g x", g=3)[:, :, 0:XW * NSEQ], ACT.Copy)
                    s.did(last, "hist")
                    if not (isinstance(h, int) and h == H - 1):
                        load_conv(h + 1)
                    sem_of(s, "hist", h)
                    for slot_, g in enumerate(GDN_ORDER[0:2]):
                        last = put_history(slot_, g)
                    s.did(last, "past")
                if slot == "L3":
                    sem_of(v, "cols", h)
                    first_tap("ktap", 0, K_ROW, h)
                    sem_of(t, "gb", h)
                    s.did(f(halves(G), rr[:, 2:4, 0:HALF], ACT.Copy), "G")
                if slot == "L4":
                    sem_of(v, "kneg", h)
                    soft(0, YW, ("kexp", h), "kln")
                    sem_of(t, "bb", h)
                    s.did(f(halves(gd["beta"]), rr[:, 2:4, 0:HALF], ACT.Copy), "bb")
                    sem_of(s, "G", h)
                    s.did(f(gd["eG"], G, ACT.Exp), "eG")
                    first_tap("qtap", 1, Q_ROW, h)
                    s.did(put_history(0, V_ROW), "vhist")
                if slot == "L5":
                    sem_of(v, "dec", h)
                    f(dec[:, 0:TP], dec[:, 0:TP], ACT.Exp)
                    s.did(f(dec[0:TS, TP:T], dec[0:TS, TP:T], ACT.Exp), "dec")
                    sem_of(v, "kls", h)
                    s.did(f(ng[:, 0, 0:YW], ng[:, 0, 0:YW], ACT.Exp), "ksig")
                if slot == "L6":
                    sem_of(v, "ks", h)
                    s.did(f(work, gd["nK"], ACT.Square), "sqk")
                    soft(1, YW, ("qexp", h), "qln")
                    sem_of(t, "ssk", h)
                    norm_scale(work, "lnk", "rnk", h)
                    first_tap("vtap", 0, V_ROW, h, "vhist")
                if slot == "C0":
                    sem_of(v, "qls", h)
                    s.did(f(ng[:, 1, 0:YW], ng[:, 1, 0:YW], ACT.Exp), "qsig")
                    sem_of(v, "vneg", h)
                    soft(0, YW, ("vexp", h), "vln")
                if slot == "C1":
                    sem_of(v, "qs", h)
                    s.did(f(G, gd["nQ"], ACT.Square), "sqq")
                    sem_of(v, "vls", h)
                    s.did(f(ng[:, 0, 0:YW], ng[:, 0, 0:YW], ACT.Exp), "vsig")
                    sem_of(t, "ssq", h)
                    norm_scale(G, "lnq", "rnq", h)
                if slot == "C3":
                    sem_of(v, "zneg", h)
                    soft(2, T, ("zexp", h), "zln")
                    sem_of(t, "stash", h)
                    if not isinstance(h, int) or h > 0:
                        act.wait_ge(cv_out, h * 32)
                    n = XW * (NSEQ + 1)
                    f(cout[:, 0:2].rearrange("r g p -> r (g p)"), rr[0:n, 2, 0:2 * P], ACT.Copy)
                    s.did(f(cout[:, 2], rr[0:n, 3, 0:P], ACT.Copy), "cout")
                    sem_of(s, "cout", h)
                    for dst, r0, n in ((conv_p, 0, XW), (conv_s, XW, XW * NSEQ)):
                        d = dst[0].rearrange("b j (g h p) -> (b j) g h p", g=3, h=H)[:, :, ds(h, 1), :]
                        act.dma_start(d.rearrange("r g o p -> r g (o p)"), cout[r0:r0 + n]).then_inc(cv_out, 16)

            def load_conv(h):
                src = state_conv[0].rearrange("b j (g h p) -> (b j) g h p", g=3, h=H)
                act.dma_start(cin[:], src[:, :, ds(h, 1), :].rearrange("r g o p -> r g (o p)")).then_inc(cv_in, 16)

            def gdn_sigmoid_z(h):
                v, s, t = st["ga"]
                sem_of(v, "zls", h)
                s.did(f(ng[:, 2, 0:T], ng[:, 2, 0:T], ACT.Exp), "zsig")

            def gdn_first_inverse(h):
                v, s, t = st["ga"]
                s.did(f(gd["K"], gd["nK"], ACT.Copy), "K")
                sem_of(t, "t0", h)
                f(gd["Tm"][:, 0:TP], rr[:, 1, :], ACT.Copy)
                s.did(f(gd["Tm"][0:TS, TP:T], rr[0:TS, 2, 0:TS], ACT.Copy), "tm0")

            def gdn_head(h, nxt):
                v, s, t = st["gr"]
                X, Tt, VN, oo, sqr = (gd[n] for n in ("X", "Tt", "VN", "oo", "sq"))
                act.wait_ge(st_out, h * 32 + 32 * H)
                load_state(state_gdn, h)
                for n, m in enumerate(LEVELS[1:], 1):
                    sem_of(t, f"x{m}", h)
                    last = f(X[:, 0:TP // 2], rr[:, 0, 0:TP // 2], ACT.Copy)
                    if m in SLEVELS:
                        last = f(X[0:TS, TP // 2:T // 2], rr[0:TS, 1, 0:TS // 2], ACT.Copy)
                    s.did(last, f"x{m}")
                    sem_of(t, f"tr{m}", h)
                    last = f(Tt[:, 0:TP], rr[:, 1, :], ACT.Copy)
                    if m in SLEVELS:
                        last = f(Tt[0:TS, TP:T], rr[0:TS, 0, 0:TS], ACT.Copy)
                    s.did(last, f"tt{m}")
                    if m == 32:
                        sem_of(t, "svn", h)
                        s.did(f(X[0:TS, VNS:VNS + P], rr[0:TS, 3, SVN:SVN + P], ACT.Copy), "vns")
                    if nxt is not None:
                        gdn_prepare(f"L{n}", nxt)
                    if m == 16:
                        sem_of(t, "srt", h)
                        s.did(f(X[0:TS, RS:RS + P], rr[0:TS, 2, SRT:SRT + P], ACT.Copy), "rs")
                    if m == 64:
                        sem_of(t, "os", h)
                        s.did(f(oo[:, TP:T], rr[:, 2, OS:OS + TS], ACT.Copy), "os")
                for c in range(NC):
                    sem_of(t, f"vn{c}", h)
                    s.did(f(VN[:, c * P:(c + 1) * P], rr[:, 0, P:2 * P], ACT.Copy), f"vn{c}")
                    if nxt is not None:
                        gdn_prepare(f"C{c}", nxt)
                sem_of(t, "o", h)
                s.did(f(oo[:, 0:TP], rr[:, 1, :], ACT.Copy), "oo")
                sem_of(s, "oo", h)
                s.did(f(sqr, oo, ACT.Square), "sq")
                if nxt is not None:
                    gdn_first_inverse(nxt)
                    gdn_sigmoid_z(nxt)
                sem_of(t, "ss", h)
                s.did(f(halves(sqr), rr[:, 2:4, 0:HALF], ACT.Ln, bias=epsc[:, 0:1], scale=1.0 / P), "ln")
                sem_of(s, "ln", h)
                s.did(f(sqr, sqr, ACT.Exp, scale=-0.5), "rn")
                sem_of(v, "sn1", h)
                store_states(gdn_p, gdn_s, h)
                sem_of(v, "og", h)
                s.did(f(oh[:, ds(h, 1)].rearrange("p o n -> p (o n)"), oo, ACT.Copy), "hi")

            def mlp(key):
                v, s, _ = st[key]

                with act.Fori(0, NGRP) as g:
                    for k in range(KT):
                        sem_of(v, f"s{k}", g)
                        s.did(f(oh[:, k], B[:, 2 + k % 2], ACT.Copy), f"hi{k}")

            load_state(state_hgrn, 0)
            norm("n0", None)
            for slot in range(3, 10):
                hgrn_prepare(slot, 0)
            with act.Fori(0, H - 1) as h:
                hgrn_head(h, h + 1)
            hgrn_head(H - 1, None)
            load_conv(0)
            norm("n1", U_MLP0 - 1)
            mlp("up0")
            norm("n2", U_AB - 1)
            gdn_pre()
            for slot in GDN_SLOTS:
                gdn_prepare(slot, 0)
            gdn_first_inverse(0)
            gdn_sigmoid_z(0)
            with act.Fori(0, H - 2) as h:
                gdn_head(h, h + 1)
            gdn_head(H - 2, H - 1)
            gdn_head(H - 1, None)
            norm("n3", U_MLP1 - 1)
            mlp("up1")
            norm("n4", U_END - 1)
            v, s, t = st["y"]
            for i in range(NC):
                sem_of(t, "t", i)
                if i >= 2:
                    act.wait_ge(y_out[i % 2], 16 * (i // 2))
                s.did(f(xrow[i % 2].rearrange("p (a n) -> p a n", a=2), rr[:, 2:4, :], ACT.Copy), "e")
                sem_of(s, "e", i)
                act.dma_start(y_prompt[0, i * P:(i + 1) * P, :], xrow[i % 2]).then_inc(y_out[i % 2], 16)
            v2, s2, t2 = st["ys"]
            sem_of(t2, "t", 0)
            act.wait_ge(y_out[0], 16 * (NC // 2))
            s2.did(f(xrow[NC % 2][0:TS].rearrange("p (a n) -> p a n", a=2), rr[0:TS, 2:4, :], ACT.Copy), "e")
            sem_of(s2, "e", 0)
            act.dma_start(y_sample.rearrange("b t d -> (b t) d"), xrow[NC % 2][0:TS]).then_inc(y_out[0], 16)
            act.wait_ge(y_out[0], 16 * (NC // 2 + 1))
            act.wait_ge(y_out[1], 16 * (NC // 2))
            act.wait_ge(st_out, 32 * H + 32 * H)
            act.wait_ge(cv_out, 32 * H)

        @block.vector
        def _(dve):
            tt, ts, stt, cp = nc.vector.tensor_tensor, nc.vector.tensor_scalar, nc.vector.scalar_tensor_tensor, nc.vector.tensor_copy
            pred = nc.vector.copy_predicated
            dve.wait_ge(c_in, 16 * N_CONST)
            for n, stage_ in enumerate(cstage):
                masks = cp(cu[:, n * CU_HALF:(n + 1) * CU_HALF], stage_)

            def after(steps, name, i):
                dve.wait_ge(steps.sem, steps.after(name, i))

            v, s, t = st["init"]
            v.did(masks, "masks")
            after(v, "masks", 0)
            nc.vector.memset(epsc[:], EPS).then_inc(unit_out, 2)
            for buf in (hg["KL"], hg["QL"], gt4[:], gcol[:], dtb[:]):
                nc.vector.memset(buf, 0.0)
            v.did(nc.vector.memset(zeros[:], 0.0), "fill")
            after(t, "vec", 0)
            v.did(cp(vec[:], rr[:, 0, 0:V_N]), "vec")
            nc.vector.memset(xp[:], 0.0)
            v.did(cp(cw[:].rearrange("p j s -> p (j s)"), rr[:, 1, 0:CONV * 3 * H]), "cw")
            lb = vec[:, V_LB:V_LB + H]
            after(v, "vec", 0)
            v.did(tt(lbt[:, 3], lb, lb, ALU.subtract), "lb1")
            after(s, "lb1", 0)
            v.did(nc.vector.reciprocal(lbt[:, 2], lbt[:, 3]), "lb2")
            after(v, "lb2", 0)
            v.did(tt(lbt[:, 3], lbt[:, 3], lbt[:, 2], ALU.mult), "lb3")
            after(v, "lb3", 0)
            v.did(tt(lbt[:, 3], lbt[:, 3], lbt[:, 3], ALU.subtract), "lb4")
            after(v, "lb4", 0)
            ts(lbt[:, 0], lbt[:, 3], -1.0, 1.0, ALU.mult, ALU.add)
            v.did(ts(lbt[:, 1], lbt[:, 3], LB_FLOOR, None, ALU.max), "lb5")
            after(s, "lb3", 0)
            v.did(ts(lbt[:, 1], lbt[:, 1], float(-np.log(LN_SHIFT)), None, ALU.add), "lb6")

            v, s, t = st["x"]
            for i in range(NC):
                after(t, "t", i)
                v.did(cp(xT[:, :, i * P:(i + 1) * P], rr[:, 2:4, :].rearrange("p a (k n) -> p (a k) n", n=P)), "copy")
            v2, _, t2 = st["xs"]
            after(t2, "t", 0)
            v2.did(cp(xT[:, :, TP:T], rr[:, 2, 0:KT * TS].rearrange("p (k n) -> p k n", n=TS)), "copy")

            def norm(key, wcol, u_before):
                v, _, _ = st[key]
                if u_before is None:
                    after(st["xs"][0], "copy", 0)
                else:
                    dve.wait_ge(unit_out, unit_done(u_before))
                for k in range(KT):
                    w = vec[:, wcol + k:wcol + k + 1]
                    v.did(ts(xh[:, k], xT[:, k], w, None, ALU.mult), f"hi{k}")
                    after(v, f"hi{k}", 0)
                    v.did(stt(out=xl[:, k], in0=xT[:, k], scalar=w, in1=xh[:, k].bitcast(F32),
                              op0=ALU.mult, op1=ALU.subtract), f"lo{k}")

            def computed(U, r, j):
                dve.wait_ge(w_used, r + (U + j + 1))
                return psum_out((U + j) % SPLIT)

            def out_tail(h, v, s, wcol, oo, rn, gate, gate_of):
                after(s, "rn", h)
                v.did(stt(out=oo, in0=oo, scalar=vec[:, wcol:wcol + 1], in1=rn, op0=ALU.mult, op1=ALU.mult), "on")
                after(v, "on", h)
                after(gate_of, "gate", h)
                v.did(tt(oo, oo, gate, ALU.mult), "og")
                after(s, "hi", h)
                v.did(tt(ol[:, ds(h, 1)].rearrange("p o n -> p (o n)"), oo,
                         oh[:, ds(h, 1)].rearrange("p o n -> p (o n)"), ALU.subtract), "lo")

            def last_of(ap, m):
                b = blocks(ap, m)
                return b[:, :, m - 1:m].broadcast_to([b.shape[0], b.shape[1], m])

            def less_than_last(out, ap):
                tt(blocks(out[:, 0:TP], P), last_of(ap[:, 0:TP], P), blocks(ap[:, 0:TP], P), ALU.subtract)
                return tt(blocks(out[:, TP:T], SLEN), last_of(ap[:, TP:T], SLEN), blocks(ap[:, TP:T], SLEN), ALU.subtract)

            def over_chunks(ap):
                return ap.unsqueeze(1).broadcast_to([ap.shape[0], NC, P])

            def apart(out, vs):
                for a in range(2):
                    last = tt(blocks(out[a], P), vs.unsqueeze(1).broadcast_to([TS, NSEQ // 2, P]),
                              cf[0:TS, C_SEQ + 4 * a:C_SEQ + 4 * a + 4].unsqueeze(2).broadcast_to([TS, NSEQ // 2, P]),
                              ALU.mult)
                return last

            def decay_samples(decay):
                return tt(S0[:], S0[:], blocks(decay, SLEN)[:, :, SLEN - 1:SLEN].broadcast_to([P, NSEQ, P]), ALU.mult)

            def prompt_state(c, h, v, bank, decay):
                if c == 0:
                    v.did(cp(Sp[:, 0], bank), "S0")
                else:
                    after(v, f"S{c - 1}", h)
                    v.did(stt(out=Sp[:, c], in0=Sp[:, c - 1], scalar=decay, in1=bank, op0=ALU.mult, op1=ALU.add), f"S{c}")

            def negative_abs(row, w):
                return stt(out=ng[:, row, 0:w], in0=pr[:, row, 0:w], scalar=-1.0, in1=pr[:, row, 0:w], op0=ALU.mult,
                           op1=ALU.min)

            def log_sigmoid(row, w):
                return stt(out=ng[:, row, 0:w], in0=pr[:, row, 0:w], scalar=0.0, in1=ng[:, row, 0:w], op0=ALU.min,
                           op1=ALU.subtract)

            def hgrn_prepare(slot, h):
                v, s, t = st["ha"]
                T1 = xp[:, 0, XW:XW + T]

                def evacuate(j, dst):
                    tt(halves(dst), computed(U_HIN, h * 4, j), halves(rstd[:]), ALU.mult).then_inc(unit_out, 1)

                def evacuated(j):
                    dve.wait_ge(unit_out, h * 4 + (U_HIN + j + 3))

                if slot == 2:
                    v.did(cp(hc[:, 0:3], lbt[:, 0:3, ds(h, 1)].rearrange("p r o -> p (r o)")), "cols")
                    evacuate(0, pr[:, 1, 0:T])
                    evacuated(0)
                    v.did(negative_abs(1, T), "fneg")
                if slot == 3:
                    after(s, "fln", h)
                    v.did(log_sigmoid(1, T), "fls")
                    after(v, "fls", h)
                    v.did(tt(pr[:, 1, 0:T], ng[:, 1, 0:T], pr[:, 1, 0:T], ALU.subtract), "fb")
                    v.did(ts(T1, ng[:, 1, 0:T], hc[:, 2:3], hc[:, 1:2], ALU.add, ALU.subtract), "cd")
                    after(v, "cd", h)
                    v.did(stt(out=T1, in0=T1, scalar=-1.0, in1=T1, op0=ALU.mult, op1=ALU.min), "nabs")
                if slot == 4:
                    v.did(ts(ng[:, 1, 0:T], ng[:, 1, 0:T], hc[:, 2:3], hc[:, 1:2], ALU.add, ALU.max), "cmax")
                    evacuate(1, pr[:, 0, 0:T])
                    evacuated(1)
                    v.did(negative_abs(0, T), "qneg")
                if slot == 5:
                    after(s, "qln", h)
                    v.did(log_sigmoid(0, T), "qls")
                    after(v, "cmax", h)
                    v.did(tt(ng[:, 1, 0:T], ng[:, 1, 0:T], T1, ALU.add), "lf")
                if slot == 6:
                    evacuate(2, pr[:, 2, 0:T])
                    evacuated(2)
                    v.did(negative_abs(2, T), "gneg")
                if slot == 7:
                    after(s, "gln", h)
                    v.did(log_sigmoid(2, T), "gls")
                    evacuate(3, hg["val"])
                if slot == 8:
                    after(s, "qsig", h)
                    v.did(tt(hg["Q"], pr[:, 0, 0:T], ng[:, 0, 0:T], ALU.mult), "Q")
                    v.did(ts(hg["K"], pr[:, 1, 0:T], hc[:, 0:1], None, ALU.mult), "K")
                    after(v, "lf", h)
                    v.did(nc.vector.tensor_tensor_scan(hg["b"], reset, ng[:, 1, 0:T], 0.0, ALU.mult, ALU.add), "scan")
                    after(v, "scan", h)
                    v.did(less_than_last(hg["bd"], hg["b"]), "bd")
                if slot == 9:
                    after(s, "gsig", h)
                    v.did(tt(hg["gate"], pr[:, 2, 0:T], ng[:, 2, 0:T], ALU.mult), "gate")

            def hgrn_head(h, nxt):
                (v, s, t), (va, sa, ta) = st["hr"], st["ha"]
                Q, K, val, b, eb, qe, kd, dd, KL, A = (hg[n] for n in ("Q", "K", "val", "b", "eb", "qe", "kd", "dd",
                                                                       "KL", "A"))
                after(sa, "ebd", h)
                after(va, "K", h)
                v.did(tt(qe, Q, eb, ALU.mult), "qe")
                v.did(tt(kd, K, hg["bd"], ALU.mult), "kd")

                def differences(n, m):
                    w = width(m)
                    mid = first_half(b[:, 0:w], m)[:, :, m - 1:m].broadcast_to([P, w // (2 * m), m])
                    if n >= 2:
                        after(v, f"kl{LEVELS[n - 2]}", h)
                    tt(second_half(dd[:, n % 2, 0:w], m), second_half(b[:, 0:w], m), mid, ALU.subtract)
                    v.did(tt(first_half(dd[:, n % 2, 0:w], m), mid, first_half(b[:, 0:w], m), ALU.subtract), f"d{m}")

                def keep(n, m):
                    ready, kept = fixed(dve, t.after(f"lv{m}", h)), fixed(dve, v.after(f"pred{m // 2}" if n else "adiag", h))
                    dve.wait_ge(c_in, 16 * N_CONST)
                    dve.wait_ge(t.sem, ready)
                    dve.wait_ge(v.sem, kept)
                    last = pred(second_half(A[:, 0:TP], m), blocks(mask[:, 0, n, 0:TP // 2], m),
                                blocks(rr[:, n % 2, 0:TP // 2], m))
                    if m in SLEVELS:
                        last = pred(second_half(A[0:TS, TP:T], m), blocks(mask[0:TS, 0, n, TP // 2:T // 2], m),
                                    blocks(rr[0:TS, n % 2, TP // 2:T // 2], m))
                    v.did(last, f"pred{m}")

                differences(0, 1)
                after(t, "diag", h)
                tt(blocks(A[:, 0:TP], P), blocks(rr[:, 2, :], P), over_chunks(eye), ALU.mult)
                v.did(tt(A[0:TS, TP:T], rr[0:TS, 3, 0:TS], cf[0:TS, C_EYE:C_EYE + TS], ALU.mult), "adiag")
                for n, m in enumerate(LEVELS):
                    w = width(m)
                    if m < LEVELS[-1]:
                        differences(n + 1, 2 * m)
                    after(s, f"e{m}", h)
                    if n >= 2:
                        after(t, f"lv{LEVELS[n - 2]}", h)
                    tt(blocks(QL[:, n % 2, 0:w // 2], m), second_half(Q[:, 0:w], m), second_half(dd[:, n % 2, 0:w], m), ALU.mult)
                    v.did(tt(first_half(KL[:, n % 2, 0:w], m), first_half(K[:, 0:w], m), first_half(dd[:, n % 2, 0:w], m),
                             ALU.mult), f"kl{m}")
                    if n:
                        keep(n - 1, LEVELS[n - 1])
                    if m == 16:
                        after(t, "dS", h)
                        dve.wait_ge(st_in, h * 16 + 16)
                        for c in range(NC):
                            end = c * P + P - 1
                            prompt_state(c, h, v, rr[:, 2, c * P:(c + 1) * P], eb[:, end:end + 1])
                    if m == 32:
                        after(s, "kdTs", h)
                        v.did(apart([hg["vbig"][0:TS, a, 0:4 * P] for a in range(2)], vTs[:]), "vbig")
                        after(t, "os", h)
                        v.did(decay_samples(eb[:, TP:T]), "sdec")
                    if m == 64:
                        after(t, "dSs", h)
                        after(v, "sdec", h)
                        v.did(tt(S0[:], S0[:], rr[:, 2:4, :].rearrange("p a (b n) -> p (a b) n", n=P), ALU.add), "snew")
                    if nxt is not None:
                        hgrn_prepare(n, nxt)
                keep(len(LEVELS) - 1, LEVELS[-1])
                if nxt is not None:
                    hgrn_prepare(7, nxt)
                    hgrn_prepare(8, nxt)
                out_tail(h, v, s, V_HON, hg["oo"], hg["sq"], hg["gate"], va)
                if nxt is not None:
                    hgrn_prepare(9, nxt)

            def gdn_pre():
                v, s, t = st["gp"]
                cp(dtb[0:H], gsc[0:H, 1:2]).then_inc(dt_ready, 1)
                b = [B[0:64, n] for n in range(4)]
                tt(halves(b[0]), computed(U_AB, 0, 0)[0:64], halves(rstd[0:64]), ALU.mult).then_inc(unit_out, 1)
                dve.wait_ge(unit_out, unit_done(U_AB))
                dve.wait_ge(dt_ready, 1)
                v.did(ts(b[0], b[0], dtb[:, 0:1], None, ALU.add), "x")
                after(v, "x", 0)
                v.did(stt(out=b[1], in0=b[0], scalar=-1.0, in1=b[0], op0=ALU.mult, op1=ALU.min), "neg")
                after(s, "ln", 0)
                v.did(stt(out=b[2], in0=b[0], scalar=0.0, in1=b[1], op0=ALU.min, op1=ALU.subtract), "ls")
                v.did(stt(out=b[3][0:H], in0=b[0][0:H], scalar=0.0, in1=b[1][0:H], op0=ALU.max, op1=ALU.add), "g")
                after(v, "g", 0)
                v.did(ts(b[3][0:H], b[3][0:H], gsc[:, 2:3], -1.0, ALU.mult, ALU.mult), "g2")
                after(v, "g2", 0)
                v.did(nc.vector.tensor_tensor_scan(gt4[0:H], reset[0:H], b[3][0:H], 0.0, ALU.mult, ALU.add), "scan")
                after(v, "scan", 0)
                v.did(less_than_last(b[3][0:H], gt4[0:H]), "dl")

            def gdn_prepare(slot, h):
                v, s, t = st["ga"]
                nQ, nK, nV, work, G, dec = (gd[n] for n in ("nQ", "nK", "nV", "work", "G", "dec"))
                of_head = lambda r: gcol[:, :, H * r:H * (r + 1)][:, :, ds(h, 1)]

                def evacuate(j, row):
                    ps = computed(U_GIN, h * 4, j)
                    cut = TP - HALF
                    tt(xp[:, row, XW:XW + HALF], ps[:, 0], rstd[:, 0:HALF], ALU.mult)
                    tt(xp[:, row, XW + HALF:XW + TP], ps[:, 1, 0:cut], rstd[:, HALF:TP], ALU.mult)
                    tt(blocks(xp[:, row, SB0:XPW], SROW)[:, :, XW:SROW], blocks(ps[:, 1, cut:HALF], SLEN),
                       blocks(rstd[:, TP:T], SLEN), ALU.mult).then_inc(unit_out, 1)

                def convolve(name, tap, row, g):
                    after(s, tap, h)
                    for j in range(1, CONV):
                        if j > 1:
                            after(v, f"{name}{j - 1}", h)
                        v.did(stt(out=pr[:, row, 0:YW], in0=xp[:, row, j:j + YW], scalar=hcw[:, j, g:g + 1],
                                  in1=pr[:, row, 0:YW], op0=ALU.mult, op1=ALU.add), f"{name}{j}")
                    after(v, f"{name}3", h)
                    v.did(negative_abs(row, YW), f"{name}neg")

                def silu(name, row, dst):
                    after(s, f"{name}sig", h)
                    tt(dst[:, 0:TP], pr[:, row, 0:TP], ng[:, row, 0:TP], ALU.mult)
                    v.did(tt(blocks(dst[:, TP:T], SLEN), blocks(pr[:, row, SB0:XPW], SROW)[:, :, 0:SLEN],
                             blocks(ng[:, row, SB0:XPW], SROW)[:, :, 0:SLEN], ALU.mult), f"{name}s")

                def decayed(bank, name):
                    dst = work if name == "kkd" else dec
                    tt(dst[:, 0:TP].rearrange("p (a n) -> p a n", a=2), rr[:, 2:4, 0:2 * P],
                       dec[:, 0:TP].rearrange("p (a n) -> p a n", a=2), ALU.mult)
                    v.did(tt(dst[0:TS, TP:T], rr[0:TS, bank, 2 * P:2 * P + TS], dec[0:TS, TP:T], ALU.mult), name)

                if slot == "L1":
                    cp(hc[:, 4:5], cf[:, ds(h + C_HSEL, 1)])
                    cp(hcw[:], cw[:].rearrange("p j (g x) -> p j g x", g=3)[:, :, :, ds(h, 1)]
                       .rearrange("p j g o -> p j (g o)"))
                    v.did(cp(gnext[:], of_head(0).rearrange("p c o -> p (c o)")), "cols")
                    after(v, "cols", h)
                    v.did(ts(work, gt4[:], hc[:, 4:5], None, ALU.mult), "gsel")
                if slot == "L2":
                    evacuate(0, 0)
                if slot == "L3":
                    evacuate(1, 1)
                    convolve("k", "ktap", 0, K_ROW)
                if slot == "L4":
                    after(s, "G", h)
                    for c in range(NC):
                        cols = slice(c * P, (c + 1) * P)
                        ts(dec[:, cols], G[:, cols], gnext[:, c:c + 1], 0.0, ALU.subtract, ALU.min)
                    v.did(ts(dec[0:TS, TP:T], G[0:TS, TP:T], gnext[0:TS, NC:NC + 1], 0.0, ALU.subtract, ALU.min), "dec")
                    after(s, "kln", h)
                    v.did(log_sigmoid(0, YW), "kls")
                if slot == "L5":
                    convolve("q", "qtap", 1, Q_ROW)
                    silu("k", 0, nK)
                    evacuate(2, 0)
                if slot == "L6":
                    after(s, "qln", h)
                    v.did(log_sigmoid(1, YW), "qls")
                    after(s, "rnk", h)
                    after(v, "ks", h)
                    v.did(tt(nK, nK, work, ALU.mult), "kn")
                    after(v, "kn", h)
                    v.did(tt(work, nK, gd["beta"], ALU.mult), "kb")
                    convolve("v", "vtap", 0, V_ROW)
                if slot == "C0":
                    silu("q", 1, nQ)
                    after(t, "kk", h)
                    decayed(2, "kkd")
                    after(s, "vln", h)
                    v.did(log_sigmoid(0, YW), "vls")
                if slot == "C1":
                    silu("v", 0, nV)
                    after(s, "rnq", h)
                    v.did(stt(out=nQ, in0=nQ, scalar=float(P) ** -0.5, in1=G, op0=ALU.mult, op1=ALU.mult), "qn")
                    after(v, "kkd", h)
                    tt(blocks(gd["NL"][:, 0:TP], P), blocks(work[:, 0:TP], P), over_chunks(cf[:, C_NSTR:C_NSTR + P]), ALU.mult)
                    v.did(tt(gd["NL"][0:TS, TP:T], work[0:TS, TP:T], cf[0:TS, C_NSTRS:C_NSTRS + TS], ALU.mult), "nl")
                if slot == "C2":
                    after(t, "qk", h)
                    decayed(3, "qkd")
                    tt(halves(pr[:, 2, 0:T]), computed(U_GIN, h * 4, 3), halves(rstd[:]), ALU.mult).then_inc(unit_out, 1)
                    dve.wait_ge(unit_out, h * 4 + (U_GIN + 3 + 3))
                    v.did(negative_abs(2, T), "zneg")
                if slot == "C3":
                    after(s, "zln", h)
                    v.did(log_sigmoid(2, T), "zls")
                if slot == "inverse":
                    Tt, NL = gd["Tt"], gd["NL"]
                    cp(blocks(Tt[:, 0:TP], P), over_chunks(eye))
                    v.did(cp(Tt[0:TS, TP:T], cf[0:TS, C_EYE:C_EYE + TS]), "tt0")
                    ready = fixed(dve, v.after("tt0", h))
                    dve.wait_ge(c_in, 16 * N_CONST)
                    dve.wait_ge(v.sem, ready)
                    pred(second_half(Tt[:, 0:TP], 1), blocks(mask[:, 0, 0, 0:TP // 2], 1), second_half(NL[:, 0:TP], 1))
                    v.did(pred(second_half(Tt[0:TS, TP:T], 1), blocks(mask[0:TS, 0, 0, TP // 2:T // 2], 1),
                               second_half(NL[0:TS, TP:T], 1)), "tt1")
                if slot == "move":
                    after(v, "qkd", h)
                    tt(blocks(gd["A"][:, 0:TP], P), blocks(dec[:, 0:TP], P), over_chunks(cf[:, C_INCL:C_INCL + P]), ALU.mult)
                    v.did(tt(gd["A"][0:TS, TP:T], dec[0:TS, TP:T], cf[0:TS, C_INCLS:C_INCLS + TS], ALU.mult), "A")
                    after(v, "qn", h)
                    v.did(tt(gd["qe"], nQ, gd["eG"], ALU.mult), "qe")
                    for r in range(4):
                        cp(gcols[:, :, r:r + 1], of_head(r))
                    cp(eGs[:, 0:NC], blocks(gd["eG"][:, 0:TP], P)[:, :, P - 1])
                    cp(eGs[:, NC:], gd["eG"][:, TP:T])
                    v.did(cp(betas[:], gd["beta"][:, TP:T]), "cols2")
                    after(v, "cols2", h)
                    v.did(stt(out=nbe[:], in0=gcols[:, :, 1], scalar=-1.0, in1=gcols[:, :, 3], op0=ALU.mult, op1=ALU.mult),
                          "nbe")
                if slot == "gate":
                    after(s, "zsig", h)
                    v.did(tt(gd["gate"], pr[:, 2, 0:T], ng[:, 2, 0:T], ALU.mult), "gate")

            def gdn_head(h, nxt):
                (v, s, t), (va, sa, ta) = st["gr"], st["ga"]
                Tm, vT, kdT = gd["Tm"], gd["vT"], gd["kdT"]
                after(va, "nbe", h)

                def turned(dst, col, name):
                    for a in range(2):
                        last = tt(blocks(dst[:, a * 2 * P:(a + 1) * 2 * P], P), blocks(rr[:, 2 + a, 0:2 * P], P),
                                  gcols[:, 2 * a:2 * a + 2, col:col + 1].broadcast_to([P, 2, P]), ALU.mult)
                    v.did(last, name)

                for n, m in enumerate(LEVELS[1:], 1):
                    if n == 1:
                        after(sa, "tm0", h)
                    ready = fixed(dve, t.after(f"dt{m}", h))
                    dve.wait_ge(c_in, 16 * N_CONST)
                    dve.wait_ge(t.sem, ready)
                    last = pred(first_half(Tm[:, 0:TP], m), blocks(mask[:, 1, n, 0:TP // 2], m), blocks(rr[:, 0, 256:512], m))
                    if m in SLEVELS:
                        last = pred(first_half(Tm[0:TS, TP:T], m), blocks(mask[0:TS, 1, n, TP // 2:T // 2], m),
                                    blocks(rr[0:TS, 1, TS // 2:TS], m))
                    v.did(last, f"pred{m}")
                    if m == 2:
                        after(t, "vT", h)
                        turned(vT, 1, "vb")
                    if m == 4:
                        after(t, "sks", h)
                        turned(kdT, 2, "kdt")
                        v.did(ts(kdTs[:], rr[0:TS, 2, SRT:SRT + P], gcols[0:TS, NC, 2:3], None, ALU.mult), "kdts")
                        v.did(tt(rt[:], rr[:, 2, SKS:SKS + TS], eGs[:, NC:], ALU.mult), "sr1")
                        after(v, "sr1", h)
                        v.did(tt(rt[:], gd["nV"][:, TP:T], rt[:], ALU.subtract), "sr2")
                        after(v, "sr2", h)
                        v.did(tt(rt[:], rt[:], betas[:], ALU.mult), "sr3")
                    if nxt is not None:
                        gdn_prepare(f"L{n}", nxt)
                for c in range(NC):
                    if c:
                        after(t, f"ks{c}", h)
                        v.did(stt(out=vT[:, c * P:(c + 1) * P], in0=rr[:, 0, 0:P], scalar=nbe[:, c:c + 1],
                                  in1=vT[:, c * P:(c + 1) * P], op0=ALU.mult, op1=ALU.add), f"r{c}")
                    else:
                        dve.wait_ge(st_in, h * 16 + 16 * (H + 1))
                    after(t, f"dS{c}", h)
                    prompt_state(c, h, v, rr[:, 0, 2 * P:3 * P], eGs[:, c:c + 1])
                    if c == 0:
                        after(s, "vns", h)
                        after(t, "tr64", h)
                        v.did(apart(gd_vbig, gd["X"][0:TS, VNS:VNS + P]), "vbig")
                        after(t, "os", h)
                        v.did(decay_samples(eGs[:, NC:]), "sdec")
                    if nxt is not None:
                        gdn_prepare(f"C{c}", nxt)
                if nxt is not None:
                    gdn_prepare("inverse", nxt)
                for a in range(2):
                    after(t, f"dSs{a}", h)
                    after(v, "sdec", h)
                    half = S0[:, 4 * a:4 * a + 4, :].rearrange("p b n -> p (b n)")
                    v.did(tt(half, half, rr[:, 0, :], ALU.add), f"sn{a}")
                if nxt is not None:
                    after(t, "o", h)
                    gdn_prepare("move", nxt)
                out_tail(h, v, s, V_GON, gd["oo"], gd["sq"], gd["gate"], va)
                if nxt is not None:
                    gdn_prepare("gate", nxt)

            def out_proj(U):
                with dve.Fori(0, 2) as i:
                    for j in range(4):
                        x = xT[:, ds(i * 4 + j, 1)].rearrange("p o (a n) -> p (o a) n", a=2)
                        tt(x, x, computed(U, i * 4, j), ALU.add).then_inc(unit_out, 1)

            def mlp(U, nkey, key):
                v, s, _ = st[key]
                after(st[nkey][1], "rstd", 0)
                with dve.Fori(0, NGRP) as g:
                    r = g * (2 * KT)

                    def rest(k):
                        after(s, f"hi{k}", g)
                        v.did(tt(ol[:, k], B[:, 2 + k % 2], oh[:, k], ALU.subtract), f"lo{k}")

                    for k in range(KT):
                        tt(halves(B[:, k % 2]), computed(U, r, k), halves(rstd[:]), ALU.mult).then_inc(unit_out, 1)
                        dve.wait_ge(unit_out, r + (U + k + 3))
                        v.did(stt(out=B[:, 2 + k % 2], in0=B[:, k % 2], scalar=0.0, in1=B[:, k % 2],
                                  op0=ALU.max, op1=ALU.mult), f"s{k}")
                        if k:
                            rest(k - 1)
                    rest(KT - 1)
                    for k in range(KT):
                        tt(halves(xT[:, k]), halves(xT[:, k]), computed(U, r, KT + k), ALU.add).then_inc(unit_out, 1)

            norm("n0", V_MIX, None)
            after(st["n0"][1], "rstd", 0)
            for slot in range(2, 10):
                hgrn_prepare(slot, 0)
            with dve.Fori(0, H - 1) as h:
                hgrn_head(h, h + 1)
            hgrn_head(H - 1, None)
            out_proj(U_HOUT)
            norm("n1", V_MLP, U_MLP0 - 1)
            mlp(U_MLP0, "n1", "up0")
            norm("n2", V_MIX + KT, U_AB - 1)
            after(st["n2"][1], "rstd", 0)
            gdn_pre()
            after(st["gp"][1], "cols", 0)
            for slot in GDN_SLOTS + ["inverse", "move", "gate"]:
                gdn_prepare(slot, 0)
            with dve.Fori(0, H - 1) as h:
                gdn_head(h, h + 1)
            gdn_head(H - 1, None)
            out_proj(U_GOUT)
            norm("n3", V_MLP + KT, U_MLP1 - 1)
            mlp(U_MLP1, "n3", "up1")
            after(st["n4"][1], "rstd", 0)

            def result(i, cols, steps):
                n = cols.stop - cols.start
                for k in range(KT):
                    last = stt(out=ycol[i % 2][:, k * P:k * P + n], in0=xT[:, k, cols], scalar=vec[:, V_FIN + k:V_FIN + k + 1],
                               in1=rstd[:, cols], op0=ALU.mult, op1=ALU.mult)
                steps.did(last, "y")

            v, s, t = st["y"]
            for i in range(NC):
                if i >= 2:
                    after(t, "t", i - 2)
                result(i, slice(i * P, (i + 1) * P), v)
            after(t, "t", NC - 2)
            result(NC, slice(TP, T), st["ys"][0])


_INS = ['x_prompt', 'x_sample', 'state_hgrn', 'state_gdn', 'state_gdn_conv', 'norm_mix', 'norm_mlp', 'norm_final',
        'hgrn_w_in', 'hgrn_lb', 'hgrn_out_norm', 'hgrn_w_out', 'gdn_w_in', 'gdn_conv_w', 'gdn_A_log', 'gdn_dt_bias',
        'gdn_out_norm', 'gdn_w_out', 'mlp_w_up', 'mlp_w_down']
_OUTS = [(1, TP, D), (NSEQ, SLEN, D), (1, 1, H, P, P), (1, NSEQ, H, P, P), (1, 1, H, P, P), (1, NSEQ, H, P, P),
         (1, 1, XW, 3 * D), (1, NSEQ, XW, 3 * D)]


def kernel(**inputs):
    import concourse.bacc as _bacc
    from concourse.bass_utils import run_bass_kernel_spmd as _run

    nc = _bacc.Bacc("TRN2", target_bir_lowering=False, num_devices=1)
    arrays, args = {}, []
    named = [(name, np.ascontiguousarray(inputs[name])) for name in _INS]
    named += list(zip(("const_f", "const_u"), shape_constants()))
    for name, a in named:
        arrays[f"in_{name}_dram"] = a
        args.append(nc.dram_tensor(f"in_{name}_dram", a.shape, mybir.dt.from_np(a.dtype), kind="ExternalInput").ap())
    for i, shape in enumerate(_OUTS):
        args.append(nc.dram_tensor(f"out_{i}_dram", shape, F32, kind="ExternalOutput").ap())
    build(nc, *args)
    r = _run(nc, [arrays], core_ids=[0])
    return tuple(r.results[0][f"out_{i}_dram"] for i in range(len(_OUTS)))
```

```python
from contextlib import ExitStack

import numpy as np

import concourse.bass as bass
from concourse import mybir

F32 = mybir.dt.float32
F32R = mybir.dt.float32r
U8 = mybir.dt.uint8
ALU = mybir.AluOpType
ACT = mybir.ActivationFunctionType
ds = bass.ds

P = 128
D = 1024
KT = D // P
TP = 512
NSEQ, SLEN = 8, 4
TS = NSEQ * SLEN
T = TP + TS
HALF = T // 2
NC = TP // P
H = 8
FF = 4 * D
NGRP = FF // D
EPS = 1e-6
LB_FLOOR = 1e-30
LN_SHIFT = 2.0 ** 60
CONV = 4
XW = CONV - 1
SB0 = XW + TP
SROW = XW + SLEN
XPW = SB0 + NSEQ * SROW
YW = XPW - XW
LEVELS = [1, 2, 4, 8, 16, 32, 64]
SLEVELS = [m for m in LEVELS if 2 * m <= SLEN]
RAW, SPLIT = 4, 2

V_MIX, V_MLP, V_FIN, V_LB, V_HON, V_GON, V_CONV = 0, 16, 32, 40, 48, 49, 50
V_N = V_CONV

C_EYE, C_INCL, C_NSTR, C_IND, C_RESET, C_SEQ, C_INCLS, C_NSTRS, C_HSEL = 0, 128, 256, 384, 640, 1184, 1192, 1224, 1256
C_W = C_HSEL + H
CU_HALF = len(LEVELS) * (T // 2)

WS_ROWS = 22
HGRN_ORDER = [1, 0, 3, 2]
GDN_ORDER = [1, 0, 2, 3]
Q_ROW, K_ROW, V_ROW = 0, 1, 2
GDN_SLOTS = ["L0", "L1", "L2x", "L2", "L3x", "L3", "L4x", "L4", "L5x", "L5", "L6x", "L6", "C0", "C1", "C2"]

SRT = 352
SVN = 288
RS, VNS = T // 2, T // 2 + P


def shape_constants():
    cf = np.zeros((P, C_W), np.float32)
    p = np.arange(P)
    cf[:, C_EYE:C_EYE + P] = np.eye(P)
    cf[:, C_INCL:C_INCL + P] = p[None, :] >= p[:, None]
    cf[:, C_NSTR:C_NSTR + P] = -(p[None, :] > p[:, None]).astype(np.float32)
    cf[0:32, C_IND:C_IND + P] = 1
    cf[32:64, C_IND + P:C_IND + 2 * P] = 1
    t = np.arange(T)
    first = np.where(t < TP, t % P == 0, (t - TP) % SLEN == 0)
    cf[:, C_RESET:C_RESET + T] = ~first
    s = np.arange(TS)
    cf[:TS, C_SEQ:C_SEQ + NSEQ] = s[:, None] // SLEN == np.arange(NSEQ)[None, :]
    same = s[:, None] // SLEN == s[None, :] // SLEN
    cf[:TS, C_INCLS:C_INCLS + TS] = same & (s[None, :] >= s[:, None])
    cf[:TS, C_NSTRS:C_NSTRS + TS] = -(same & (s[None, :] > s[:, None])).astype(np.float32)
    cf[:, C_HSEL:C_HSEL + H] = p[:, None] % 32 == np.arange(H)[None, :]
    cu = np.zeros((P, 2, len(LEVELS), T // 2), np.float32)
    for n, m in enumerate(LEVELS):
        c = np.arange(T // 2)
        blk, local = c // m, np.where(c < TP // 2, (c // m) % (P // (2 * m)), (c - TP // 2) // m)
        rb, rh = p // (2 * m), (p // m) % 2
        hit = rb[:, None] == local[None, :]
        cu[:, 0, n] = hit & (rh[:, None] == 0)
        cu[:, 1, n] = hit & (rh[:, None] == 1)
    return cf, cu.reshape(P, -1)


N_CONST = 12


class Steps:

    def __init__(self, sem, names):
        self.sem, self.names, self.at = sem, names, 0

    def did(self, instruction, name):
        assert self.names[self.at % len(self.names)] == name, (self.names[self.at % len(self.names)], name)
        self.at += 1
        instruction.then_inc(self.sem, 1)

    def after(self, name, i):
        return i * len(self.names) + (self.names.index(name) + 1)


def fixed(eng, value):
    return value if isinstance(value, int) else eng.to_reg(value)


def build(nc, x_prompt, x_sample, state_hgrn, state_gdn, state_conv, norm_mix, norm_mlp, norm_final, hgrn_w_in,
          hgrn_lb, hgrn_out_norm, hgrn_w_out, gdn_w_in, gdn_conv_w, gdn_A_log, gdn_dt_bias, gdn_out_norm, gdn_w_out,
          mlp_w_up, mlp_w_down, const_f, const_u, y_prompt, y_sample, hgrn_p, hgrn_s, gdn_p, gdn_s, conv_p, conv_s):
    with ExitStack() as ctx:
        def sb(name, shape, dt=F32):
            return ctx.enter_context(nc.sbuf_tensor(name, shape, dt))

        def sem(name):
            return ctx.enter_context(nc.semaphore(name))

        xT = sb("xT", [P, KT, T])
        xh = sb("xh", [P, KT, T], F32R)
        xl = sb("xl", [P, KT, T], F32R)
        oh = sb("oh", [P, KT, T], F32R)
        ol = sb("ol", [P, KT, T], F32R)
        w_raw = sb("w_raw", [P, RAW, KT, P])
        w_hi = sb("w_hi", [P, SPLIT, KT, P], F32R)
        w_lo = sb("w_lo", [P, SPLIT, KT, P], F32R)
        cf = sb("cf", [P, C_W])
        cu = sb("cu", [P, 2 * len(LEVELS) * (T // 2)], U8)
        vec = sb("vec", [P, V_N])
        cw = sb("cw", [P, CONV, 3 * H])
        hc = sb("hc", [P, 16])
        lbt = sb("lbt", [P, 4, H])
        ones = sb("ones", [P, P])
        epsc = sb("epsc", [P, 2])
        zeros = sb("zeros", [P, 1])
        rstd = sb("rstd", [P, T])
        eye = cf[:, C_EYE:C_EYE + P]
        reset = cf[:, C_RESET:C_RESET + T]
        mask = cu[:, :].rearrange("p (a l n) -> p a l n", a=2, l=len(LEVELS))

        ws = sb("ws", [P, WS_ROWS, T])

        def rows(names):
            at, out = 0, {}
            for entry in names:
                name, n = entry if isinstance(entry, tuple) else (entry, 1)
                out[name] = ws[:, at] if n == 1 else ws[:, at:at + n]
                at += n
            assert at <= WS_ROWS
            return out

        xrow = [ws[:, 0:4].rearrange("p a n -> p (a n)")[:, n * D:(n + 1) * D] for n in range(2)]
        ycol = [ws[:, 4:8].rearrange("p a n -> p (a n)")[:, n * D:(n + 1) * D] for n in range(2)]
        cstage = [ws[:, n:n + 4].rearrange("p a n -> p (a n)")[:, 0:CU_HALF] for n in (8, 12)]
        sq = ws[:, 16:18]
        acc = ws[:, 18]
        B = ws[:, 0:4]

        pr = sb("pr", [P, 3, XPW])
        ng = sb("ng", [P, 3, XPW])
        xp = sb("xp", [P, 2, XPW])
        hg = rows(["Q", "K", "val", "gate", "b", "bd", "eb", "oo", "qe", "kd", "QL", "A", "sq", ("dd", 2), ("KL", 2),
                   "vT", "kdT", ("vbig", 2)])
        gd = rows(["nQ", "nK", "nV", "work", "G", "beta", "eG", "dec",
                   "K", "qe", "gate", "A", "NL", "Tm", "Tt", "X", "kdT", "vT", "VN", "oo", "sq", "spare"])
        QL = hg["QL"].rearrange("p (a n) -> p a n", a=2)
        gd_vbig = [gd[n][0:TS, 0:4 * P] for n in ("Tm", "spare")]
        vTs = sb("vTs", [TS, P])
        kdTs = sb("kdTs", [TS, P])
        Sp = sb("Sp", [P, NC, P])
        S0 = sb("S0", [P, NSEQ, P])
        gt4 = sb("gt4", [P, T])
        gcol = sb("gcol", [P, NC + 1, 4 * H])
        gnext = sb("gnext", [P, NC + 1])
        gcols = sb("gcols", [P, NC + 1, 4])
        nbe = sb("nbe", [P, NC + 1])
        eGs = sb("eGs", [P, NC + TS])
        betas = sb("betas", [P, TS])
        hcw = sb("hcw", [P, CONV, 3])
        rt = sb("rt", [P, TS])
        hist = sb("hist", [P, 3, XW * NSEQ])
        cstash = sb("cstash", [P, 3, XW * (NSEQ + 1)])
        cout = sb("cout", [XW * (NSEQ + 1), 3, P])
        cin = sb("cin", [XW * NSEQ, 3, P])
        gsc = sb("gsc", [H, 4])
        dtb = sb("dtb", [64, 1])

        pj = ctx.enter_context(nc.psum_tensor("pj", [P, 2, 2, 512], F32))
        rr = ctx.enter_context(nc.psum_tensor("rr", [P, 4, 512], F32))

        w_in = [sem(f"weights_loaded{j}") for j in range(RAW)]
        ab_in = sem("ab_loaded")
        w_split = sem("weights_split")
        w_used = sem("weights_used")
        unit_out = sem("unit_evacuated")
        c_in = sem("constants_loaded")
        x_in = [sem(f"x_loaded{n}") for n in range(2)]
        st_in = sem("state_loaded")
        st_out = sem("state_stored")
        cv_in = sem("conv_rows_loaded")
        cv_out = sem("conv_rows_stored")
        y_out = [sem(f"y_stored{n}") for n in range(2)]
        x_done = sem("residual_tile_done")

        def levels(lists):
            return [n for names in lists for n in names]

        VS = dict(
            init=["masks", "fill", "vec", "cw", "lb1", "lb2", "lb3", "lb4", "lb5", "lb6"],
            x=["copy"], xs=["copy"],
            norm=[f"{n}{k}" for k in range(KT) for n in ("acc", "hi", "lo")], normf=[f"acc{k}" for k in range(KT)],
            ha=["cols", "fneg", "fls", "fb", "cd", "nabs", "cmax", "qneg", "qls", "lf", "gneg", "gls", "Q", "K", "scan",
                "bd", "gate"],
            hr=["qe", "kd", "d1", "adiag", "d2", "kl1", "d4", "kl2", "pred1", "d8", "kl4", "pred2", "d16", "kl8", "pred4",
                "d32", "kl16", "pred8", "S0", "S1", "S2", "S3", "d64", "kl32", "pred16", "vbig", "sdec", "kl64", "pred32",
                "snew", "pred64", "on", "og", "lo"],
            gp=["x", "neg", "ls", "g", "g2", "scan", "dl"],
            ga=["cols", "gsel", "k1", "k2", "k3", "kneg", "kls", "q1", "q2", "q3", "qneg", "dec", "ks", "qls", "kn", "kb",
                "v1", "v2", "v3", "vneg", "qs", "kkd", "vls", "vs", "qn", "zneg", "qkd", "nl", "zls", "tt0", "tt1", "A",
                "qe", "cols2", "nbe"],
            gr=["pred2", "vb", "pred4", "kdt", "kdts", "gate", "sr1", "pred8", "sr2", "sr3", "pred16", "pred32", "pred64",
                "S0", "r1", "S1", "r2", "S2", "vbig", "sdec", "r3", "S3", "sn0", "sn1"],
            gf=["on", "og", "lo"],
            up=["s0"] + levels([(f"s{k}", f"lo{k - 1}") for k in range(1, KT)]) + [f"lo{KT - 1}"],
            y=["y"], ys=["y"],
        )
        SS = dict(
            init=["lb1", "lb2", "lb3"],
            norm=[f"sq{k}" for k in range(KT)] + ["ln", "rstd"], normf=[f"sq{k}" for k in range(KT)] + ["ln", "rstd"],
            ha=["fexp", "fln", "kexp", "cexp", "cln", "qexp", "qln", "qsig", "gexp", "gln", "gsig", "ebd"],
            hr=["e1", "e2", "e4", "vT", "kdT", "e8", "kdTs", "e16", "e32", "os", "e64", "oo", "sq", "ln", "rn", "hi"],
            gp=["A", "exp", "ln", "be", "el", "eg", "cols"],
            ga=["hist", "past", "ktap", "qtap", "vhist", "kexp", "kln", "G", "ksig", "qexp", "qln", "bb", "dec",
                "sqk", "vtap", "qsig", "lnk", "rnk", "eG", "sqq", "vexp", "vln", "vsig", "lnq", "rnq", "zexp", "zln", "cout",
                "zsig", "K", "tm0"],
            gr=["x2", "tt2", "x4", "tt4", "x8", "tt8", "x16", "tt16", "x32", "rs", "tt32", "vns", "x64", "os",
                "vn0", "vn1", "vn2", "vn3", "oo", "sq"],
            gf=["ln", "rn", "hi"],
            up=[f"hi{k}" for k in range(KT)],
            y=["e"], ys=["e"],
        )
        TT = dict(
            init=["vec"], x=["t"], xs=["t"],
            norm=["sum"], normf=["sum"],
            hr=["diag", "lv1", "lv2", "vT", "kdT", "lv4", "smp", "lv8", "dS", "lv16", "os", "lv32", "dSs", "lv64", "o", "ss"],
            gp=["cols"],
            ga=["cin", "gb", "bb", "ssk", "kk", "ssq", "qk", "stash", "t0"],
            gr=["x2", "dt2", "tr2", "vT", "x4", "dt4", "tr4", "kT", "x8", "sks", "dt8", "tr8", "x16", "dt16", "tr16",
                "srt", "x32", "dt32", "tr32", "svn", "x64", "os", "dt64",
                "vn0", "dS0", "ks1", "vn1", "dS1", "ks2", "vn2", "dS2", "ks3", "vn3", "dS3", "o", "dSs0", "dSs1"],
            gf=["ss"],
            y=["t"], ys=["t"],
        )
        dt_ready = sem("dt_bias_ready")
        ones_set = sem("ones_set")
        st = {}

        def stage(kind, key):
            if key not in st:
                st[key] = tuple(Steps(sem(f"{e}_{key}"), d[kind]) if kind in d else None
                                for e, d in (("vector", VS), ("scalar", SS), ("tensor", TT)))
            return st[key]

        for kind, key in [("init", "init"), ("x", "x"), ("xs", "xs"), ("norm", "n0"), ("norm", "n1"), ("norm", "n2"),
                          ("norm", "n3"), ("normf", "n4"), ("ha", "ha"), ("hr", "hr"), ("gp", "gp"), ("ga", "ga"),
                          ("gr", "gr"), ("gf", "gf"), ("up", "up0"),
                          ("up", "up1"), ("y", "y"), ("ys", "ys")]:
            stage(kind, key)

        def halves(ap):
            return ap.rearrange("p (a n) -> p a n", a=2)

        def first_half(ap, m):
            return ap.rearrange("p (n two m) -> p n two m", two=2, m=m)[:, :, 0, :]

        def second_half(ap, m):
            return ap.rearrange("p (n two m) -> p n two m", two=2, m=m)[:, :, 1, :]

        def blocks(ap, m):
            return ap.rearrange("p (n m) -> p n m", m=m)

        def width(m):
            return T if m in SLEVELS else TP

        def psum_out(slot):
            return pj[:, slot, :, 0:HALF]

        U_HIN = 0
        U_HOUT = U_HIN + 4 * H
        U_MLP0 = U_HOUT + KT
        U_AB = U_MLP0 + 2 * KT * NGRP
        U_GIN = U_AB + 1
        U_GOUT = U_GIN + 4 * H
        U_MLP1 = U_GOUT + KT
        U_END = U_MLP1 + 2 * KT * NGRP

        def unit_done(u):
            return u + 3

        block = ctx.enter_context(nc.Block())

        @block.sync
        def _(sp):
            c = 16
            sp.dma_start(cf[:], const_f).then_inc(c_in, c)
            for stage_, part in zip(cstage, (const_u[:, 0:CU_HALF], const_u[:, CU_HALF:2 * CU_HALF])):
                sp.dma_start(stage_, part).then_inc(c_in, c)
            rows = xp[:, 0, :]
            for src, r, n in ((norm_mix, V_MIX, 16), (norm_mlp, V_MLP, 16)):
                sp.dma_start(rows[r:r + n, 0:P], src.rearrange("d (k p) -> (d k) p", p=P)).then_inc(c_in, c)
            sp.dma_start(rows[V_FIN:V_FIN + 8, 0:P], norm_final.rearrange("(k p) -> k p", p=P)).then_inc(c_in, c)
            sp.dma_start(rows[V_LB:V_LB + 8, 0:P], hgrn_lb.rearrange("d (k p) -> (d k) p", p=P)).then_inc(c_in, c)
            sp.dma_start(rows[V_HON:V_HON + 1, 0:P], hgrn_out_norm).then_inc(c_in, c)
            sp.dma_start(rows[V_GON:V_GON + 1, 0:P], gdn_out_norm).then_inc(c_in, c)
            sp.dma_start(xp[0:CONV * 3 * H, 1, 0:P],
                         gdn_conv_w[0].rearrange("j (s p) -> (j s) p", p=P)).then_inc(c_in, c)
            sp.dma_start(gsc[:, 0:1], gdn_A_log.rearrange("a h -> h a")).then_inc(c_in, c)
            sp.dma_start(gsc[:, 1:2], gdn_dt_bias.rearrange("a h -> h a")).then_inc(c_in, c)

            xs = stage("x", "x")[2]
            for n in range(NC):
                if n >= 2:
                    sp.wait_ge(xs.sem, n - 1)
                sp.dma_start(xrow[n % 2], x_prompt[0, n * P:(n + 1) * P, :]).then_inc(x_in[n % 2], 16)
            sp.wait_ge(xs.sem, NC - 1)
            sp.dma_start(xrow[0][0:TS], x_sample.rearrange("b t d -> (b t) d")).then_inc(x_in[0], 16)

            def load(U, r, j, src):
                slot = (U + j) % RAW
                if not isinstance(r, int) or r + U + j >= RAW:
                    free = fixed(sp, r * 2 + (2 * (U + j) - 6))
                    sp.wait_ge(x_in[0], 16)
                    sp.wait_ge(w_split, free)
                sp.dma_start(w_raw[:, slot], src).then_inc(w_in[slot], 16)

            hin = hgrn_w_in[0].rearrange("(k p) n -> p k n", p=P)
            gin = gdn_w_in[0].rearrange("(k p) n -> p k n", p=P)
            for j in range(4):
                load(U_HIN, 0, j, hin[:, :, HGRN_ORDER[j] * D:HGRN_ORDER[j] * D + P])
            with sp.Fori(1, H) as h:
                for j in range(4):
                    load(U_HIN, h * 4, j, hin[:, :, ds(h * P + HGRN_ORDER[j] * D, P)])

            def out_proj(U, w):
                view = w[0].rearrange("(k p) n -> p k n", p=P)
                with sp.Fori(0, 2) as i:
                    for j in range(4):
                        load(U, i * 4, j, view[:, :, ds(i * (4 * P) + j * P, P)])

            def mlp(layer, U):
                up = mlp_w_up[layer].rearrange("(k p) n -> p k n", p=P)
                down = mlp_w_down[layer].rearrange("(g k p) n -> p g k n", p=P, k=KT)
                with sp.Fori(0, NGRP) as g:
                    for j in range(KT):
                        load(U, g * (2 * KT), j, up[:, :, ds(g * D + j * P, P)])
                    for j in range(KT):
                        load(U, g * (2 * KT), KT + j,
                             down[:, ds(g, 1), :, j * P:(j + 1) * P].rearrange("p o k n -> p (o k) n"))

            out_proj(U_HOUT, hgrn_w_out)
            mlp(0, U_MLP0)
            slot = U_AB % RAW
            sp.wait_ge(w_split, 2 * U_AB - 6)
            with nc.allow_non_contiguous_dma(reason="16 columns"):
                for n in range(2):
                    sp.dma_start(w_raw[:, slot, :, 32 * n:32 * n + H],
                                 gin[:, :, 4 * D + n * H:4 * D + (n + 1) * H]).then_inc(w_in[slot], 16)
            with sp.Fori(0, H) as h:
                for j in range(4):
                    load(U_GIN, h * 4, j, gin[:, :, ds(h * P + GDN_ORDER[j] * D, P)])
            out_proj(U_GOUT, gdn_w_out)
            mlp(1, U_MLP1)

        @block.gpsimd
        def _(pool):
            nc.gpsimd.memset(ones[:], 1.0).then_inc(ones_set, 1)

            def split(n, j, extra=0):
                u, s = n * 4 + j, j % SPLIT
                loaded, free = fixed(pool, n * 16 + (16 + extra)), fixed(pool, u - 1)
                pool.wait_ge(ones_set, 1)
                pool.wait_ge(w_in[j], loaded)
                if not (isinstance(n, int) and u < SPLIT):
                    pool.wait_ge(w_used, free)
                nc.gpsimd.tensor_scalar(w_hi[:, s], w_raw[:, j], 1.0, 1.0, ALU.mult, ALU.mult).then_inc(w_split, 1)
                pool.wait_ge(w_split, u * 2 + 1)
                nc.gpsimd.tensor_tensor(w_lo[:, s], w_raw[:, j], w_hi[:, s], ALU.subtract).then_inc(w_split, 1)

            for j in range(RAW):
                split(0, j)
            with pool.Fori(1, U_AB // 4) as n:
                for j in range(RAW):
                    split(n, j)
            ab = U_AB % RAW
            with pool.Fori(U_AB // 4, U_END // 4) as n:
                for j in range(RAW):
                    split(n, j, 16 if j == ab else 0)
            for j in range(U_END % 4):
                split(U_END // 4, j, 16 if j == ab else 0)

        @block.tensor
        def _(pe):
            mm = nc.tensor.matmul

            def tiles(U, r, j, hi, lo, k0, k1, k_ready=None):
                u, s = r + (U + j), (U + j) % SPLIT
                if k0 == 0:
                    pe.wait_ge(w_split, u * 2 + 2)
                    pe.wait_ge(unit_out, u + 1)
                for k in range(k0, k1):
                    if k_ready:
                        k_ready(k)
                    for a, (w, v) in enumerate(((w_hi, hi), (w_hi, lo), (w_lo, hi))):
                        for b in range(2):
                            last = mm(pj[:, s, b, 0:HALF], w[:, s, k, :], v[:, k, b * HALF:(b + 1) * HALF],
                                      start=(k == 0 and a == 0), stop=(k == KT - 1 and a == 2))
                if k1 == KT:
                    last.then_inc(w_used, 1)

            def unit(U, r, j, hi, lo, k_ready=None):
                tiles(U, r, j, hi, lo, 0, KT, k_ready)

            def head_projections(U, h, first=0, end=4):
                done = [first * KT]

                def more(n):
                    for i in range(done[0], min(done[0] + n, end * KT)):
                        tiles(U, h * 4, i // KT, xh, xl, i % KT, i % KT + 1)
                    done[0] += n
                return more

            def sum_features(bank, src, start=True, stop=True):
                for b in range(2):
                    last = mm(rr[:, bank + b, 0:HALF], ones[:], src[:, b * HALF:(b + 1) * HALF], start=start, stop=stop)
                return last

            def norm(key):
                v, _, t = st[key]
                pe.wait_ge(v.sem, v.after(f"acc{KT - 1}", 0))
                t.did(sum_features(0, acc), "sum")

            def first_unit(U, key):
                tiles(U, 0, 0, xh, xl, 0, KT - 1, wait_norm(key))
                norm(key)
                tiles(U, 0, 0, xh, xl, KT - 1, KT, wait_norm(key))

            def tr(out, in_):
                n = in_.shape[0]
                return nc.tensor.transpose(out, in_, cf[0:n, C_EYE:C_EYE + n])

            v, s, t = st["init"]
            pe.wait_ge(c_in, 16 * N_CONST)
            pe.wait_ge(ones_set, 1)
            pe.wait_ge(v.sem, v.after("fill", 0))
            tr(rr[:, 0, 0:V_N], xp[0:V_N, 0, 0:P])
            t.did(tr(rr[:, 1, 0:CONV * 3 * H], xp[0:CONV * 3 * H, 1, 0:P]), "vec")

            v, s, t = st["x"]
            for i in range(NC):
                pe.wait_ge(x_in[i % 2], 16 * (i // 2 + 1))
                if i:
                    pe.wait_ge(v.sem, v.after("copy", i - 1))
                for k in range(KT):
                    last = tr(rr[:, 2 + k // 4, (k % 4) * P:(k % 4 + 1) * P], xrow[i % 2][:, k * P:(k + 1) * P])
                t.did(last, "t")
            pe.wait_ge(x_in[0], 16 * (NC // 2 + 1))
            pe.wait_ge(v.sem, v.after("copy", NC - 1))
            for k in range(KT):
                last = tr(rr[:, 2, k * TS:(k + 1) * TS], xrow[0][0:TS, k * P:(k + 1) * P])
            st["xs"][2].did(last, "t")

            def wait_norm(key):
                v = st[key][0]
                return lambda k: pe.wait_ge(v.sem, v.after(f"lo{k}", 0))

            def output_projections(U, key):
                v, done = st[key][0], [0]

                def more(n):
                    if done[0] == 0:
                        pe.wait_ge(v.sem, v.after("lo", H - 2))
                    for i in range(done[0], min(done[0] + n, 2 * (H - 1))):
                        j, k = divmod(i, H - 1)
                        tiles(U, 0, j, oh, ol, k, k + 1)
                    done[0] += n
                return more

            def hgrn_rec(h, more):
                (v, s, t), va = st["hr"], st["ha"][0]
                Q, K, val, qe, kd, A, KL, vT, kdT = (hg[n] for n in ("Q", "K", "val", "qe", "kd", "A", "KL", "vT", "kdT"))

                def level(n, tiles):
                    m = LEVELS[n]
                    more(tiles)
                    pe.wait_ge(v.sem, v.after(f"kl{m}", h))
                    if n >= 2:
                        pe.wait_ge(v.sem, v.after(f"pred{LEVELS[n - 2]}", h))
                    for c in range(NC):
                        last = mm(rr[:, n % 2, c * 64:(c + 1) * 64], KL[:, n % 2, c * P:(c + 1) * P],
                                  QL[:, n % 2, c * 64:(c + 1) * 64], start=True, stop=True)
                    if m in SLEVELS:
                        last = mm(rr[0:TS, n % 2, TP // 2:T // 2], KL[:, n % 2, TP:T], QL[:, n % 2, TP // 2:T // 2],
                                  start=True, stop=True)
                    t.did(last, f"lv{m}")

                pe.wait_ge(va.sem, va.after("K", h))
                pe.wait_ge(st["ha"][1].sem, st["ha"][1].after("ebd", h))
                for c in range(NC):
                    cols = slice(c * P, (c + 1) * P)
                    mm(rr[:, 2, cols], K[:, cols], Q[:, cols], start=True, stop=True)
                t.did(mm(rr[0:TS, 3, 0:TS], K[:, TP:T], Q[:, TP:T], start=True, stop=True), "diag")
                level(0, 6)
                level(1, 3)
                pe.wait_ge(v.sem, v.after("adiag", h))
                for c in range(NC):
                    last = tr(rr[:, 2, c * P:(c + 1) * P], val[:, c * P:(c + 1) * P])
                t.did(last, "vT")
                for c in range(NC):
                    last = tr(rr[:, 3, c * P:(c + 1) * P], kd[:, c * P:(c + 1) * P])
                t.did(last, "kdT")
                level(2, 3)
                taken = fixed(pe, s.after("vT", h))
                pe.wait_ge(c_in, 16 * N_CONST)
                pe.wait_ge(s.sem, taken)
                tr(rr[0:TS, 2, 0:P], val[:, TP:T])
                t.did(tr(rr[0:TS, 2, P:2 * P], kd[:, TP:T]), "smp")
                level(3, 3)
                pe.wait_ge(s.sem, s.after("kdTs", h))
                for c in range(NC):
                    last = mm(rr[:, 2, c * P:(c + 1) * P], kdT[:, c * P:(c + 1) * P], vT[:, c * P:(c + 1) * P],
                              start=True, stop=True)
                t.did(last, "dS")
                level(4, 3)
                pe.wait_ge(st_in, h * 16 + 16)
                mm(rr[:, 3, 0:TS], vTs[:], A[0:TS, TP:T], start=True, stop=False)
                for b in range(NSEQ):
                    last = mm(rr[:, 3, b * SLEN:(b + 1) * SLEN], S0[:, b, :],
                              qe[:, TP + b * SLEN:TP + (b + 1) * SLEN], start=False, stop=(b == NSEQ - 1))
                t.did(last, "os")
                level(5, 3)
                pe.wait_ge(v.sem, v.after("vbig", h))
                pe.wait_ge(s.sem, s.after("os", h))
                for a in range(2):
                    last = mm(rr[:, 2 + a, :], kdTs[:], hg["vbig"][0:TS, a, 0:4 * P], start=True, stop=True)
                t.did(last, "dSs")
                level(6, 3)
                more(3)
                pe.wait_ge(v.sem, v.after("pred64", h))
                for c in range(NC):
                    cols = slice(c * P, (c + 1) * P)
                    last = mm(rr[:, 1, cols], vT[:, cols], A[:, cols], start=True, stop=(c == 0))
                    if c:
                        last = mm(rr[:, 1, cols], Sp[:, c - 1, :], qe[:, cols], start=False, stop=True)
                t.did(last, "o")
                more(2)
                pe.wait_ge(s.sem, s.after("sq", h))
                t.did(sum_features(2, hg["sq"]), "ss")
                more(3)

            def gdn_pre():
                v, s, t = st["gp"]
                pe.wait_ge(v.sem, v.after("dl", 0))
                pe.wait_ge(s.sem, s.after("eg", 0))
                for c in range(NC):
                    tr(rr[:, 2, c * P:(c + 1) * P], gt4[:, c * P:(c + 1) * P])
                t.did(tr(rr[0:TS, 3, 0:P], gt4[:, TP:T]), "cols")

            def held(*waits):
                values = [(steps.sem, fixed(pe, steps.after(name, h))) for steps, name, h in waits]
                pe.wait_ge(c_in, 16 * N_CONST)
                for sem_, value in values:
                    pe.wait_ge(sem_, value)

            def gdn_prepare(slot, h):
                v, s, t = st["ga"]
                nQ, nK, work = gd["nQ"], gd["nK"], gd["work"]
                if slot == "L1":
                    loaded = fixed(pe, h * 16 + 16)
                    pe.wait_ge(c_in, 16 * N_CONST)
                    pe.wait_ge(cv_in, loaded)
                    for g in range(3):
                        last = tr(rr[:, 3, SVN + g * 32:SVN + g * 32 + XW * NSEQ], cin[:, g, :])
                    t.did(last, "cin")
                if slot in ("L3", "L4"):
                    g, name = (0, "gb") if slot == "L3" else (1, "bb")
                    pe.wait_ge(s.sem, s.after("G" if g else "hist", h))
                    pe.wait_ge(v.sem, v.after("gsel", h))
                    for b in range(2):
                        last = mm(rr[:, 2 + b, 0:HALF], cf[:, C_IND + g * P:C_IND + (g + 1) * P],
                                  work[:, b * HALF:(b + 1) * HALF], start=True, stop=True)
                    t.did(last, name)
                if slot == "L5":
                    pe.wait_ge(s.sem, s.after("sqk", h))
                    t.did(sum_features(2, work), "ssk")
                if slot == "L6":
                    pe.wait_ge(v.sem, v.after("kb", h))
                    for c in range(NC):
                        cols = slice(c * P, (c + 1) * P)
                        mm(rr[:, 2 + c // 2, c % 2 * P:(c % 2 + 1) * P], nK[:, cols], work[:, cols], start=True, stop=True)
                    t.did(mm(rr[0:TS, 2, 2 * P:2 * P + TS], nK[:, TP:T], work[:, TP:T], start=True, stop=True), "kk")
                if slot == "C0":
                    pe.wait_ge(s.sem, s.after("sqq", h))
                    pe.wait_ge(v.sem, v.after("kkd", h))
                    t.did(sum_features(2, gd["G"]), "ssq")
                if slot == "C1":
                    pe.wait_ge(v.sem, v.after("qn", h))
                    for c in range(NC):
                        cols = slice(c * P, (c + 1) * P)
                        mm(rr[:, 2 + c // 2, c % 2 * P:(c % 2 + 1) * P], nK[:, cols], nQ[:, cols], start=True, stop=True)
                    t.did(mm(rr[0:TS, 3, 2 * P:2 * P + TS], nK[:, TP:T], nQ[:, TP:T], start=True, stop=True), "qk")
                if slot == "C2":
                    held((v, "qkd", h))
                    for g in range(3):
                        n = XW * (NSEQ + 1)
                        last = tr(rr[0:n, 2 + g // 2, g % 2 * P:(g % 2 + 1) * P], cstash[:, g, :])
                    t.did(last, "stash")

            def gdn_first_inverse(h, *bank_left):
                v, s, t = st["ga"]
                Tt = gd["Tt"]
                pe.wait_ge(v.sem, v.after("tt1", h))
                for c in range(NC):
                    cols = slice(c * P, (c + 1) * P)
                    tr(rr[:, 1, cols], Tt[:, cols])
                held((v, "tt1", h), *bank_left)
                t.did(tr(rr[0:TS, 2, 0:TS], Tt[0:TS, TP:T]), "t0")

            def gdn_finish(h):
                _, s, t = st["gf"]
                pe.wait_ge(st["gr"][1].sem, st["gr"][1].after("sq", h))
                t.did(sum_features(2, gd["sq"]), "ss")

            def gdn_rec(h, prev, nxt, more, later):
                (v, s, t), (va, sa, ta) = st["gr"], st["ga"]
                K, qe, A, NL, Tm, Tt, X, kdT, vT, VN = (gd[n] for n in ("K", "qe", "A", "NL", "Tm", "Tt", "X", "kdT",
                                                                        "vT", "VN"))

                for n, m in enumerate(LEVELS[1:]):
                    smp = m in SLEVELS
                    if n == 0:
                        pe.wait_ge(sa.sem, sa.after("tm0", h))
                        pe.wait_ge(va.sem, va.after("A", h))
                        if prev is not None:
                            gdn_finish(prev)
                    else:
                        pe.wait_ge(s.sem, s.after(f"tt{LEVELS[n]}", h))
                    for c in range(NC):
                        cols = slice(c * P, (c + 1) * P)
                        last = mm(rr[:, 0, c * 64:(c + 1) * 64], NL[:, cols], first_half(Tm[:, cols], m),
                                  start=True, stop=True)
                    if smp:
                        last = mm(rr[0:TS, 1, 0:TS // 2], NL[0:TS, TP:T], first_half(Tm[0:TS, TP:T], m),
                                  start=True, stop=True)
                    t.did(last, f"x{m}")
                    if m == 8:
                        pe.wait_ge(st_in, h * 16 + 16 * (H + 1))
                        for b in range(NSEQ):
                            last = mm(rr[:, 1, b * SLEN:(b + 1) * SLEN], S0[:, b, :],
                                      K[:, TP + b * SLEN:TP + (b + 1) * SLEN], start=True, stop=True)
                        t.did(last, "sks")
                    if m == 64:
                        pe.wait_ge(s.sem, s.after("vns", h))
                        mm(rr[:, 1, 0:TS], X[0:TS, VNS:VNS + P], A[0:TS, TP:T], start=True, stop=False)
                        for b in range(NSEQ):
                            last = mm(rr[:, 1, b * SLEN:(b + 1) * SLEN], S0[:, b, :],
                                      qe[:, TP + b * SLEN:TP + (b + 1) * SLEN], start=False, stop=(b == NSEQ - 1))
                        t.did(last, "os")
                    more(2)
                    if m == LEVELS[-1]:
                        break
                    pe.wait_ge(s.sem, s.after(f"x{m}", h))
                    for c in range(NC):
                        last = mm(rr[:, 0, 256 + c * 64:256 + (c + 1) * 64], Tt[:, c * P:(c + 1) * P],
                                  X[:, c * 64:(c + 1) * 64], start=True, stop=True)
                    if smp:
                        last = mm(rr[0:TS, 1, TS // 2:TS], Tt[0:TS, TP:T], X[0:TS, TP // 2:T // 2],
                                  start=True, stop=True)
                    t.did(last, f"dt{m}")
                    more(1)
                    pe.wait_ge(v.sem, v.after(f"pred{m}", h))
                    for c in range(NC):
                        cols = slice(c * P, (c + 1) * P)
                        last = tr(rr[:, 1, cols], Tm[:, cols])
                    if smp:
                        last = tr(rr[0:TS, 0, 0:TS], Tm[0:TS, TP:T])
                    t.did(last, f"tr{m}")
                    if m == 2:
                        if prev is not None:
                            pe.wait_ge(st["gf"][1].sem, st["gf"][1].after("ln", prev))
                        for c in range(NC):
                            last = tr(rr[:, 2 + c // 2, c % 2 * P:(c % 2 + 1) * P], gd["nV"][:, c * P:(c + 1) * P])
                        t.did(last, "vT")
                    if m == 4:
                        pe.wait_ge(v.sem, v.after("vb", h))
                        if nxt is not None:
                            pe.wait_ge(sa.sem, sa.after("hist", nxt))
                        for c in range(NC):
                            tr(rr[:, 2 + c // 2, c % 2 * P:(c % 2 + 1) * P], K[:, c * P:(c + 1) * P])
                        t.did(tr(rr[0:TS, 2, SRT:SRT + P], K[:, TP:T]), "kT")
                    if m == 8:
                        pe.wait_ge(v.sem, v.after("kdts", h))
                    if m == 16:
                        held((v, "sr3", h), *([] if nxt is None else [(sa, "G", nxt)]))
                        t.did(tr(rr[0:TS, 2, SRT:SRT + P], rt[:]), "srt")
                    if m == 32:
                        held((s, "rs", h), *([] if nxt is None else [(sa, "bb", nxt)]))
                        t.did(mm(rr[0:TS, 3, SVN:SVN + P], Tt[0:TS, TP:T], X[0:TS, RS:RS + P], start=True, stop=True), "svn")
                    if nxt is not None:
                        if m == 2:
                            pe.wait_ge(v.sem, v.after("vb", h))
                        gdn_prepare(f"L{n + 1}", nxt)
                held((s, "x64", h))
                for c in range(NC):
                    last = mm(rr[0:m, 0, 256 + c * m:256 + (c + 1) * m], X[:, c * m:(c + 1) * m],
                              Tt[:, c * P + m:(c + 1) * P], start=True, stop=True)
                t.did(last, "dt64")
                if nxt is not None:
                    gdn_prepare("L6", nxt)
                pe.wait_ge(v.sem, v.after("pred64", h))
                for c in range(NC):
                    cols = slice(c * P, (c + 1) * P)
                    later(1)
                    if c:
                        pe.wait_ge(v.sem, v.after(f"S{c - 1}", h))
                        t.did(mm(rr[:, 0, 0:P], K[:, cols], Sp[:, c - 1, :], start=True, stop=True), f"ks{c}")
                        later(1)
                        pe.wait_ge(v.sem, v.after(f"r{c}", h))
                    t.did(mm(rr[:, 0, P:2 * P], Tt[:, cols], vT[:, cols], start=True, stop=True), f"vn{c}")
                    later(1)
                    pe.wait_ge(s.sem, s.after(f"vn{c}", h))
                    t.did(mm(rr[:, 0, 2 * P:3 * P], kdT[:, cols], VN[:, cols], start=True, stop=True), f"dS{c}")
                    last = mm(rr[:, 1, cols], VN[:, cols], A[:, cols], start=True, stop=(c == 0))
                    if c:
                        last = mm(rr[:, 1, cols], Sp[:, c - 1, :], qe[:, cols], start=False, stop=True)
                    if c == NC - 1:
                        t.did(last, "o")
                    if nxt is not None:
                        gdn_prepare(f"C{c}", nxt)
                pe.wait_ge(v.sem, v.after("S3", h))
                t.did(mm(rr[:, 0, :], kdTs[:], gd_vbig[0], start=True, stop=True), "dSs0")
                later(2)
                if nxt is not None:
                    pe.wait_ge(s.sem, s.after("oo", h))
                    gdn_first_inverse(nxt, (sa, "cout", nxt))
                pe.wait_ge(v.sem, v.after("sn0", h))
                t.did(mm(rr[:, 0, :], kdTs[:], gd_vbig[1], start=True, stop=True), "dSs1")
                later(3)
            def out_proj(U, key):
                v = st[key][0]
                pe.wait_ge(v.sem, v.after("lo", H - 1))
                for j in range(2):
                    tiles(U, 0, j, oh, ol, H - 1, H)
                for j in range(2, KT):
                    unit(U, 0, j, oh, ol)

            def mlp(U, nkey, ukey):
                v = st[ukey][0]

                def group(g):
                    for j in range(KT):
                        if j == 0 and isinstance(g, int):
                            first_unit(U, nkey)
                        else:
                            unit(U, g * (2 * KT), j, xh, xl)
                    for j in range(KT):
                        unit(U, g * (2 * KT), KT + j, oh, ol,
                             (lambda k: pe.wait_ge(v.sem, v.after(f"lo{k}", g))) if j == 0 else None)

                group(0)
                with pe.Fori(1, NGRP) as g:
                    group(g)

            first_unit(U_HIN, "n0")
            for j in range(1, 4):
                unit(U_HIN, 0, j, xh, xl)
            with pe.Fori(0, H - 1) as h:
                hgrn_rec(h, head_projections(U_HIN, h + 1))
            hgrn_rec(H - 1, output_projections(U_HOUT, "hr"))
            out_proj(U_HOUT, "hr")
            mlp(U_MLP0, "n1", "up0")
            first_unit(U_AB, "n2")
            gdn_pre()
            more = head_projections(U_GIN, 0)
            pe.wait_ge(st["gp"][1].sem, st["gp"][1].after("cols", 0))
            for slot in GDN_SLOTS:
                more(16 if slot == "L0" else 2)
                gdn_prepare(slot, 0)
            gdn_first_inverse(0, (st["ga"][1], "cout", 0))
            head_projections(U_GIN, 1, 0, 2)(2 * KT)
            gdn_rec(0, None, 1, head_projections(U_GIN, 1, 2, 4), head_projections(U_GIN, 2, 0, 2))
            with pe.Fori(1, H - 2) as h:
                gdn_rec(h, h - 1, h + 1, head_projections(U_GIN, h + 1, 2, 4), head_projections(U_GIN, h + 2, 0, 2))
            gdn_rec(H - 2, H - 3, H - 1, head_projections(U_GIN, H - 1, 2, 4), lambda n: None)
            gdn_rec(H - 1, H - 2, None, lambda n: None, output_projections(U_GOUT, "gf"))
            gdn_finish(H - 1)
            out_proj(U_GOUT, "gf")
            mlp(U_MLP1, "n3", "up1")
            norm("n4")
            v, s, t = st["y"]
            for i in range(NC):
                pe.wait_ge(v.sem, v.after("y", i))
                if i:
                    pe.wait_ge(s.sem, s.after("e", i - 1))
                for k in range(KT):
                    last = tr(rr[:, 2 + k // 4, (k % 4) * P:(k % 4 + 1) * P], ycol[i % 2][:, k * P:(k + 1) * P])
                t.did(last, "t")
            v2, s2, t2 = st["ys"]
            pe.wait_ge(v2.sem, v2.after("y", 0))
            pe.wait_ge(s.sem, s.after("e", NC - 1))
            for k in range(KT):
                last = tr(rr[0:TS, 2 + k // 4, (k % 4) * P:(k % 4 + 1) * P], ycol[NC % 2][:, k * P:k * P + TS])
            t2.did(last, "t")

        @block.scalar
        def _(act):
            f = nc.scalar.activation
            nc.scalar.preload_act_table_set("natural_log_exp_and_others")
            sem_of = lambda steps, name, i: act.wait_ge(steps.sem, steps.after(name, i))

            v, s, t = st["init"]
            sem_of(v, "lb1", 0)
            s.did(f(lbt[:, 3], lbt[:, 3], ACT.Exp), "lb1")
            sem_of(v, "lb5", 0)
            s.did(f(lbt[:, 1], lbt[:, 1], ACT.Ln, scale=LN_SHIFT), "lb2")
            s.did(f(lbt[:, 2], lbt[:, 0], ACT.Ln), "lb3")

            def norm(key, u):
                v, s, t = st[key]
                if u is None:
                    act.wait_ge(st["xs"][0].sem, 1)
                for k in range(KT):
                    if u is not None:
                        act.wait_ge(unit_out, unit_done(u + k))
                    if k >= 2:
                        sem_of(v, f"acc{k - 2}", 0)
                    s.did(f(sq[:, k % 2], xT[:, k], ACT.Square), f"sq{k}")
                sem_of(t, "sum", 0)
                s.did(f(halves(rstd[:]), rr[:, 0:2, 0:HALF], ACT.Ln, bias=epsc[:, 0:1], scale=1.0 / D), "ln")
                sem_of(s, "ln", 0)
                s.did(f(rstd[:], rstd[:], ACT.Exp, scale=-0.5), "rstd")

            def load_state(src, h):
                act.dma_start(S0[:], src[0, :, ds(h, 1)].rearrange("b o k v -> k (o b) v")).then_inc(st_in, 16)

            def store_states(dst_p, dst_s, h):
                act.dma_start(dst_p[0, 0, ds(h, 1)].rearrange("o k v -> k (o v)"), Sp[:, NC - 1]).then_inc(st_out, 16)
                act.dma_start(dst_s[0, :, ds(h, 1)].rearrange("b o k v -> k (o b) v"), S0[:]).then_inc(st_out, 16)

            def hgrn_prepare(slot, h):
                v, s, t = st["ha"]
                T1 = xp[:, 0, XW:XW + T]
                if slot == 3:
                    sem_of(v, "fneg", h)
                    s.did(f(ng[:, 1, 0:T], ng[:, 1, 0:T], ACT.Exp), "fexp")
                    sem_of(s, "fexp", h)
                    s.did(f(ng[:, 1, 0:T], ng[:, 1, 0:T], ACT.Ln, bias=1.0), "fln")
                if slot == 4:
                    sem_of(v, "nabs", h)
                    s.did(f(pr[:, 1, 0:T], pr[:, 1, 0:T], ACT.Exp), "kexp")
                    s.did(f(T1, T1, ACT.Exp), "cexp")
                    sem_of(s, "cexp", h)
                    s.did(f(T1, T1, ACT.Ln, bias=1.0), "cln")
                if slot == 5:
                    sem_of(v, "qneg", h)
                    s.did(f(ng[:, 0, 0:T], ng[:, 0, 0:T], ACT.Exp), "qexp")
                    sem_of(s, "qexp", h)
                    s.did(f(ng[:, 0, 0:T], ng[:, 0, 0:T], ACT.Ln, bias=1.0), "qln")
                if slot == 6:
                    sem_of(v, "qls", h)
                    s.did(f(ng[:, 0, 0:T], ng[:, 0, 0:T], ACT.Exp), "qsig")
                if slot == 7:
                    sem_of(v, "gneg", h)
                    s.did(f(ng[:, 2, 0:T], ng[:, 2, 0:T], ACT.Exp), "gexp")
                    sem_of(s, "gexp", h)
                    s.did(f(ng[:, 2, 0:T], ng[:, 2, 0:T], ACT.Ln, bias=1.0), "gln")
                if slot == 8:
                    sem_of(v, "gls", h)
                    s.did(f(ng[:, 2, 0:T], ng[:, 2, 0:T], ACT.Exp), "gsig")
                if slot == 9:
                    sem_of(v, "bd", h)
                    f(hg["eb"], hg["b"], ACT.Exp)
                    s.did(f(hg["bd"], hg["bd"], ACT.Exp), "ebd")

            def hgrn_head(h, nxt):
                v, s, t = st["hr"]
                dd, oo, vT, kdT, sqr = hg["dd"], hg["oo"], hg["vT"], hg["kdT"], hg["sq"]
                for n, m in enumerate(LEVELS):
                    sem_of(v, f"d{m}", h)
                    s.did(f(dd[:, n % 2, 0:width(m)], dd[:, n % 2, 0:width(m)], ACT.Exp), f"e{m}")
                    if m == 4:
                        sem_of(t, "vT", h)
                        s.did(f(vT[:, 0:TP], rr[:, 2, :], ACT.Copy), "vT")
                        sem_of(t, "kdT", h)
                        s.did(f(kdT[:, 0:TP], rr[:, 3, :], ACT.Copy), "kdT")
                    if m == 8:
                        sem_of(t, "smp", h)
                        f(vTs[:], rr[0:TS, 2, 0:P], ACT.Copy)
                        s.did(f(kdTs[:], rr[0:TS, 2, P:2 * P], ACT.Copy), "kdTs")
                    if m == 32:
                        sem_of(t, "os", h)
                        s.did(f(oo[:, TP:T], rr[:, 3, 0:TS], ACT.Copy), "os")
                    if nxt is not None:
                        hgrn_prepare(n, nxt)
                if nxt is not None:
                    hgrn_prepare(7, nxt)
                sem_of(t, "o", h)
                s.did(f(oo[:, 0:TP], rr[:, 1, :], ACT.Copy), "oo")
                sem_of(s, "oo", h)
                s.did(f(sqr, oo, ACT.Square), "sq")
                sem_of(v, "snew", h)
                store_states(hgrn_p, hgrn_s, h)
                if nxt is not None:
                    hgrn_prepare(8, nxt)
                sem_of(t, "ss", h)
                s.did(f(halves(sqr), rr[:, 2:4, 0:HALF], ACT.Ln, bias=epsc[:, 0:1], scale=1.0 / P), "ln")
                sem_of(s, "ln", h)
                s.did(f(sqr, sqr, ACT.Exp, scale=-0.5), "rn")
                if nxt is not None:
                    hgrn_prepare(9, nxt)
                sem_of(v, "og", h)
                s.did(f(oh[:, ds(h, 1)].rearrange("p o n -> p (o n)"), oo, ACT.Copy), "hi")
                if nxt is not None:
                    act.wait_ge(st_out, h * 32 + 32)
                    load_state(state_hgrn, nxt)

            def gdn_pre():
                v, s, t = st["gp"]
                act.wait_ge(c_in, 16 * N_CONST)
                s.did(f(gsc[0:H, 2:3], gsc[0:H, 0:1], ACT.Exp), "A")
                sem_of(v, "neg", 0)
                s.did(f(B[0:64, 1], B[0:64, 1], ACT.Exp), "exp")
                sem_of(s, "exp", 0)
                s.did(f(B[0:64, 1], B[0:64, 1], ACT.Ln, bias=1.0), "ln")
                sem_of(v, "ls", 0)
                s.did(f(gt4[32:64], B[32:64, 2], ACT.Exp), "be")
                sem_of(v, "dl", 0)
                s.did(f(gt4[64:64 + H], B[0:H, 3], ACT.Exp), "el")
                s.did(f(gt4[96:96 + H], gt4[0:H], ACT.Exp), "eg")
                sem_of(t, "cols", 0)
                f(gcol[:, 0:NC].rearrange("p c (r x) -> p (c r) x", x=H), blocks(rr[:, 2, :], 32)[:, :, 0:H], ACT.Copy)
                s.did(f(blocks(gcol[0:TS, NC], H), blocks(rr[0:TS, 3, 0:P], 32)[:, :, 0:H], ACT.Copy), "cols")

            def sample_rows(slot):
                return blocks(xp[:, slot, SB0:XPW], SROW)

            def put_history(slot, g):
                return f(sample_rows(slot)[:, :, 0:XW], blocks(hist[:, g, :], XW), ACT.Copy)

            def first_tap(name, slot, g, h, past="past"):
                v, s, t = st["ga"]
                sem_of(s, past, h)
                act.wait_ge(unit_out, (h * 4 + (U_GIN + GDN_ORDER.index(g))) + 3)
                f(cstash[:, g, 0:XW], xp[:, slot, TP:TP + XW], ACT.Copy)
                f(blocks(cstash[:, g, XW:], XW), sample_rows(slot)[:, :, SLEN:SROW], ACT.Copy)
                s.did(f(pr[:, slot, 0:YW], xp[:, slot, 0:YW], ACT.Copy, scale=hcw[:, 0, g:g + 1]), name)

            def soft(row, w, exp, ln):
                s = st["ga"][1]
                s.did(f(ng[:, row, 0:w], ng[:, row, 0:w], ACT.Exp), exp[0])
                sem_of(s, *exp)
                s.did(f(ng[:, row, 0:w], ng[:, row, 0:w], ACT.Ln, bias=1.0), ln)

            def norm_scale(row, ln, rn, h):
                s = st["ga"][1]
                s.did(f(halves(row), rr[:, 2:4, 0:HALF], ACT.Ln, bias=epsc[:, 0:1]), ln)
                sem_of(s, ln, h)
                s.did(f(row, row, ACT.Exp, scale=-0.5), rn)

            def gdn_prepare(slot, h):
                v, s, t = st["ga"]
                work, G, dec = gd["work"], gd["G"], gd["dec"]
                if slot == "L1":
                    sem_of(t, "cin", h)
                    last = f(hist[:], rr[:, 3, SVN:SVN + 96].rearrange("p (g x) -> p g x", g=3)[:, :, 0:XW * NSEQ], ACT.Copy)
                    s.did(last, "hist")
                    if not (isinstance(h, int) and h == H - 1):
                        load_conv(h + 1)
                    sem_of(s, "hist", h)
                    for slot_, g in enumerate(GDN_ORDER[0:2]):
                        last = put_history(slot_, g)
                    s.did(last, "past")
                if slot == "L2x":
                    sem_of(v, "cols", h)
                    first_tap("ktap", 0, K_ROW, h)
                if slot == "L3x":
                    first_tap("qtap", 1, Q_ROW, h)
                    sem_of(v, "k3", h)
                    s.did(put_history(0, V_ROW), "vhist")
                if slot == "L3":
                    sem_of(v, "kneg", h)
                    soft(0, YW, ("kexp", h), "kln")
                if slot == "L4x":
                    sem_of(t, "gb", h)
                    s.did(f(halves(G), rr[:, 2:4, 0:HALF], ACT.Copy), "G")
                if slot == "L4":
                    sem_of(v, "kls", h)
                    s.did(f(ng[:, 0, 0:YW], ng[:, 0, 0:YW], ACT.Exp), "ksig")
                    sem_of(v, "qneg", h)
                    soft(1, YW, ("qexp", h), "qln")
                if slot == "L5x":
                    sem_of(t, "bb", h)
                    s.did(f(halves(gd["beta"]), rr[:, 2:4, 0:HALF], ACT.Copy), "bb")
                    sem_of(v, "dec", h)
                    f(dec[:, 0:TP], dec[:, 0:TP], ACT.Exp)
                    s.did(f(dec[0:TS, TP:T], dec[0:TS, TP:T], ACT.Exp), "dec")
                    sem_of(v, "ks", h)
                    s.did(f(work, gd["nK"], ACT.Square), "sqk")
                    first_tap("vtap", 0, V_ROW, h, "vhist")
                    sem_of(v, "qls", h)
                    s.did(f(ng[:, 1, 0:YW], ng[:, 1, 0:YW], ACT.Exp), "qsig")
                if slot == "L5":
                    sem_of(t, "ssk", h)
                    norm_scale(work, "lnk", "rnk", h)
                    s.did(f(gd["eG"], G, ACT.Exp), "eG")
                if slot == "L6x":
                    sem_of(s, "eG", h)
                    sem_of(v, "qs", h)
                    s.did(f(G, gd["nQ"], ACT.Square), "sqq")
                if slot == "L6":
                    sem_of(v, "vneg", h)
                    soft(0, YW, ("vexp", h), "vln")
                if slot == "C0":
                    sem_of(v, "vls", h)
                    s.did(f(ng[:, 0, 0:YW], ng[:, 0, 0:YW], ACT.Exp), "vsig")
                    sem_of(t, "ssq", h)
                    norm_scale(G, "lnq", "rnq", h)
                if slot == "C1":
                    sem_of(v, "zneg", h)
                    soft(2, T, ("zexp", h), "zln")
                if slot == "C2":
                    sem_of(t, "stash", h)
                    if not isinstance(h, int) or h > 0:
                        act.wait_ge(cv_out, h * 32)
                    n = XW * (NSEQ + 1)
                    f(cout[:, 0:2].rearrange("r g p -> r (g p)"), rr[0:n, 2, 0:2 * P], ACT.Copy)
                    s.did(f(cout[:, 2], rr[0:n, 3, 0:P], ACT.Copy), "cout")
                    sem_of(s, "cout", h)
                    for dst, r0, n in ((conv_p, 0, XW), (conv_s, XW, XW * NSEQ)):
                        d = dst[0].rearrange("b j (g h p) -> (b j) g h p", g=3, h=H)[:, :, ds(h, 1), :]
                        act.dma_start(d.rearrange("r g o p -> r g (o p)"), cout[r0:r0 + n]).then_inc(cv_out, 16)
                    sem_of(v, "zls", h)
                    s.did(f(ng[:, 2, 0:T], ng[:, 2, 0:T], ACT.Exp), "zsig")

            def load_conv(h):
                src = state_conv[0].rearrange("b j (g h p) -> (b j) g h p", g=3, h=H)
                act.dma_start(cin[:], src[:, :, ds(h, 1), :].rearrange("r g o p -> r g (o p)")).then_inc(cv_in, 16)

            def gdn_first_inverse(h):
                v, s, t = st["ga"]
                s.did(f(gd["K"], gd["nK"], ACT.Copy), "K")
                sem_of(t, "t0", h)
                f(gd["Tm"][:, 0:TP], rr[:, 1, :], ACT.Copy)
                s.did(f(gd["Tm"][0:TS, TP:T], rr[0:TS, 2, 0:TS], ACT.Copy), "tm0")

            def gdn_finish(step, h):
                v, s, t = st["gf"]
                sqr, oo = gd["sq"], gd["oo"]
                if step == "scale":
                    sem_of(t, "ss", h)
                    s.did(f(halves(sqr), rr[:, 2:4, 0:HALF], ACT.Ln, bias=epsc[:, 0:1], scale=1.0 / P), "ln")
                    sem_of(s, "ln", h)
                    s.did(f(sqr, sqr, ACT.Exp, scale=-0.5), "rn")
                if step == "hi":
                    sem_of(v, "og", h)
                    s.did(f(oh[:, ds(h, 1)].rearrange("p o n -> p (o n)"), oo, ACT.Copy), "hi")

            def gdn_head(h, prev, nxt):
                v, s, t = st["gr"]
                X, Tt, VN, oo, sqr = (gd[n] for n in ("X", "Tt", "VN", "oo", "sq"))
                for n, m in enumerate(LEVELS[1:], 1):
                    sem_of(t, f"x{m}", h)
                    last = f(X[:, 0:TP // 2], rr[:, 0, 0:TP // 2], ACT.Copy)
                    if m in SLEVELS:
                        last = f(X[0:TS, TP // 2:T // 2], rr[0:TS, 1, 0:TS // 2], ACT.Copy)
                    s.did(last, f"x{m}")
                    if nxt is not None:
                        gdn_prepare(f"L{n}x", nxt)
                    if m == 32:
                        sem_of(t, "srt", h)
                        s.did(f(X[0:TS, RS:RS + P], rr[0:TS, 2, SRT:SRT + P], ACT.Copy), "rs")
                    if m == 2:
                        if prev is not None:
                            gdn_finish("scale", prev)
                        act.wait_ge(st_out, h * 32 + 32 * H)
                        load_state(state_gdn, h)
                    if m == 64:
                        sem_of(t, "os", h)
                        s.did(f(oo[:, TP:T], rr[:, 1, 0:TS], ACT.Copy), "os")
                    if m == LEVELS[-1]:
                        if nxt is not None:
                            gdn_prepare("L6", nxt)
                        break
                    sem_of(t, f"tr{m}", h)
                    last = f(Tt[:, 0:TP], rr[:, 1, :], ACT.Copy)
                    if m in SLEVELS:
                        last = f(Tt[0:TS, TP:T], rr[0:TS, 0, 0:TS], ACT.Copy)
                    s.did(last, f"tt{m}")
                    if m == 4 and prev is not None:
                        gdn_finish("hi", prev)
                    if nxt is not None:
                        gdn_prepare(f"L{n}", nxt)
                    if m == 32:
                        sem_of(t, "svn", h)
                        s.did(f(X[0:TS, VNS:VNS + P], rr[0:TS, 3, SVN:SVN + P], ACT.Copy), "vns")
                for c in range(NC):
                    sem_of(t, f"vn{c}", h)
                    s.did(f(VN[:, c * P:(c + 1) * P], rr[:, 0, P:2 * P], ACT.Copy), f"vn{c}")
                    if nxt is not None:
                        gdn_prepare(f"C{c}", nxt)
                sem_of(t, "o", h)
                s.did(f(oo[:, 0:TP], rr[:, 1, :], ACT.Copy), "oo")
                sem_of(s, "oo", h)
                s.did(f(sqr, oo, ACT.Square), "sq")
                if nxt is not None:
                    gdn_first_inverse(nxt)
                sem_of(v, "sn1", h)
                store_states(gdn_p, gdn_s, h)

            def mlp(key):
                v, s, _ = st[key]

                with act.Fori(0, NGRP) as g:
                    for k in range(KT):
                        sem_of(v, f"s{k}", g)
                        s.did(f(oh[:, k], B[:, 2 + k % 2], ACT.Copy), f"hi{k}")

            load_state(state_hgrn, 0)
            norm("n0", None)
            for slot in range(3, 10):
                hgrn_prepare(slot, 0)
            with act.Fori(0, H - 1) as h:
                hgrn_head(h, h + 1)
            hgrn_head(H - 1, None)
            load_conv(0)
            norm("n1", U_HOUT)
            mlp("up0")
            norm("n2", U_AB - KT)
            gdn_pre()
            for slot in GDN_SLOTS:
                gdn_prepare(slot, 0)
            gdn_first_inverse(0)
            gdn_head(0, None, 1)
            with act.Fori(1, H - 2) as h:
                gdn_head(h, h - 1, h + 1)
            gdn_head(H - 2, H - 3, H - 1)
            gdn_head(H - 1, H - 2, None)
            gdn_finish("scale", H - 1)
            gdn_finish("hi", H - 1)
            norm("n3", U_GOUT)
            mlp("up1")
            norm("n4", U_END - KT)
            v, s, t = st["y"]
            for i in range(NC):
                sem_of(t, "t", i)
                if i >= 2:
                    act.wait_ge(y_out[i % 2], 16 * (i // 2))
                s.did(f(xrow[i % 2].rearrange("p (a n) -> p a n", a=2), rr[:, 2:4, :], ACT.Copy), "e")
                sem_of(s, "e", i)
                act.dma_start(y_prompt[0, i * P:(i + 1) * P, :], xrow[i % 2]).then_inc(y_out[i % 2], 16)
            v2, s2, t2 = st["ys"]
            sem_of(t2, "t", 0)
            act.wait_ge(y_out[0], 16 * (NC // 2))
            s2.did(f(xrow[NC % 2][0:TS].rearrange("p (a n) -> p a n", a=2), rr[0:TS, 2:4, :], ACT.Copy), "e")
            sem_of(s2, "e", 0)
            act.dma_start(y_sample.rearrange("b t d -> (b t) d"), xrow[NC % 2][0:TS]).then_inc(y_out[0], 16)
            act.wait_ge(y_out[0], 16 * (NC // 2 + 1))
            act.wait_ge(y_out[1], 16 * (NC // 2))
            act.wait_ge(st_out, 32 * H + 32 * H)
            act.wait_ge(cv_out, 32 * H)

        @block.vector
        def _(dve):
            tt, ts, stt, cp = nc.vector.tensor_tensor, nc.vector.tensor_scalar, nc.vector.scalar_tensor_tensor, nc.vector.tensor_copy
            pred = nc.vector.copy_predicated
            dve.wait_ge(c_in, 16 * N_CONST)
            for n, stage_ in enumerate(cstage):
                masks = cp(cu[:, n * CU_HALF:(n + 1) * CU_HALF], stage_)

            def after(steps, name, i):
                dve.wait_ge(steps.sem, steps.after(name, i))

            v, s, t = st["init"]
            v.did(masks, "masks")
            after(v, "masks", 0)
            nc.vector.memset(epsc[:], EPS).then_inc(unit_out, 2)
            for buf in (hg["KL"], hg["QL"], gt4[:], gcol[:], dtb[:]):
                nc.vector.memset(buf, 0.0)
            v.did(nc.vector.memset(zeros[:], 0.0), "fill")
            after(t, "vec", 0)
            v.did(cp(vec[:], rr[:, 0, 0:V_N]), "vec")
            nc.vector.memset(xp[:], 0.0)
            v.did(cp(cw[:].rearrange("p j s -> p (j s)"), rr[:, 1, 0:CONV * 3 * H]), "cw")
            lb = vec[:, V_LB:V_LB + H]
            after(v, "vec", 0)
            v.did(tt(lbt[:, 3], lb, lb, ALU.subtract), "lb1")
            after(s, "lb1", 0)
            v.did(nc.vector.reciprocal(lbt[:, 2], lbt[:, 3]), "lb2")
            after(v, "lb2", 0)
            v.did(tt(lbt[:, 3], lbt[:, 3], lbt[:, 2], ALU.mult), "lb3")
            after(v, "lb3", 0)
            v.did(tt(lbt[:, 3], lbt[:, 3], lbt[:, 3], ALU.subtract), "lb4")
            after(v, "lb4", 0)
            ts(lbt[:, 0], lbt[:, 3], -1.0, 1.0, ALU.mult, ALU.add)
            v.did(ts(lbt[:, 1], lbt[:, 3], LB_FLOOR, None, ALU.max), "lb5")
            after(s, "lb3", 0)
            v.did(ts(lbt[:, 1], lbt[:, 1], float(-np.log(LN_SHIFT)), None, ALU.add), "lb6")

            v, s, t = st["x"]
            for i in range(NC):
                after(t, "t", i)
                v.did(cp(xT[:, :, i * P:(i + 1) * P], rr[:, 2:4, :].rearrange("p a (k n) -> p (a k) n", n=P)), "copy")
            v2, _, t2 = st["xs"]
            after(t2, "t", 0)
            v2.did(cp(xT[:, :, TP:T], rr[:, 2, 0:KT * TS].rearrange("p (k n) -> p k n", n=TS)), "copy")

            def norm_tile(key, wcol, k):
                v, s, _ = st[key]
                after(s, f"sq{k}", 0)
                if k == 0:
                    v.did(cp(acc, sq[:, 0]), "acc0")
                else:
                    after(v, f"acc{k - 1}", 0)
                    v.did(tt(acc, acc, sq[:, k % 2], ALU.add), f"acc{k}")
                if wcol is None:
                    return
                w = vec[:, wcol + k:wcol + k + 1]
                v.did(ts(xh[:, k], xT[:, k], w, None, ALU.mult), f"hi{k}")
                after(v, f"hi{k}", 0)
                v.did(stt(out=xl[:, k], in0=xT[:, k], scalar=w, in1=xh[:, k].bitcast(F32),
                          op0=ALU.mult, op1=ALU.subtract), f"lo{k}")

            def add_units(U, r, key, wcol):
                for k in range(KT):
                    tt(halves(xT[:, k]), halves(xT[:, k]), computed(U, r, k), ALU.add).then_inc(unit_out, 1)
                    if k:
                        norm_tile(key, wcol, k - 1)
                norm_tile(key, wcol, KT - 1)

            def computed(U, r, j):
                dve.wait_ge(w_used, r + (U + j + 1))
                return psum_out((U + j) % SPLIT)

            def out_tail(h, v, s, wcol, oo, rn, gate, gate_of):
                after(s, "rn", h)
                v.did(stt(out=oo, in0=oo, scalar=vec[:, wcol:wcol + 1], in1=rn, op0=ALU.mult, op1=ALU.mult), "on")
                after(v, "on", h)
                after(gate_of, "gate", h)
                v.did(tt(oo, oo, gate, ALU.mult), "og")
                after(s, "hi", h)
                v.did(tt(ol[:, ds(h, 1)].rearrange("p o n -> p (o n)"), oo,
                         oh[:, ds(h, 1)].rearrange("p o n -> p (o n)"), ALU.subtract), "lo")

            def last_of(ap, m):
                b = blocks(ap, m)
                return b[:, :, m - 1:m].broadcast_to([b.shape[0], b.shape[1], m])

            def less_than_last(out, ap):
                tt(blocks(out[:, 0:TP], P), last_of(ap[:, 0:TP], P), blocks(ap[:, 0:TP], P), ALU.subtract)
                return tt(blocks(out[:, TP:T], SLEN), last_of(ap[:, TP:T], SLEN), blocks(ap[:, TP:T], SLEN), ALU.subtract)

            def over_chunks(ap):
                return ap.unsqueeze(1).broadcast_to([ap.shape[0], NC, P])

            def apart(out, vs):
                for a in range(2):
                    last = tt(blocks(out[a], P), vs.unsqueeze(1).broadcast_to([TS, NSEQ // 2, P]),
                              cf[0:TS, C_SEQ + 4 * a:C_SEQ + 4 * a + 4].unsqueeze(2).broadcast_to([TS, NSEQ // 2, P]),
                              ALU.mult)
                return last

            def decay_samples(decay):
                return tt(S0[:], S0[:], blocks(decay, SLEN)[:, :, SLEN - 1:SLEN].broadcast_to([P, NSEQ, P]), ALU.mult)

            def prompt_state(c, h, v, bank, decay):
                if c == 0:
                    v.did(cp(Sp[:, 0], bank), "S0")
                else:
                    after(v, f"S{c - 1}", h)
                    v.did(stt(out=Sp[:, c], in0=Sp[:, c - 1], scalar=decay, in1=bank, op0=ALU.mult, op1=ALU.add), f"S{c}")

            def negative_abs(row, w):
                return stt(out=ng[:, row, 0:w], in0=pr[:, row, 0:w], scalar=-1.0, in1=pr[:, row, 0:w], op0=ALU.mult,
                           op1=ALU.min)

            def log_sigmoid(row, w):
                return stt(out=ng[:, row, 0:w], in0=pr[:, row, 0:w], scalar=0.0, in1=ng[:, row, 0:w], op0=ALU.min,
                           op1=ALU.subtract)

            def hgrn_prepare(slot, h):
                v, s, t = st["ha"]
                T1 = xp[:, 0, XW:XW + T]

                def evacuate(j, dst):
                    tt(halves(dst), computed(U_HIN, h * 4, j), halves(rstd[:]), ALU.mult).then_inc(unit_out, 1)

                def evacuated(j):
                    dve.wait_ge(unit_out, h * 4 + (U_HIN + j + 3))

                if slot == 2:
                    v.did(cp(hc[:, 0:3], lbt[:, 0:3, ds(h, 1)].rearrange("p r o -> p (r o)")), "cols")
                    evacuate(0, pr[:, 1, 0:T])
                    evacuated(0)
                    v.did(negative_abs(1, T), "fneg")
                if slot == 3:
                    after(s, "fln", h)
                    v.did(log_sigmoid(1, T), "fls")
                    after(v, "fls", h)
                    v.did(tt(pr[:, 1, 0:T], ng[:, 1, 0:T], pr[:, 1, 0:T], ALU.subtract), "fb")
                    v.did(ts(T1, ng[:, 1, 0:T], hc[:, 2:3], hc[:, 1:2], ALU.add, ALU.subtract), "cd")
                    after(v, "cd", h)
                    v.did(stt(out=T1, in0=T1, scalar=-1.0, in1=T1, op0=ALU.mult, op1=ALU.min), "nabs")
                if slot == 4:
                    v.did(ts(ng[:, 1, 0:T], ng[:, 1, 0:T], hc[:, 2:3], hc[:, 1:2], ALU.add, ALU.max), "cmax")
                    evacuate(1, pr[:, 0, 0:T])
                    evacuated(1)
                    v.did(negative_abs(0, T), "qneg")
                if slot == 5:
                    after(s, "qln", h)
                    v.did(log_sigmoid(0, T), "qls")
                    after(v, "cmax", h)
                    v.did(tt(ng[:, 1, 0:T], ng[:, 1, 0:T], T1, ALU.add), "lf")
                if slot == 6:
                    evacuate(2, pr[:, 2, 0:T])
                    evacuated(2)
                    v.did(negative_abs(2, T), "gneg")
                if slot == 7:
                    after(s, "gln", h)
                    v.did(log_sigmoid(2, T), "gls")
                if slot == 8:
                    after(s, "qsig", h)
                    v.did(tt(hg["Q"], pr[:, 0, 0:T], ng[:, 0, 0:T], ALU.mult), "Q")
                    v.did(ts(hg["K"], pr[:, 1, 0:T], hc[:, 0:1], None, ALU.mult), "K")
                    after(v, "lf", h)
                    v.did(nc.vector.tensor_tensor_scan(hg["b"], reset, ng[:, 1, 0:T], 0.0, ALU.mult, ALU.add), "scan")
                    after(v, "scan", h)
                    v.did(less_than_last(hg["bd"], hg["b"]), "bd")
                if slot == 9:
                    after(s, "gsig", h)
                    v.did(tt(hg["gate"], pr[:, 2, 0:T], ng[:, 2, 0:T], ALU.mult), "gate")
                    evacuate(3, hg["val"])

            def hgrn_head(h, nxt):
                (v, s, t), (va, sa, ta) = st["hr"], st["ha"]
                Q, K, val, b, eb, qe, kd, dd, KL, A = (hg[n] for n in ("Q", "K", "val", "b", "eb", "qe", "kd", "dd",
                                                                       "KL", "A"))
                after(sa, "ebd", h)
                after(va, "K", h)
                v.did(tt(qe, Q, eb, ALU.mult), "qe")
                v.did(tt(kd, K, hg["bd"], ALU.mult), "kd")

                def differences(n, m):
                    w = width(m)
                    mid = first_half(b[:, 0:w], m)[:, :, m - 1:m].broadcast_to([P, w // (2 * m), m])
                    if n >= 2:
                        after(v, f"kl{LEVELS[n - 2]}", h)
                    tt(second_half(dd[:, n % 2, 0:w], m), second_half(b[:, 0:w], m), mid, ALU.subtract)
                    v.did(tt(first_half(dd[:, n % 2, 0:w], m), mid, first_half(b[:, 0:w], m), ALU.subtract), f"d{m}")

                def keep(n, m):
                    ready, kept = fixed(dve, t.after(f"lv{m}", h)), fixed(dve, v.after(f"pred{m // 2}" if n else "adiag", h))
                    dve.wait_ge(c_in, 16 * N_CONST)
                    dve.wait_ge(t.sem, ready)
                    dve.wait_ge(v.sem, kept)
                    last = pred(second_half(A[:, 0:TP], m), blocks(mask[:, 0, n, 0:TP // 2], m),
                                blocks(rr[:, n % 2, 0:TP // 2], m))
                    if m in SLEVELS:
                        last = pred(second_half(A[0:TS, TP:T], m), blocks(mask[0:TS, 0, n, TP // 2:T // 2], m),
                                    blocks(rr[0:TS, n % 2, TP // 2:T // 2], m))
                    v.did(last, f"pred{m}")

                differences(0, 1)
                after(t, "diag", h)
                tt(blocks(A[:, 0:TP], P), blocks(rr[:, 2, :], P), over_chunks(eye), ALU.mult)
                v.did(tt(A[0:TS, TP:T], rr[0:TS, 3, 0:TS], cf[0:TS, C_EYE:C_EYE + TS], ALU.mult), "adiag")
                for n, m in enumerate(LEVELS):
                    w = width(m)
                    if m < LEVELS[-1]:
                        differences(n + 1, 2 * m)
                    after(s, f"e{m}", h)
                    if n >= 2:
                        after(t, f"lv{LEVELS[n - 2]}", h)
                    tt(blocks(QL[:, n % 2, 0:w // 2], m), second_half(Q[:, 0:w], m), second_half(dd[:, n % 2, 0:w], m), ALU.mult)
                    v.did(tt(first_half(KL[:, n % 2, 0:w], m), first_half(K[:, 0:w], m), first_half(dd[:, n % 2, 0:w], m),
                             ALU.mult), f"kl{m}")
                    if n:
                        keep(n - 1, LEVELS[n - 1])
                    if m == 16:
                        after(t, "dS", h)
                        dve.wait_ge(st_in, h * 16 + 16)
                        for c in range(NC):
                            end = c * P + P - 1
                            prompt_state(c, h, v, rr[:, 2, c * P:(c + 1) * P], eb[:, end:end + 1])
                    if m == 32:
                        after(s, "kdTs", h)
                        v.did(apart([hg["vbig"][0:TS, a, 0:4 * P] for a in range(2)], vTs[:]), "vbig")
                        after(t, "os", h)
                        v.did(decay_samples(eb[:, TP:T]), "sdec")
                    if m == 64:
                        after(t, "dSs", h)
                        after(v, "sdec", h)
                        v.did(tt(S0[:], S0[:], rr[:, 2:4, :].rearrange("p a (b n) -> p (a b) n", n=P), ALU.add), "snew")
                    if nxt is not None:
                        hgrn_prepare(n, nxt)
                keep(len(LEVELS) - 1, LEVELS[-1])
                if nxt is not None:
                    hgrn_prepare(7, nxt)
                    hgrn_prepare(8, nxt)
                out_tail(h, v, s, V_HON, hg["oo"], hg["sq"], hg["gate"], va)
                if nxt is not None:
                    hgrn_prepare(9, nxt)

            def gdn_pre():
                v, s, t = st["gp"]
                cp(dtb[0:H], gsc[0:H, 1:2]).then_inc(dt_ready, 1)
                b = [B[0:64, n] for n in range(4)]
                tt(halves(b[0]), computed(U_AB, 0, 0)[0:64], halves(rstd[0:64]), ALU.mult).then_inc(unit_out, 1)
                dve.wait_ge(unit_out, unit_done(U_AB))
                dve.wait_ge(dt_ready, 1)
                v.did(ts(b[0], b[0], dtb[:, 0:1], None, ALU.add), "x")
                after(v, "x", 0)
                v.did(stt(out=b[1], in0=b[0], scalar=-1.0, in1=b[0], op0=ALU.mult, op1=ALU.min), "neg")
                after(s, "ln", 0)
                v.did(stt(out=b[2], in0=b[0], scalar=0.0, in1=b[1], op0=ALU.min, op1=ALU.subtract), "ls")
                v.did(stt(out=b[3][0:H], in0=b[0][0:H], scalar=0.0, in1=b[1][0:H], op0=ALU.max, op1=ALU.add), "g")
                after(v, "g", 0)
                v.did(ts(b[3][0:H], b[3][0:H], gsc[:, 2:3], -1.0, ALU.mult, ALU.mult), "g2")
                after(v, "g2", 0)
                v.did(nc.vector.tensor_tensor_scan(gt4[0:H], reset[0:H], b[3][0:H], 0.0, ALU.mult, ALU.add), "scan")
                after(v, "scan", 0)
                v.did(less_than_last(b[3][0:H], gt4[0:H]), "dl")

            def gdn_prepare(slot, h):
                v, s, t = st["ga"]
                nQ, nK, nV, work, G, dec = (gd[n] for n in ("nQ", "nK", "nV", "work", "G", "dec"))
                of_head = lambda r: gcol[:, :, H * r:H * (r + 1)][:, :, ds(h, 1)]

                def evacuate(j, row):
                    ps = computed(U_GIN, h * 4, j)
                    cut = TP - HALF
                    tt(xp[:, row, XW:XW + HALF], ps[:, 0], rstd[:, 0:HALF], ALU.mult)
                    tt(xp[:, row, XW + HALF:XW + TP], ps[:, 1, 0:cut], rstd[:, HALF:TP], ALU.mult)
                    tt(blocks(xp[:, row, SB0:XPW], SROW)[:, :, XW:SROW], blocks(ps[:, 1, cut:HALF], SLEN),
                       blocks(rstd[:, TP:T], SLEN), ALU.mult).then_inc(unit_out, 1)

                def convolve(name, tap, row, g):
                    after(s, tap, h)
                    for j in range(1, CONV):
                        if j > 1:
                            after(v, f"{name}{j - 1}", h)
                        v.did(stt(out=pr[:, row, 0:YW], in0=xp[:, row, j:j + YW], scalar=hcw[:, j, g:g + 1],
                                  in1=pr[:, row, 0:YW], op0=ALU.mult, op1=ALU.add), f"{name}{j}")
                    after(v, f"{name}3", h)
                    v.did(negative_abs(row, YW), f"{name}neg")

                def silu(name, row, dst):
                    after(s, f"{name}sig", h)
                    tt(dst[:, 0:TP], pr[:, row, 0:TP], ng[:, row, 0:TP], ALU.mult)
                    v.did(tt(blocks(dst[:, TP:T], SLEN), blocks(pr[:, row, SB0:XPW], SROW)[:, :, 0:SLEN],
                             blocks(ng[:, row, SB0:XPW], SROW)[:, :, 0:SLEN], ALU.mult), f"{name}s")

                def decayed(bank, name):
                    dst = work if name == "kkd" else dec
                    tt(dst[:, 0:TP].rearrange("p (a n) -> p a n", a=2), rr[:, 2:4, 0:2 * P],
                       dec[:, 0:TP].rearrange("p (a n) -> p a n", a=2), ALU.mult)
                    v.did(tt(dst[0:TS, TP:T], rr[0:TS, bank, 2 * P:2 * P + TS], dec[0:TS, TP:T], ALU.mult), name)

                if slot == "L0":
                    evacuate(0, 0)
                    evacuate(1, 1)
                if slot == "L1":
                    cp(hc[:, 4:5], cf[:, ds(h + C_HSEL, 1)])
                    cp(hcw[:], cw[:].rearrange("p j (g x) -> p j g x", g=3)[:, :, :, ds(h, 1)]
                       .rearrange("p j g o -> p j (g o)"))
                    v.did(cp(gnext[:], of_head(0).rearrange("p c o -> p (c o)")), "cols")
                    after(v, "cols", h)
                    v.did(ts(work, gt4[:], hc[:, 4:5], None, ALU.mult), "gsel")
                if slot == "L2":
                    convolve("k", "ktap", 0, K_ROW)
                if slot == "L3":
                    after(s, "kln", h)
                    v.did(log_sigmoid(0, YW), "kls")
                    convolve("q", "qtap", 1, Q_ROW)
                if slot == "L4":
                    after(s, "G", h)
                    for c in range(NC):
                        cols = slice(c * P, (c + 1) * P)
                        ts(dec[:, cols], G[:, cols], gnext[:, c:c + 1], 0.0, ALU.subtract, ALU.min)
                    v.did(ts(dec[0:TS, TP:T], G[0:TS, TP:T], gnext[0:TS, NC:NC + 1], 0.0, ALU.subtract, ALU.min), "dec")
                    silu("k", 0, nK)
                    after(s, "qln", h)
                    v.did(log_sigmoid(1, YW), "qls")
                    evacuate(2, 0)
                if slot == "L5":
                    after(s, "rnk", h)
                    after(v, "ks", h)
                    v.did(tt(nK, nK, work, ALU.mult), "kn")
                    after(v, "kn", h)
                    v.did(tt(work, nK, gd["beta"], ALU.mult), "kb")
                    convolve("v", "vtap", 0, V_ROW)
                    silu("q", 1, nQ)
                if slot == "L6":
                    after(t, "kk", h)
                    decayed(2, "kkd")
                    after(s, "vln", h)
                    v.did(log_sigmoid(0, YW), "vls")
                if slot == "C0":
                    silu("v", 0, nV)
                    after(s, "rnq", h)
                    v.did(stt(out=nQ, in0=nQ, scalar=float(P) ** -0.5, in1=G, op0=ALU.mult, op1=ALU.mult), "qn")
                if slot == "C1":
                    tt(halves(pr[:, 2, 0:T]), computed(U_GIN, h * 4, 3), halves(rstd[:]), ALU.mult).then_inc(unit_out, 1)
                    dve.wait_ge(unit_out, h * 4 + (U_GIN + 3 + 3))
                    v.did(negative_abs(2, T), "zneg")
                    after(t, "qk", h)
                    decayed(3, "qkd")
                if slot == "C2":
                    after(v, "kkd", h)
                    tt(blocks(gd["NL"][:, 0:TP], P), blocks(work[:, 0:TP], P), over_chunks(cf[:, C_NSTR:C_NSTR + P]), ALU.mult)
                    v.did(tt(gd["NL"][0:TS, TP:T], work[0:TS, TP:T], cf[0:TS, C_NSTRS:C_NSTRS + TS], ALU.mult), "nl")
                    after(s, "zln", h)
                    v.did(log_sigmoid(2, T), "zls")
                if slot == "inverse":
                    Tt, NL = gd["Tt"], gd["NL"]
                    cp(blocks(Tt[:, 0:TP], P), over_chunks(eye))
                    v.did(cp(Tt[0:TS, TP:T], cf[0:TS, C_EYE:C_EYE + TS]), "tt0")
                    ready = fixed(dve, v.after("tt0", h))
                    dve.wait_ge(c_in, 16 * N_CONST)
                    dve.wait_ge(v.sem, ready)
                    pred(second_half(Tt[:, 0:TP], 1), blocks(mask[:, 0, 0, 0:TP // 2], 1), second_half(NL[:, 0:TP], 1))
                    v.did(pred(second_half(Tt[0:TS, TP:T], 1), blocks(mask[0:TS, 0, 0, TP // 2:T // 2], 1),
                               second_half(NL[0:TS, TP:T], 1)), "tt1")
                if slot == "move":
                    after(v, "qkd", h)
                    tt(blocks(gd["A"][:, 0:TP], P), blocks(dec[:, 0:TP], P), over_chunks(cf[:, C_INCL:C_INCL + P]), ALU.mult)
                    v.did(tt(gd["A"][0:TS, TP:T], dec[0:TS, TP:T], cf[0:TS, C_INCLS:C_INCLS + TS], ALU.mult), "A")
                    after(v, "qn", h)
                    v.did(tt(gd["qe"], nQ, gd["eG"], ALU.mult), "qe")
                    for r in range(4):
                        cp(gcols[:, :, r:r + 1], of_head(r))
                    cp(eGs[:, 0:NC], blocks(gd["eG"][:, 0:TP], P)[:, :, P - 1])
                    cp(eGs[:, NC:], gd["eG"][:, TP:T])
                    v.did(cp(betas[:], gd["beta"][:, TP:T]), "cols2")
                    after(v, "cols2", h)
                    v.did(stt(out=nbe[:], in0=gcols[:, :, 1], scalar=-1.0, in1=gcols[:, :, 3], op0=ALU.mult, op1=ALU.mult),
                          "nbe")

            def gdn_finish(step, h):
                v, s, t = st["gf"]
                oo = gd["oo"]
                if step == "on":
                    after(s, "rn", h)
                    v.did(stt(out=oo, in0=oo, scalar=vec[:, V_GON:V_GON + 1], in1=gd["sq"], op0=ALU.mult, op1=ALU.mult), "on")
                if step == "og":
                    after(v, "on", h)
                    after(st["gr"][0], "gate", h)
                    v.did(tt(oo, oo, gd["gate"], ALU.mult), "og")
                if step == "lo":
                    after(s, "hi", h)
                    v.did(tt(ol[:, ds(h, 1)].rearrange("p o n -> p (o n)"), oo,
                             oh[:, ds(h, 1)].rearrange("p o n -> p (o n)"), ALU.subtract), "lo")

            def gdn_head(h, prev, nxt):
                (v, s, t), (va, sa, ta) = st["gr"], st["ga"]
                Tm, vT, kdT = gd["Tm"], gd["vT"], gd["kdT"]
                after(va, "nbe", h)

                def turned(dst, col, name):
                    for a in range(2):
                        last = tt(blocks(dst[:, a * 2 * P:(a + 1) * 2 * P], P), blocks(rr[:, 2 + a, 0:2 * P], P),
                                  gcols[:, 2 * a:2 * a + 2, col:col + 1].broadcast_to([P, 2, P]), ALU.mult)
                    v.did(last, name)

                if nxt is not None:
                    gdn_prepare("L0", nxt)
                for n, m in enumerate(LEVELS[1:], 1):
                    if n == 1:
                        after(sa, "tm0", h)
                    if m == 8:
                        after(t, "sks", h)
                        v.did(tt(rt[:], rr[:, 1, 0:TS], eGs[:, NC:], ALU.mult), "sr1")
                    ready = fixed(dve, t.after(f"dt{m}", h))
                    dve.wait_ge(c_in, 16 * N_CONST)
                    dve.wait_ge(t.sem, ready)
                    if m == LEVELS[-1]:
                        v.did(cp(second_half(gd["Tt"][0:m, 0:TP], m), blocks(rr[0:m, 0, 256:512], m)), "pred64")
                        if nxt is not None:
                            gdn_prepare("L6", nxt)
                        break
                    last = pred(first_half(Tm[:, 0:TP], m), blocks(mask[:, 1, n, 0:TP // 2], m), blocks(rr[:, 0, 256:512], m))
                    if m in SLEVELS:
                        last = pred(first_half(Tm[0:TS, TP:T], m), blocks(mask[0:TS, 1, n, TP // 2:T // 2], m),
                                    blocks(rr[0:TS, 1, TS // 2:TS], m))
                    v.did(last, f"pred{m}")
                    if m == 2:
                        after(t, "vT", h)
                        turned(vT, 1, "vb")
                        if prev is not None:
                            gdn_finish("on", prev)
                    if m == 4:
                        after(t, "kT", h)
                        turned(kdT, 2, "kdt")
                        v.did(ts(kdTs[:], rr[0:TS, 2, SRT:SRT + P], gcols[0:TS, NC, 2:3], None, ALU.mult), "kdts")
                        if prev is not None:
                            gdn_finish("og", prev)
                            after(st["gf"][0], "og", prev)
                        after(sa, "zsig", h)
                        v.did(tt(gd["gate"], pr[:, 2, 0:T], ng[:, 2, 0:T], ALU.mult), "gate")
                    if m == 8:
                        after(v, "sr1", h)
                        if prev is not None:
                            gdn_finish("lo", prev)
                        v.did(tt(rt[:], gd["nV"][:, TP:T], rt[:], ALU.subtract), "sr2")
                        after(v, "sr2", h)
                        v.did(tt(rt[:], rt[:], betas[:], ALU.mult), "sr3")
                    if nxt is not None:
                        gdn_prepare(f"L{n}", nxt)
                for c in range(NC):
                    if c:
                        after(t, f"ks{c}", h)
                        v.did(stt(out=vT[:, c * P:(c + 1) * P], in0=rr[:, 0, 0:P], scalar=nbe[:, c:c + 1],
                                  in1=vT[:, c * P:(c + 1) * P], op0=ALU.mult, op1=ALU.add), f"r{c}")
                    else:
                        dve.wait_ge(st_in, h * 16 + 16 * (H + 1))
                    after(t, f"dS{c}", h)
                    prompt_state(c, h, v, rr[:, 0, 2 * P:3 * P], eGs[:, c:c + 1])
                    if c == 2:
                        after(s, "vns", h)
                        after(t, "dt64", h)
                        v.did(apart(gd_vbig, gd["X"][0:TS, VNS:VNS + P]), "vbig")
                        after(t, "os", h)
                        v.did(decay_samples(eGs[:, NC:]), "sdec")
                    if nxt is not None:
                        gdn_prepare(f"C{c}", nxt)
                if nxt is not None:
                    gdn_prepare("inverse", nxt)
                for a in range(2):
                    after(t, f"dSs{a}", h)
                    after(v, "sdec", h)
                    half = S0[:, 4 * a:4 * a + 4, :].rearrange("p b n -> p (b n)")
                    v.did(tt(half, half, rr[:, 0, :], ALU.add), f"sn{a}")
                if nxt is not None:
                    after(t, "o", h)
                    gdn_prepare("move", nxt)

            def mlp(U, nkey, key, nxt, wcol):
                v, s, _ = st[key]
                after(st[nkey][1], "rstd", 0)

                def up(g):
                    r = g * (2 * KT)

                    def rest(k):
                        after(s, f"hi{k}", g)
                        v.did(tt(ol[:, k], B[:, 2 + k % 2], oh[:, k], ALU.subtract), f"lo{k}")

                    for k in range(KT):
                        tt(halves(B[:, k % 2]), computed(U, r, k), halves(rstd[:]), ALU.mult).then_inc(unit_out, 1)
                        dve.wait_ge(unit_out, r + (U + k + 3))
                        v.did(stt(out=B[:, 2 + k % 2], in0=B[:, k % 2], scalar=0.0, in1=B[:, k % 2],
                                  op0=ALU.max, op1=ALU.mult), f"s{k}")
                        if k:
                            rest(k - 1)
                    rest(KT - 1)

                with dve.Fori(0, NGRP - 1) as g:
                    up(g)
                    for k in range(KT):
                        tt(halves(xT[:, k]), halves(xT[:, k]), computed(U, g * (2 * KT), KT + k), ALU.add).then_inc(unit_out, 1)
                up(NGRP - 1)
                add_units(U + (2 * NGRP - 1) * KT, 0, nxt, wcol)

            after(st["xs"][0], "copy", 0)
            for k in range(KT):
                norm_tile("n0", V_MIX, k)
            after(st["n0"][1], "rstd", 0)
            for slot in range(2, 10):
                hgrn_prepare(slot, 0)
            with dve.Fori(0, H - 1) as h:
                hgrn_head(h, h + 1)
            hgrn_head(H - 1, None)
            add_units(U_HOUT, 0, "n1", V_MLP)
            mlp(U_MLP0, "n1", "up0", "n2", V_MIX + KT)
            after(st["n2"][1], "rstd", 0)
            gdn_pre()
            after(st["gp"][1], "cols", 0)
            for slot in GDN_SLOTS + ["inverse", "move"]:
                gdn_prepare(slot, 0)
            gdn_head(0, None, 1)
            with dve.Fori(1, H - 2) as h:
                gdn_head(h, h - 1, h + 1)
            gdn_head(H - 2, H - 3, H - 1)
            gdn_head(H - 1, H - 2, None)
            gdn_finish("on", H - 1)
            gdn_finish("og", H - 1)
            gdn_finish("lo", H - 1)
            add_units(U_GOUT, 0, "n3", V_MLP + KT)
            mlp(U_MLP1, "n3", "up1", "n4", None)
            after(st["n4"][1], "rstd", 0)

            def result(i, cols, steps):
                n = cols.stop - cols.start
                for k in range(KT):
                    last = stt(out=ycol[i % 2][:, k * P:k * P + n], in0=xT[:, k, cols], scalar=vec[:, V_FIN + k:V_FIN + k + 1],
                               in1=rstd[:, cols], op0=ALU.mult, op1=ALU.mult)
                steps.did(last, "y")

            v, s, t = st["y"]
            for i in range(NC):
                if i >= 2:
                    after(t, "t", i - 2)
                result(i, slice(i * P, (i + 1) * P), v)
            after(t, "t", NC - 2)
            result(NC, slice(TP, T), st["ys"][0])


_INS = ['x_prompt', 'x_sample', 'state_hgrn', 'state_gdn', 'state_gdn_conv', 'norm_mix', 'norm_mlp', 'norm_final',
        'hgrn_w_in', 'hgrn_lb', 'hgrn_out_norm', 'hgrn_w_out', 'gdn_w_in', 'gdn_conv_w', 'gdn_A_log', 'gdn_dt_bias',
        'gdn_out_norm', 'gdn_w_out', 'mlp_w_up', 'mlp_w_down']
_OUTS = [(1, TP, D), (NSEQ, SLEN, D), (1, 1, H, P, P), (1, NSEQ, H, P, P), (1, 1, H, P, P), (1, NSEQ, H, P, P),
         (1, 1, XW, 3 * D), (1, NSEQ, XW, 3 * D)]


def kernel(**inputs):
    import concourse.bacc as _bacc
    from concourse.bass_utils import run_bass_kernel_spmd as _run

    nc = _bacc.Bacc("TRN2", target_bir_lowering=False, num_devices=1)
    arrays, args = {}, []
    named = [(name, np.ascontiguousarray(inputs[name])) for name in _INS]
    named += list(zip(("const_f", "const_u"), shape_constants()))
    for name, a in named:
        arrays[f"in_{name}_dram"] = a
        args.append(nc.dram_tensor(f"in_{name}_dram", a.shape, mybir.dt.from_np(a.dtype), kind="ExternalInput").ap())
    for i, shape in enumerate(_OUTS):
        args.append(nc.dram_tensor(f"out_{i}_dram", shape, F32, kind="ExternalOutput").ap())
    build(nc, *args)
    r = _run(nc, [arrays], core_ids=[0])
    return tuple(r.results[0][f"out_{i}_dram"] for i in range(len(_OUTS)))
```
